# Optimizing a Trainium2 kernel written in Bass

```python
import math
import jax, jax.numpy as jnp
from jax import lax
import numpy as np

D_MODEL = 1024
BATCH = 1
SEQ = 256
DEPTH = 2

GRID_W = 64
CTX_LEN = 256
MIX_WIDTH = D_MODEL
DA_WIDTH = MIX_WIDTH // 2
DA_HEADS = 4
DA_VDIM = DA_WIDTH // DA_HEADS
DA_HEAD_DIM = DA_VDIM // 2
SG_WIDTH = MIX_WIDTH - DA_WIDTH
SG_GROUPS = 4
SG_GROUP_DIM = SG_WIDTH // SG_GROUPS
CHUNK = 128
Q_BLOCK = 128
ROPE_BASE = 10000.0
D_FF = 2816
N_EXPERTS = 8
TOP_K = 2
D_EXPERT = 3584
N_DENSE = (DEPTH + 1) // 2
N_MOE = DEPTH // 2
EPS = 1e-6
IN_COLS = 3 * DA_WIDTH + 2 * SG_WIDTH

kernel_name = "hybrid_diffattn_sgu_moe_dit"

def rmsnorm(x, g):
    xf = x.astype(jnp.float32)
    y = xf * lax.rsqrt(jnp.mean(xf * xf, axis=-1, keepdims=True) + EPS)
    return (y * g.astype(jnp.float32)).astype(x.dtype)

def layernorm(x, g, b):
    xf = x.astype(jnp.float32)
    mu = jnp.mean(xf, axis=-1, keepdims=True)
    var = jnp.mean(jnp.square(xf - mu), axis=-1, keepdims=True)
    y = (xf - mu) * lax.rsqrt(var + EPS)
    return (y * g.astype(jnp.float32) + b.astype(jnp.float32)).astype(x.dtype)

def modulate(h, shift, scale):
    return h * (1 + scale) + shift

def axial_rope_tables(n_tokens, dtype):
    rows = n_tokens // GRID_W
    row = jnp.repeat(jnp.arange(rows, dtype=jnp.float32), GRID_W)
    col = jnp.tile(jnp.arange(GRID_W, dtype=jnp.float32), rows)
    half = DA_HEAD_DIM // 2
    inv = ROPE_BASE ** (-jnp.arange(0, half, 2, dtype=jnp.float32) / half)
    ang_r = row[:, None] * inv
    ang_c = col[:, None] * inv
    ang = jnp.concatenate([ang_r, ang_r, ang_c, ang_c], axis=-1)
    return jnp.cos(ang).astype(dtype), jnp.sin(ang).astype(dtype)

def apply_rope(x, cos, sin):
    xs = x.reshape(x.shape[:-1] + (2, 2, DA_HEAD_DIM // 4))
    rot = jnp.concatenate([-xs[..., 1:2, :], xs[..., 0:1, :]], axis=-2).reshape(x.shape)
    return x * cos[:, None, None, :] + rot * sin[:, None, None, :]

def diff_attention(q, k, v, lam):
    b, sq = q.shape[0], q.shape[1]
    nb = sq // Q_BLOCK
    qb = q.reshape(b, nb, Q_BLOCK, DA_HEADS, 2, DA_HEAD_DIM).transpose(1, 0, 2, 3, 4, 5)
    scale = DA_HEAD_DIM ** -0.5

    def block(qi):
        s = jnp.einsum('bqhmd,bkhmd->bhmqk', qi, k).astype(jnp.float32) * scale
        p = jax.nn.softmax(s, axis=-1)
        w = p[:, :, 0] - lam.astype(jnp.float32) * p[:, :, 1]
        return jnp.einsum('bhqk,bkhe->bqhe', w.astype(v.dtype), v)

    out = lax.map(block, qb)
    return out.transpose(1, 0, 2, 3, 4).reshape(b, sq, DA_HEADS, DA_VDIM)

def diff_head_out(o, subln_g, lambda_init):
    o = rmsnorm(o, subln_g) * (1.0 - lambda_init)
    return o.reshape(o.shape[0], o.shape[1], DA_WIDTH)

def spatial_gating(u, gv, ln_g, ln_b, w_s, b_s):
    b, s, _ = u.shape
    vn = layernorm(gv, ln_g, ln_b)
    vc = vn.reshape(b, s // CHUNK, CHUNK, SG_GROUPS, SG_GROUP_DIM)
    mixed = jnp.einsum('gpq,bcqge->bcpge', w_s, vc) + b_s.T[None, None, :, :, None]
    return u * mixed.reshape(b, s, SG_WIDTH)

def swiglu(h, w1, w3, w2):
    return (jax.nn.silu(h @ w1) * (h @ w3)) @ w2

def moe_swiglu(h, router_w, w1, w3, w2):
    shp = h.shape
    t = h.reshape(-1, shp[-1])
    logits = (t @ router_w).astype(jnp.float32)
    top_v, top_i = lax.top_k(logits, TOP_K)
    top_w = jax.nn.softmax(top_v, axis=-1)
    gates = jnp.sum(jax.nn.one_hot(top_i, N_EXPERTS, dtype=jnp.float32) * top_w[..., None], axis=1)
    gates = gates.astype(h.dtype)
    y = jnp.zeros_like(t)
    for e in range(N_EXPERTS):
        y = y + gates[:, e:e + 1] * swiglu(t, w1[e], w3[e], w2[e])
    return y.reshape(shp)

def split_heads_qkv(p):
    q, k, v = p[..., :DA_WIDTH], p[..., DA_WIDTH:2 * DA_WIDTH], p[..., 2 * DA_WIDTH:3 * DA_WIDTH]
    b, s = p.shape[0], p.shape[1]
    q = q.reshape(b, s, DA_HEADS, 2, DA_HEAD_DIM)
    k = k.reshape(b, s, DA_HEADS, 2, DA_HEAD_DIM)
    v = v.reshape(b, s, DA_HEADS, DA_VDIM)
    return q, k, v

def setup_inputs(seed: int = 0) -> dict:
    key = jax.random.key(seed)
    ks = jax.random.split(key, 28)
    f32 = jnp.float32
    nrm = lambda k, shape, s: (jax.random.normal(k, shape, f32) * s)
    gain = lambda k, shape: 1.0 + 0.05 * jax.random.normal(k, shape, f32)
    D = D_MODEL
    return {
        "x": nrm(ks[0], (BATCH, SEQ, D), 1.0),
        "c": nrm(ks[1], (BATCH, D), 1.0),
        "ctx": nrm(ks[2], (BATCH, CTX_LEN, D), 1.0),
        "c_ctx": nrm(ks[3], (D,), 1.0),
        "ada_w": nrm(ks[4], (DEPTH, D, 6 * D), 0.5 * D ** -0.5),
        "ada_b": nrm(ks[5], (DEPTH, 6 * D), 0.02),
        "pre_mix_g": gain(ks[6], (DEPTH, D)),
        "post_mix_g": gain(ks[7], (DEPTH, D)),
        "pre_ffn_g": gain(ks[8], (DEPTH, D)),
        "post_ffn_g": gain(ks[9], (DEPTH, D)),
        "w_in": nrm(ks[10], (DEPTH, D, IN_COLS), D ** -0.5),
        "w_out": nrm(ks[11], (DEPTH, MIX_WIDTH, D), MIX_WIDTH ** -0.5),
        "lam_q1": nrm(ks[12], (DEPTH, DA_HEAD_DIM), 0.1),
        "lam_k1": nrm(ks[13], (DEPTH, DA_HEAD_DIM), 0.1),
        "lam_q2": nrm(ks[14], (DEPTH, DA_HEAD_DIM), 0.1),
        "lam_k2": nrm(ks[15], (DEPTH, DA_HEAD_DIM), 0.1),
        "subln_g": gain(ks[16], (DEPTH, DA_VDIM)),
        "sg_ln_g": gain(ks[17], (DEPTH, SG_WIDTH)),
        "sg_ln_b": nrm(ks[18], (DEPTH, SG_WIDTH), 0.02),
        "sg_w": nrm(ks[19], (DEPTH, SG_GROUPS, CHUNK, CHUNK), CHUNK ** -0.5),
        "sg_b": 1.0 + nrm(ks[20], (DEPTH, SG_GROUPS, CHUNK), 0.02),
        "ffn_w1": nrm(ks[21], (N_DENSE, D, D_FF), D ** -0.5),
        "ffn_w3": nrm(ks[22], (N_DENSE, D, D_FF), D ** -0.5),
        "ffn_w2": nrm(ks[23], (N_DENSE, D_FF, D), D_FF ** -0.5),
        "router_w": nrm(ks[24], (N_MOE, D, N_EXPERTS), D ** -0.5),
        "moe_w1": nrm(ks[25], (N_MOE, N_EXPERTS, D, D_EXPERT), D ** -0.5),
        "moe_w3": nrm(ks[26], (N_MOE, N_EXPERTS, D, D_EXPERT), D ** -0.5),
        "moe_w2": nrm(ks[27], (N_MOE, N_EXPERTS, D_EXPERT, D), D_EXPERT ** -0.5),
    }

def reference(x, c, ctx, c_ctx, ada_w, ada_b, pre_mix_g, post_mix_g, pre_ffn_g, post_ffn_g,
              w_in, w_out, lam_q1, lam_k1, lam_q2, lam_k2, subln_g, sg_ln_g, sg_ln_b, sg_w, sg_b,
              ffn_w1, ffn_w3, ffn_w2, router_w, moe_w1, moe_w3, moe_w2):
    n_lat = x.shape[1]
    cos, sin = axial_rope_tables(n_lat, x.dtype)
    x_lat, x_ctx = x, ctx
    for l in range(DEPTH):
        last = l == DEPTH - 1
        lambda_init = 0.8 - 0.6 * math.exp(-0.3 * l)
        ms = jnp.split(jax.nn.silu(c) @ ada_w[l] + ada_b[l], 6, axis=-1)
        ms = [m[:, None, :] for m in ms]
        mc = jnp.split(jax.nn.silu(c_ctx) @ ada_w[l] + ada_b[l], 6, axis=-1)
        lam = (jnp.exp(jnp.sum(lam_q1[l] * lam_k1[l])) - jnp.exp(jnp.sum(lam_q2[l] * lam_k2[l]))
               + lambda_init)

        h_lat = modulate(rmsnorm(x_lat, pre_mix_g[l]), ms[0], ms[1])
        h_ctx = modulate(rmsnorm(x_ctx, pre_mix_g[l]), mc[0], mc[1])
        p_lat = h_lat @ w_in[l]
        q_l, k_l, v_l = split_heads_qkv(p_lat)
        q_l = apply_rope(q_l, cos, sin)
        k_l = apply_rope(k_l, cos, sin)
        u_l = p_lat[..., 3 * DA_WIDTH:3 * DA_WIDTH + SG_WIDTH]
        g_l = p_lat[..., 3 * DA_WIDTH + SG_WIDTH:]
        if last:
            p_kv = h_ctx @ w_in[l][:, DA_WIDTH:3 * DA_WIDTH]
            bc, sc = p_kv.shape[0], p_kv.shape[1]
            k_c = p_kv[..., :DA_WIDTH].reshape(bc, sc, DA_HEADS, 2, DA_HEAD_DIM)
            v_c = p_kv[..., DA_WIDTH:].reshape(bc, sc, DA_HEADS, DA_VDIM)
        else:
            p_ctx = h_ctx @ w_in[l]
            q_c, k_c, v_c = split_heads_qkv(p_ctx)
        k_all = jnp.concatenate([k_c, k_l], axis=1)
        v_all = jnp.concatenate([v_c, v_l], axis=1)
        a_lat = diff_head_out(diff_attention(q_l, k_all, v_all, lam), subln_g[l], lambda_init)
        s_lat = spatial_gating(u_l, g_l, sg_ln_g[l], sg_ln_b[l], sg_w[l], sg_b[l])
        o_lat = jnp.concatenate([a_lat, s_lat], axis=-1) @ w_out[l]
        x_lat = x_lat + ms[2] * rmsnorm(o_lat, post_mix_g[l])
        if not last:
            u_c = p_ctx[..., 3 * DA_WIDTH:3 * DA_WIDTH + SG_WIDTH]
            g_c = p_ctx[..., 3 * DA_WIDTH + SG_WIDTH:]
            a_ctx = diff_head_out(diff_attention(q_c, k_c, v_c, lam), subln_g[l], lambda_init)
            s_ctx = spatial_gating(u_c, g_c, sg_ln_g[l], sg_ln_b[l], sg_w[l], sg_b[l])
            o_ctx = jnp.concatenate([a_ctx, s_ctx], axis=-1) @ w_out[l]
            x_ctx = x_ctx + mc[2] * rmsnorm(o_ctx, post_mix_g[l])

        f_lat = modulate(rmsnorm(x_lat, pre_ffn_g[l]), ms[3], ms[4])
        if l % 2 == 0:
            i = l // 2
            y_lat = swiglu(f_lat, ffn_w1[i], ffn_w3[i], ffn_w2[i])
        else:
            i = l // 2
            y_lat = moe_swiglu(f_lat, router_w[i], moe_w1[i], moe_w3[i], moe_w2[i])
        x_lat = x_lat + ms[5] * rmsnorm(y_lat, post_ffn_g[l])
        if not last:
            f_ctx = modulate(rmsnorm(x_ctx, pre_ffn_g[l]), mc[3], mc[4])
            i = l // 2
            if l % 2 == 0:
                y_ctx = swiglu(f_ctx, ffn_w1[i], ffn_w3[i], ffn_w2[i])
            else:
                y_ctx = moe_swiglu(f_ctx, router_w[i], moe_w1[i], moe_w3[i], moe_w2[i])
            x_ctx = x_ctx + mc[5] * rmsnorm(y_ctx, post_ffn_g[l])
    return x_lat


_drawn_inputs = setup_inputs


def setup_inputs(seed=0):
    import zlib

    import numpy as np

    out = dict(_drawn_inputs(seed))
    spreads = {}
    factors = {'lam_k2': 2.872, 'subln_g': 12.689, 'sg_ln_g': 3.564, 'sg_ln_b': 50.725, 'sg_b': 26.969}
    for name, (base, spread) in spreads.items():
        noise = np.random.default_rng([zlib.crc32(name.encode()), seed]).standard_normal(out[name].shape)
        drawn = base * np.exp(spread * noise) if base else spread * noise
        out[name] = __import__('jax').numpy.asarray(drawn.astype(out[name].dtype))
    for name, factor in factors.items():
        out[name] = (out[name] * factor).astype(out[name].dtype)
    return out
```

```python
from contextlib import ExitStack
import math

import numpy as np
import concourse.bass as bass
from concourse import mybir

F32 = mybir.dt.float32
F32R = mybir.dt.float32r
I32 = mybir.dt.int32
U32 = mybir.dt.uint32
ALU = mybir.AluOpType
ACT = mybir.ActivationFunctionType
AX = mybir.AxisListType

P = 128
D = 1024
KD = D // P
NB = 4
NLAT = 2
HEADS = 4
HD = 64
DA = 512
SG = 512
IN = 2560
FF = 2816
NE = 8
DE = 3584
EPS = 1e-6
SCALE = HD ** -0.5

UW = 1024
RAW = 6
SPL = 4
AHEAD = SPL - 1
ATS = 6
STEPS = DE // 512
UE = 12 * STEPS

C_ID, C_TRIU, C_ONES, C_IOTA, C_SELB, C_SELC, C_COS, C_SIN = 0, 128, 256, 384, 512, 768, 770, 898
C_END = 1026


def constants():
    c = np.zeros((P, C_END), np.float32)
    c[:, C_ID:C_ID + P] = np.eye(P)
    c[:, C_TRIU:C_TRIU + P] = np.triu(np.ones((P, P)))
    c[:, C_ONES:C_ONES + P] = 1
    c[:, C_IOTA:C_IOTA + P] = np.arange(P)
    for q in range(4):
        for r in range(2):
            c[32 * q + r, C_SELB + P * r:C_SELB + P * (r + 1)] = 1
            c[32 * q + r, C_SELC + r] = 1
    half = HD // 2
    inv = (np.float32(10000.0) ** (-np.arange(0, half, 2, dtype=np.float32) / np.float32(half))).astype(np.float32)
    tok = np.arange(NLAT * P)
    row, col = (tok // HD).astype(np.float32), (tok % HD).astype(np.float32)
    ar, ac = row[:, None] * inv, col[:, None] * inv
    ang = np.concatenate([ar, ar, ac, ac], -1)
    sgn = np.concatenate([-np.ones(16), np.ones(16)] * 2).astype(np.float32)
    cos, sin = np.cos(ang).astype(np.float32), np.sin(ang).astype(np.float32) * sgn
    c[:, C_COS:C_COS + 128] = cos.reshape(NLAT, P, HD).transpose(1, 0, 2).reshape(P, 128)
    c[:, C_SIN:C_SIN + 128] = sin.reshape(NLAT, P, HD).transpose(1, 0, 2).reshape(P, 128)
    return c


class Unit:

    def __init__(self, k, s, a, src, split, shape):
        self.k, self.s, self.a, self.src, self.split, self.shape = k, s, a, src, split, shape


def plan_units(ada_w, w_in, w_out, w1, w3, w2):
    units, at = [], {}
    n = dict(s=0, a=0)

    def add(key, src, split, shape):
        u = Unit(len(units), n["s"] if split else None, None if split else n["a"], src, split, shape)
        n["s" if split else "a"] += 1
        units.append(u)
        at.setdefault(key, []).append(u)

    def tall(w, k0, nk, c0, nc_):
        return w[k0 * P:(k0 + nk) * P, c0:c0 + nc_].rearrange("(k p) n -> p k n", p=P)

    for l in range(2):
        for c in range(12):
            for u in range(4):
                add(("ada", l, c), tall(ada_w[l], 2 * u, 2, 512 * c, 512), False, (2, 512))
        for j in range(5):
            for u in range(4):
                add(("in", l, j), tall(w_in[l], 2 * u, 2, 512 * j, 512), True, (2, 512))
        for n2 in range(2):
            for u in range(4):
                add(("out", l, n2), tall(w_out[l], 2 * u, 2, 512 * n2, 512), True, (2, 512))
        if l == 0:
            for g, c0 in enumerate(range(0, 22, 4)):
                gc = min(4, 22 - c0)
                for c in range(c0, c0 + gc, 2):
                    for key, w in (("w1", w1), ("w3", w3)):
                        for h in range(2):
                            add((key, c), tall(w[0], 4 * h, 4, P * c, 2 * P), True, (4, 256))
                for n2 in range(2):
                    for c in range(c0, c0 + gc, 2):
                        add(("w2", g, n2), tall(w2[0], c, 2, 512 * n2, 512), True, (2, 512))
    return units, at, n["s"]


def program(nc, x, c, ctx, c_ctx, ada_w, ada_b, pre_mix_g, post_mix_g, pre_ffn_g, post_ffn_g, w_in, w_out,
            lam_q1, lam_k1, lam_q2, lam_k2, subln_g, sg_ln_g, sg_ln_b, sg_w, sg_b, ffn_w1, ffn_w3, ffn_w2,
            router_w, moe_w1, moe_w3, moe_w2, const, out):
    units, at, NS0 = plan_units(ada_w, w_in, w_out, ffn_w1, ffn_w3, ffn_w2)
    K0 = len(units)
    split_units = [u for u in units if u.split]

    with ExitStack() as stack:
        def sem(name):
            return stack.enter_context(nc.semaphore(name))

        end = [16512]

        def place(name, shape, dt, offset=None):
            size = 4 * int(np.prod(shape[1:]))
            if offset is None:
                offset = end[0]
                end[0] += -(-size // 32) * 32
            return nc.alloc_sbuf_tensor_at(name, shape, dt, offset=offset)

        raw = place("raw", [P, RAW, UW], F32)
        w_hi = place("w_hi", [P, SPL, UW], F32R)
        w_lo = place("w_lo", [P, SPL, UW], F32R)
        xs = place("xs", [P, NB, D], F32)
        H = end[0]
        hT_hi = place("hT_hi", [P, KD, 512], F32R)
        hT_lo = place("hT_lo", [P, KD, 512], F32R)
        cst = place("cst", [P, C_END], F32)
        pcol = place("pcol", [P, 2, 68], F32)
        cstat = place("cstat", [P, KD, 32], F32)
        mod_a = place("mod_a", [P, 2, KD, 2], F32)
        mod_b = place("mod_b", [P, 2, KD, 2], F32)
        sub_bc = place("sub_bc", [P, 2, P], F32)
        lng_bc = place("lng_bc", [P, 2, SG], F32)
        lnb_bc = place("lnb_bc", [P, 2, SG], F32)
        lam_s = place("lam_s", [P, 2, 8], F32)
        rs = place("rs", [P, 128], F32)
        idx = place("idx", [P, NLAT, 8], U32)
        st = place("st", [P, 64], F32)
        st2 = place("st2", [P, 128], F32)
        att = place("att", [P, 2, 8], F32)
        flag = place("flag", [P, 1], I32)
        ab_bc = place("ab_bc", [P, D], F32)
        pg_bc = place("pg_bc", [P, D], F32)
        arow = place("arow", [P, 2, 512], F32)
        wsT = place("wsT", [P, SG], F32)
        gg = place("gg", [P, 2, 2, D], F32)
        G1 = end[0] - 4 * 4 * D
        Z = end[0]
        proj = place("proj", [P, NB, IN], F32, Z)
        xn = place("xn", [P, NB, D], F32, Z)
        hT32 = place("hT32", [P, KD, 512], F32, Z + 16384)
        rk = place("rk", [P, NB, D], F32, H)
        qT = place("qT", [P, HEADS, 512], F32, H + 16384)
        kT = place("kT", [P, HEADS, 512], F32, H + 24576)
        pr = place("pr", [P, 2, 2, 512], F32, Z + 40960)
        wT = place("wT", [P, 2, 512], F32, Z + 49152)
        rtmp = place("rtmp", [P, D], F32, Z + 40960)
        ws_raw = place("ws_raw", [P, SG], F32, Z + 53248)
        osq = place("osq", [P, P], F32, Z + 55296)
        rows = place("rows", [68, 2, P], F32, Z + 32768)
        crow = place("crow", [16, P], F32, Z + 33792)
        lam_bc = place("lam_bc", [P, 2, 4, HD], F32, Z + 34304)
        lam_t = place("lam_t", [P, 2, 2, HD], F32, Z + 36352)
        y0 = place("y0", [P, NB, D], F32, Z)
        at_hi = place("at_hi", [P, ATS, 512], F32R, Z + 16384)
        at_lo = place("at_lo", [P, ATS, 512], F32R, Z + 28672)
        ptmp = place("ptmp", [P, D], F32, Z + 40960)
        sgf = place("sgf", [P, 2, 512], F32, Z + 45056)
        a32 = place("a32", [P, 2, 512], F32, Z + 49152)
        xg_hi = place("xg_hi", [P, NLAT, D], F32R, H)
        xg_lo = place("xg_lo", [P, NLAT, D], F32R, H + 8192)
        he_hi = place("he_hi", [P, KD, P], F32R, H + 16384)
        he_lo = place("he_lo", [P, KD, P], F32R, H + 20480)
        he32 = place("he32", [P, KD, P], F32, H + 24576)
        rw = place("rw", [P, KD, NE], F32, H + 28672)
        yg = place("yg", [P, NE, D], F32, Z)
        Z2 = Z + 32768
        perm = place("perm", [P, NE, NLAT, P], F32R, Z2)
        scat = place("scat", [P, NE, NLAT * P], F32R, Z2 + 8192)
        ae_hi = place("ae_hi", [P, 2, 512], F32R, G1 + 4096)
        sge = place("sge", [P, 2, 512], F32, Z2 + 16384)
        ae32 = place("ae32", [P, 2, 512], F32, Z2 + 20480)
        ae_lo = place("ae_lo", [P, 2, 512], F32R, G1 + 12288)
        yh = place("yh", [P, 2, D], F32R, H + 16384)
        yl = place("yl", [P, 2, D], F32R, Z2 + 16384)
        ptm = place("ptm", [P, D], F32, Z)
        junk = place("junk", [P, D], F32, Z + 4096)
        assert Z2 + 24576 <= nc.sbuf_usable_end, (Z2 + 24576, nc.sbuf_usable_end)
        yout = xs[:, 2:4, :]
        ps = stack.enter_context(nc.psum_tensor("ps", [P, 8, 512], F32))

        ident = cst[:, C_ID:C_ID + P]
        ones = cst[:, C_ONES:C_ONES + P]
        triu = cst[:, C_TRIU:C_TRIU + P]
        iota = cst[:, C_IOTA:C_IOTA + P]

        raw_in = [sem(f"raw_in{i}") for i in range(RAW)]
        hi_done, lo_done = sem("hi_done"), sem("lo_done")
        unit_used, ada_used = sem("unit_used"), sem("ada_used")
        s_small, s_x, s_bc, s_out = sem("s_small"), sem("s_x"), sem("s_bc"), sem("s_out")
        dve_ch, act_ch = sem("dve_ch"), sem("act_ch")
        S = {}

        def sg(name):
            if name not in S:
                S[name] = sem(name.replace(" ", "_"))
            return S[name]

        def view(ring, u):
            return ring.rearrange("p (k n) -> p k n", k=u.shape[0])

        def raw_at(k):
            return raw[:, k % RAW, :]

        def raw_count(k):
            return 16 * (k // RAW + 1)

        block = stack.enter_context(nc.Block())

        def blocks(l):
            return range(NB)

        def in_blocks(l, j):
            return range(NB) if l == 0 or j in (1, 2) else range(NLAT)

        def out_blocks(l):
            return range(NB) if l == 0 else range(NLAT)

        items = {l: [(b, h) for b in out_blocks(l) for h in range(HEADS)] for l in range(2)}
        qk = {l: [(t, b) for b in range(NB) for t in ((0, 1) if l == 0 or b < NLAT else (1,))] for l in range(2)}
        proj_n = {l: [sum(len(in_blocks(l, i)) for i in range(j + 1)) for j in range(5)] for l in range(2)}
        layer_end = at["w2", 5, 1][-1].s
        groups = [(c0, min(4, 22 - c0)) for c0 in range(0, 22, 4)]

        def expert_units():
            seq = []
            for s in range(STEPS):
                seq += [(0, s, n) for n in range(4)] + [(1, s, n) for n in range(4)]
                if s:
                    seq += [(2, s - 1, 4 * (s - 1) + n) for n in range(4)]
            return seq + [(2, STEPS - 1, 4 * (STEPS - 1) + n) for n in range(4)]

        def end_w1(s):
            return 3 if s == 0 else 12 * s - 1

        def end_w3(s):
            return end_w1(s) + 4

        def end_w2(s):
            return end_w3(s + 1) + 4 if s + 1 < STEPS else UE - 1

        def ggc(l, g, n):
            return l * 8 + g * (4 if l == 0 else 2) + n

        def streams(l):
            return (0, 1) if l == 0 else (0,)

        NSMALL = 16 * 11

        @block.sync
        def _(sp):
            small = [(cst[:, :], const), (crow[0:8, :], c.rearrange("a (k p) -> (a k) p", p=P)),
                     (crow[8:16, :], c_ctx.rearrange("(k p) -> k p", p=P))]
            for l in range(2):
                small += [(rows[0:48, l, :], ada_b[l].rearrange("(k p) -> k p", p=P)),
                          (rows[48:56, l, :], pre_mix_g[l].rearrange("(k p) -> k p", p=P)),
                          (rows[56:64, l, :], pre_ffn_g[l].rearrange("(k p) -> k p", p=P)),
                          (rows[64:68, l, :], sg_b[l])]
            for dst, src in small:
                sp.dma_start(dst, src).then_inc(s_small, 16)
            xv = x.rearrange("a (b p) d -> p (a b) d", p=P)
            cv = ctx.rearrange("a (b p) d -> p (a b) d", p=P)
            for b in range(NB):
                sp.dma_start(xs[:, b, :], xv[:, b, :] if b < NLAT else cv[:, b - NLAT, :]).then_inc(s_x, 16)
            for u in units:
                if u.k >= RAW:
                    o = units[u.k - RAW]
                    sp.wait_ge(*((lo_done, o.s + 1) if o.split else (ada_used, o.a + 1)))
                sp.dma_start(view(raw_at(u.k), u), u.src).then_inc(raw_in[u.k % RAW], 16)

            def experts(turn):
                base = turn * NE * UE
                with sp.Fori(0, NE) as e:
                    for i, (w, s, n) in enumerate(expert_units()):
                        sp.wait_ge(lo_done, e * UE + (NS0 + base + i - RAW + 1))
                        k = K0 + base + i
                        if w == 2:
                            src, dst = moe_w2[0][e][n * P:(n + 1) * P, :], raw_at(k)
                        else:
                            wt = moe_w1 if w == 0 else moe_w3
                            src = wt[0][e][2 * n * P:2 * (n + 1) * P, 512 * s:512 * s + 512].rearrange("(k p) n -> p k n", p=P)
                            dst = raw_at(k).rearrange("p (k n) -> p k n", k=2)
                        sp.dma_start(dst, src).then_inc(raw_in[k % RAW], 16)

            experts(0)
            sp.wait_ge(sg("flag set"), 1)
            busiest = sp.value_load(flag[0:1, 0:1], min_val=0, max_val=NLAT * P)
            with sp.If(busiest > P):
                experts(1)
            for b in range(NLAT):
                sp.wait_ge(sg("final x"), b + 1)
                sp.dma_start(out.rearrange("a (b p) d -> p (a b) d", p=P)[:, b, :], xs[:, b, :]).then_inc(s_out, 16)
            sp.wait_ge(s_out, 16 * NLAT)

        @block.gpsimd
        def _(pool):
            for l in range(2):
                for i, v in enumerate((lam_q1, lam_k1, lam_q2, lam_k2)):
                    pool.dma_start(lam_bc[:, l, i, :], v[l].partition_broadcast(P)).then_inc(sg("params in"), 16)
                pool.dma_start(sub_bc[:, l, :], subln_g[l].partition_broadcast(P)).then_inc(sg("params in"), 16)
                pool.dma_start(lng_bc[:, l, :], sg_ln_g[l].partition_broadcast(P)).then_inc(sg("params in"), 16)
                pool.dma_start(lnb_bc[:, l, :], sg_ln_b[l].partition_broadcast(P)).then_inc(sg("params in"), 16)
            for l in range(2):
                if l:
                    pool.wait_ge(sg("wsT ps"), l)
                pool.dma_start(ws_raw[:, :].rearrange("p (g q) -> p g q", g=4), sg_w[l].rearrange("g p q -> p g q")).then_inc(sg("ws in"), 16)
                for g, (part, gain) in enumerate(((2, post_mix_g), (5, post_ffn_g))):
                    if l + g:
                        pool.wait_ge(sg("gg done"), ggc(l, g, 0))
                    pool.dma_start(ab_bc[:, :], ada_b[l][part * D:(part + 1) * D].partition_broadcast(P)).then_inc(s_bc, 16)
                    pool.dma_start(pg_bc[:, :], gain[l].partition_broadcast(P)).then_inc(s_bc, 16)
            pool.wait_ge(unit_used, NS0)
            pool.dma_start(rw[:, :, :], router_w[0].rearrange("(k p) e -> p k e", p=P)).then_inc(sg("rw in"), 16)

        @block.tensor
        def _(pe):
            def mm3(o, lh, ll, rh, rl, start, stop):
                pe.matmul(o, lh, rh, start=start, stop=False)
                pe.matmul(o, lh, rl, start=False, stop=False)
                return pe.matmul(o, ll, rh, start=False, stop=stop)

            def split_at(s):
                return w_hi[:, s % SPL, :], w_lo[:, s % SPL, :]

            pe.wait_ge(s_small, NSMALL)
            pe.transpose(ps[:, 0, 0:16], crow[:, :], ident[0:16, 0:16]).then_inc(sg("small T"), 1)
            for l in range(2):
                pe.transpose(ps[:, 1 + l, 0:68], rows[:, l, :], ident[0:68, 0:68]).then_inc(sg("small T"), 1)

            def ada(l):
                def post(c):
                    part = c // 2
                    pe.wait_ge(sg("arow"), 12 * l + c + 1)
                    if part in (2, 5):
                        g = part // 3
                        for r in streams(l):
                            n = ggc(l, g, (c % 2) * len(streams(l)) + r)
                            if n >= len(streams(l)):
                                pe.wait_ge(sg("gg done"), n - len(streams(l)) + 1 if l == 0 else n)
                            m = pe.matmul(ps[:, 3 + r, :], cst[:, C_SELB + P * r:C_SELB + P * r + P], arow[:, c % 2, :],
                                          start=True, stop=True)
                    else:
                        if c % 6 == 0 and (l or c):
                            pe.wait_ge(sg("mod done"), 4 * l + 2 * (c // 6))
                        for j in range(4):
                            o = ((part % 3) * KD + (c % 2) * 4 + j) * 2
                            m = pe.matmul(ps[:, 2, o:o + 2], arow[:, c % 2, P * j:P * j + P], cst[:, C_SELC:C_SELC + 2],
                                          start=True, stop=True)
                    m.then_inc(sg("ada post"), 1)

                pe.wait_ge(sg("cstat"), 1 + 2 * KD)
                pe.wait_ge(sg("pcol"), 2)
                for c in range(12):
                    if 12 * l + c >= 2:
                        pe.wait_ge(sg("arow"), 12 * l + c - 1)
                    for u in at["ada", l, c]:
                        pe.wait_ge(raw_in[u.k % RAW], raw_count(u.k))
                        w = view(raw_at(u.k), u)
                        for kk in range(2):
                            k = 2 * (u.a % 4) + kk
                            q = k % 4
                            m = pe.matmul(ps[32 * q:32 * q + 32, c % 2, :], cstat[:, k, :], w[:, kk, :],
                                          start=(k < 4), stop=(k >= 4), tile_position=(0, 32 * q))
                        m.then_inc(ada_used, 1)
                    if c:
                        post(c - 1)
                post(11)

            def turn_h(key, bank, nb):
                pe.wait_ge(sg("xn " + key), nb)
                for k in range(KD):
                    if k >= 2:
                        pe.wait_ge(sg("hT32 " + key), k - 1)
                    for b in range(nb):
                        m = pe.transpose(ps[:, bank + k % 2, P * b:P * b + P], xn[:, b, P * k:P * k + P], ident)
                    m.then_inc(sg("hT ps " + key), 1)

            def project_in(l):
                pe.wait_ge(sg("hT mix%d" % l), KD)
                pe.wait_ge(sg("gg done"), ggc(l + 1, 0, 0) if l == 0 else 12)
                pe.wait_ge(sg("mod done"), 4 * (l + 1))
                for j in range(5):
                    if j >= 2:
                        pe.wait_ge(sg("proj%d" % l), proj_n[l][j - 2])
                    for i, u in enumerate(at["in", l, j]):
                        pe.wait_ge(lo_done, u.s + 1)
                        h, lo = (view(t, u) for t in split_at(u.s))
                        for kk in range(2):
                            k = 2 * i + kk
                            for b in in_blocks(l, j):
                                m = mm3(ps[:, 4 * (j % 2) + b, :], hT_hi[:, k, P * b:P * b + P], hT_lo[:, k, P * b:P * b + P],
                                        h[:, kk, :], lo[:, kk, :], k == 0, k == KD - 1)
                        m.then_inc(unit_used, 1)

            def turn_qk(l):
                pe.wait_ge(sg("proj%d" % l), proj_n[l][4])
                for i, (t, b) in enumerate(qk[l]):
                    if b < NLAT:
                        pe.wait_ge(sg("rope%d" % l), b + 1)
                    if i >= 2:
                        pe.wait_ge(sg("qkT%d" % l), i - 1)
                    src = rk[:, b, :] if b < NLAT else proj[:, b, 0:D]
                    for h in range(HEADS):
                        m = pe.transpose(ps[:, i % 2, P * h:P * h + P], src[:, t * DA + P * h:t * DA + P * h + P], ident)
                    m.then_inc(sg("qk ps%d" % l), 1)

            def spatial(l):
                pe.wait_ge(sg("ws in"), 16 * (l + 1))
                for g in range(4):
                    m = pe.transpose(ps[:, 2, P * g:P * g + P], ws_raw[:, P * g:P * g + P], ident)
                m.then_inc(sg("wsT ps"), 1)
                pe.wait_ge(sg("wsT"), l + 1)
                for b in out_blocks(l):
                    pe.wait_ge(sg("vn%d" % l), b + 1)
                    for g in range(4):
                        m = pe.matmul(ps[:, 4 + b, P * g:P * g + P], wsT[:, P * g:P * g + P],
                                      proj[:, b, 4 * DA + P * g:4 * DA + P * g + P], start=True, stop=True)
                    m.then_inc(sg("mixed%d" % l), 1)

            def attend(l):
                its = items[l]
                n = len(its)
                pe.wait_ge(sg("qkT%d" % l), len(qk[l]))
                pe.wait_ge(sg("gated%d" % l), len(out_blocks(l)))
                for t in range(n + 2):
                    if t < n:
                        b, h = its[t]
                        k0 = 0 if b < NLAT else 256
                        if t >= 2:
                            pe.wait_ge(sg("exp%d" % l), 2 * (t - 1))
                        for m_ in range(2):
                            m = pe.matmul(ps[:, 2 * (t % 2) + m_, 0:512 - k0], qT[HD * m_:HD * m_ + HD, h, P * b:P * b + P],
                                          kT[HD * m_:HD * m_ + HD, h, k0:512], start=True, stop=True)
                        m.then_inc(sg("scores%d" % l), 1)
                    if 1 <= t <= n:
                        i = t - 1
                        b, h = its[i]
                        nk = 4 if b < NLAT else 2
                        pe.wait_ge(sg("weights%d" % l), i + 1)
                        if i >= 2:
                            pe.wait_ge(sg("wT%d" % l), i - 1)
                        for kb in range(nk):
                            m = pe.transpose(ps[:, 4 + i % 2, P * kb:P * kb + P], pr[:, i % 2, 0, P * kb:P * kb + P], ident)
                        m.then_inc(sg("wT ps%d" % l), 1)
                    if t >= 2:
                        i = t - 2
                        b, h = its[i]
                        kb0, nk = (0, 4) if b < NLAT else (2, 2)
                        pe.wait_ge(sg("wT%d" % l), i + 1)
                        if i >= 2:
                            pe.wait_ge(sg("o%d" % l), i - 1)
                        for kb in range(nk):
                            m = pe.matmul(ps[:, 6 + i % 2, 0:P], wT[:, i % 2, P * kb:P * kb + P],
                                          proj[:, kb0 + kb, 2 * DA + P * h:2 * DA + P * h + P], start=(kb == 0), stop=(kb == nk - 1))
                        m.then_inc(sg("pv%d" % l), 1)

            def turn_cat(l):
                nb = len(out_blocks(l))
                pe.wait_ge(sg("cat%d" % l), nb * HEADS)
                for k in range(KD):
                    if k >= 2:
                        pe.wait_ge(sg("catT"), KD * l + k - 1)
                    for b in range(nb):
                        col = P * k if k < 4 else 3 * DA + P * (k - 4)
                        m = pe.transpose(ps[:, k % 2, P * b:P * b + P], proj[:, b, col:col + P], ident)
                    m.then_inc(sg("catT ps"), 1)

            def project_out(l):
                pe.wait_ge(sg("catT"), KD * (l + 1))
                for n2 in range(2):
                    for i, u in enumerate(at["out", l, n2]):
                        pe.wait_ge(lo_done, u.s + 1)
                        h, lo = (view(t, u) for t in split_at(u.s))
                        for kk in range(2):
                            k = 2 * i + kk
                            for b in out_blocks(l):
                                m = mm3(ps[:, 2 * b + n2, :], hT_hi[:, k, P * b:P * b + P], hT_lo[:, k, P * b:P * b + P],
                                        h[:, kk, :], lo[:, kk, :], k == 0, k == KD - 1)
                        m.then_inc(unit_used, 1)

            def ffn():
                pe.wait_ge(sg("hT ffn0"), KD)
                for g, (c0, gc) in enumerate(groups):
                    for c in range(c0, c0 + gc, 2):
                        for wi, key in enumerate(("w1", "w3")):
                            if c >= 2:
                                pe.wait_ge(sg(("silu", "gated up")[wi]), c)
                            for i, u in enumerate(at[key, c]):
                                pe.wait_ge(lo_done, u.s + 1)
                                h, lo = (view(t, u) for t in split_at(u.s))
                                for ci in range(2):
                                    for kk in range(4):
                                        k = 4 * i + kk
                                        m = mm3(ps[:, 2 * wi + ci, :], h[:, kk, P * ci:P * ci + P], lo[:, kk, P * ci:P * ci + P],
                                                hT_hi[:, k, :], hT_lo[:, k, :], k == 0, k == KD - 1)
                                m.then_inc(unit_used, 1)
                    for n2 in range(2):
                        us = at["w2", g, n2]
                        for i, u in enumerate(us):
                            pe.wait_ge(lo_done, u.s + 1)
                            pe.wait_ge(sg("AT"), c0 + 2 * i + 2)
                            h, lo = (view(t, u) for t in split_at(u.s))
                            for b in range(NB):
                                if i == 0 and 2 * g + n2 > 0:
                                    pe.wait_ge(sg("y sum"), NB * (2 * g + n2 - 1) + b + 1)
                                for kk in range(2):
                                    a = (c0 + 2 * i + kk) % ATS
                                    m = mm3(ps[:, 4 + b, :], at_hi[:, a, P * b:P * b + P], at_lo[:, a, P * b:P * b + P],
                                            h[:, kk, :], lo[:, kk, :], i == 0 and kk == 0, i == len(us) - 1 and kk == 1)
                                if i == len(us) - 1 and b < NB - 1:
                                    m.then_inc(sg("y part"), 1)
                            m.then_inc(unit_used, 1)

            def route():
                pe.wait_ge(sg("hT32 ffn1"), KD)
                pe.wait_ge(sg("rw in"), 16)
                for tb in range(NLAT):
                    for k in range(KD):
                        m = pe.matmul(ps[:, 0, NE * tb:NE * tb + NE], hT32[:, k, P * tb:P * tb + P], rw[:, k, :],
                                      start=(k == 0), stop=(k == KD - 1))
                m.then_inc(sg("logits"), 1)
                pe.wait_ge(sg("mask"), 1)
                mask = st2[:, 64:80]
                pe.matmul(ps[:, 1, 0:8], triu, mask[:, 0:8], start=True, stop=True)
                pe.matmul(ps[:, 1, 8:16], ones, mask[:, 0:8], start=True, stop=False)
                pe.matmul(ps[:, 1, 8:16], triu, mask[:, 8:16], start=False, stop=True)
                pe.matmul(ps[:, 1, 16:24], ones, mask[:, 0:8], start=True, stop=False)
                pe.matmul(ps[:, 1, 16:24], ones, mask[:, 8:16], start=False, stop=True).then_inc(sg("counts"), 1)

            def permute(turn):
                pe.wait_ge(sg("perm"), NE * (turn + 1))
                for e in range(NE):
                    for tb in range(NLAT):
                        m = pe.matmul(ps[:, 0, e:e + 1], perm[:, e, tb, :].bitcast(F32), st2[:, 80 + 8 * tb + e:81 + 8 * tb + e],
                                      start=(tb == 0), stop=(tb == 1))
                m.then_inc(sg("slot gates"), 1)
                for e in range(NE):
                    if e >= 2:
                        pe.wait_ge(sg("scat"), NE * turn + e - 1)
                    for tb in range(NLAT):
                        m = pe.transpose(ps[:, 2 + e % 2, P * tb:P * tb + P], perm[:, e, tb, :].bitcast(F32), ident)
                    m.then_inc(sg("scat ps"), 1)
                pe.wait_ge(sg("scat"), NE * (turn + 1))
                pe.wait_ge(sg("slot gate"), turn + 1)

            def experts(turn):
                base = NS0 + turn * NE * UE
                with pe.Fori(0, NE) as e:
                    def took(s):
                        return e * UE + (base + s + 1)

                    for k in range(KD):
                        for tb in range(NLAT):
                            for part, src in enumerate((xg_hi, xg_lo)):
                                m = pe.matmul(ps[:, 2 + k // 4, P * (k % 4):P * (k % 4) + P], src[:, tb, P * k:P * k + P],
                                              perm[:, e, tb, :], start=(tb + part == 0), stop=(tb + part == 2))
                        if k % 4 == 3:
                            m.then_inc(sg("gathered"), 1)
                    pe.wait_ge(sg("he"), e + (NE * turn + 1))

                    def up(s, w):
                        for n in range(4):
                            i = (end_w1, end_w3)[w](s) - 3 + n
                            pe.wait_ge(lo_done, took(i))
                            for kk in range(2):
                                k = 2 * n + kk
                                r = [t[:, (base + i) % SPL, 512 * kk:512 * kk + 512] for t in (w_hi, w_lo)]
                                m = mm3(ps[:, 2 * (s % 2) + w, :], he_hi[:, k, :], he_lo[:, k, :], *r, k == 0, k == KD - 1)
                            m.then_inc(unit_used, 1)

                    def turn_a(s):
                        pe.wait_ge(sg("ae32"), e * STEPS + (STEPS * NE * turn + s + 1))
                        for j in range(4):
                            m = pe.transpose(ps[:, 4 + s % 2, P * j:P * j + P], ae32[:, s % 2, P * j:P * j + P], ident)
                        m.then_inc(sg("ae ps"), 1)

                    def down(s):
                        pe.wait_ge(sg("ae"), e * STEPS + (STEPS * NE * turn + s + 1))
                        for n in range(4):
                            i = end_w2(s) - 3 + n
                            pe.wait_ge(lo_done, took(i))
                            for n2 in range(2):
                                r = [t[:, (base + i) % SPL, 512 * n2:512 * n2 + 512] for t in (w_hi, w_lo)]
                                m = mm3(ps[:, 6 + n2, :], ae_hi[:, s % 2, P * n:P * n + P], ae_lo[:, s % 2, P * n:P * n + P],
                                        *r, s == 0 and n == 0, s == STEPS - 1 and n == 3)
                            m.then_inc(unit_used, 1)

                    for s in range(STEPS):
                        up(s, 0)
                        if s:
                            turn_a(s - 1)
                        up(s, 1)
                        if s:
                            down(s - 1)
                    turn_a(STEPS - 1)
                    down(STEPS - 1)
                    pe.wait_ge(sg("yg"), e + (NE * turn + 1))

            def combine(turn):
                for e in range(NE):
                    pe.wait_ge(sg("y split"), NE * turn + e + 1)
                    for tb in range(NLAT):
                        for n2 in range(2):
                            for part, src in enumerate((yh, yl)):
                                m = pe.matmul(ps[:, 2 * tb + n2, :], scat[:, e, P * tb:P * tb + P],
                                              src[:, e % 2, 512 * n2:512 * n2 + 512],
                                              start=(e == 0 and part == 0), stop=(e == NE - 1 and part == 1))
                    m.then_inc(sg("combined"), 1)
                pe.wait_ge(sg("yout"), NLAT * (turn + 1))

            for l in range(2):
                ada(l)
                turn_h("mix%d" % l, 5, NB)
                project_in(l)
                turn_qk(l)
                spatial(l)
                attend(l)
                turn_cat(l)
                project_out(l)
                turn_h("ffn%d" % l, 0, len(out_blocks(l)))
                if l == 0:
                    ffn()
            route()
            permute(0)
            experts(0)
            combine(0)
            pe.wait_ge(sg("flag set"), 1)
            busiest = pe.value_load(flag[0:1, 0:1], min_val=0, max_val=NLAT * P)
            with pe.If(busiest > P):
                permute(1)
                experts(1)
                combine(1)

        @block.scalar
        def _(act):
            cur = [0]
            chain = [0]
            stage_end = [layer_end]

            def link(ins):
                chain[0] += 1
                ins.then_inc(act_ch, 1)
                act.wait_ge(act_ch, chain[0])

            def split_upto(s):
                s = min(s, stage_end[0])
                while cur[0] <= s:
                    u = split_units[cur[0]]
                    act.wait_ge(raw_in[u.k % RAW], raw_count(u.k))
                    if u.s >= SPL:
                        act.wait_ge(unit_used, u.s - SPL + 1)
                    act.activation(w_hi[:, u.s % SPL, :], raw_at(u.k), ACT.Copy).then_inc(hi_done, 1)
                    cur[0] += 1

            def last_s(key):
                return at[key][-1].s

            act.wait_ge(sg("cstat"), 1)
            act.wait_ge(sg("small T"), 3)
            for r in range(2):
                for k in range(KD):
                    act.activation(cstat[:, k, r:r + 1], ps[:, 0, KD * r + k:KD * r + k + 1], ACT.Silu).then_inc(sg("cstat"), 1)

            act.wait_ge(sg("lam dots"), 1)
            act.activation(lam_s[:, :, 2:4], lam_s[:, :, 0:2], ACT.Exp).then_inc(sg("lam exp"), 1)

            def prenorm(key, l, which, nb):
                for b in range(nb):
                    if key == "mix0":
                        act.wait_ge(s_x, 16 * NB)
                    else:
                        act.wait_ge(sg("x " + ("ffn" if which == 0 else "mix%d" % l)), b + 1)
                    act.activation(xn[:, b, :], xs[:, b, :], ACT.Square, accum_out=st[:, b:b + 1]).then_inc(sg("ss " + key), 1)
                act.wait_ge(sg("ms " + key), 1)
                act.activation(st[:, 8:8 + nb], st[:, 4:4 + nb], ACT.Sqrt).then_inc(sg("rt " + key), 1)
                act.wait_ge(sg("mod done"), 4 * l + 2 * (which + 1))
                for k in range(KD):
                    act.wait_ge(sg("hT ps " + key), k + 1)
                    bank = (5 if which == 0 else 0) + k % 2
                    for r in range(nb // 2):
                        ins = act.activation(hT32[:, k, 256 * r:256 * r + 256], ps[:, bank, 256 * r:256 * r + 256], ACT.Identity,
                                             bias=mod_b[:, which, k, r:r + 1], scale=mod_a[:, which, k, r:r + 1])
                    ins.then_inc(sg("hT32 " + key), 1)

            def postnorm(key, srcs, junk_):
                for b, src in enumerate(srcs):
                    if b:
                        act.wait_ge(sg("ss " + key), b)
                    act.activation(junk_(b, src), src, ACT.Square, accum_out=st[:, 16 + b:17 + b]).then_inc(sg("ss " + key), 1)
                act.wait_ge(sg("ms " + key), 1)
                act.activation(st[:, 24:24 + len(srcs)], st[:, 20:20 + len(srcs)], ACT.Sqrt).then_inc(sg("rt " + key), 1)

            for l in range(2):
                nb = len(out_blocks(l))
                if l == 1:
                    act.wait_ge(sg("x ffn"), NB)
                    stage_end[0] = NS0 - 1
                prenorm("mix%d" % l, l, 0, NB)
                for j in range(5):
                    split_upto(last_s(("in", l, j)) + AHEAD)
                    act.wait_ge(unit_used, last_s(("in", l, j)) + 1)
                    if j == 0:
                        act.wait_ge(sg("hT mix%d" % l), KD)
                    for b in in_blocks(l, j):
                        act.activation(proj[:, b, 512 * j:512 * j + 512], ps[:, 4 * (j % 2) + b, :], ACT.Copy)\
                            .then_inc(sg("proj%d" % l), 1)
                for i, (t, b) in enumerate(qk[l]):
                    act.wait_ge(sg("qk ps%d" % l), i + 1)
                    dst = (qT, kT)[t]
                    act.activation(dst[:, :, P * b:P * b + P], ps[:, i % 2, :].rearrange("p (h t) -> p h t", h=HEADS), ACT.Copy)\
                        .then_inc(sg("qkT%d" % l), 1)
                act.wait_ge(sg("wsT ps"), l + 1)
                act.activation(wsT[:, :], ps[:, 2, :], ACT.Copy).then_inc(sg("wsT"), 1)
                act.wait_ge(sg("ln ms%d" % l), 1)
                act.activation(st[:, 44:44 + nb], st[:, 40:40 + nb], ACT.Sqrt).then_inc(sg("ln rt%d" % l), 1)
                its = items[l]
                n = len(its)
                for t in range(n + 2):
                    if t < n:
                        nk = 512 if its[t][0] < NLAT else 256
                        act.wait_ge(sg("rowmax%d" % l), t + 1)
                        if t >= 2:
                            act.wait_ge(sg("wT ps%d" % l), t - 1)
                        for m_ in range(2):
                            act.activation(pr[:, t % 2, m_, 0:nk], ps[:, 2 * (t % 2) + m_, 0:nk], ACT.Exp, scale=SCALE,
                                           bias=att[:, t % 2, 2 + m_:3 + m_], accum_out=att[:, t % 2, 4 + m_:5 + m_])\
                                .then_inc(sg("exp%d" % l), 1)
                    if 1 <= t <= n:
                        i = t - 1
                        nk = 512 if its[i][0] < NLAT else 256
                        act.wait_ge(sg("wT ps%d" % l), i + 1)
                        if i >= 2:
                            act.wait_ge(sg("pv%d" % l), i - 1)
                        act.activation(wT[:, i % 2, 0:nk], ps[:, 4 + i % 2, 0:nk], ACT.Copy).then_inc(sg("wT%d" % l), 1)
                    if t >= 2:
                        i = t - 2
                        b, h = its[i]
                        act.wait_ge(sg("o%d" % l), i + 1)
                        if i:
                            act.wait_ge(sg("o sq%d" % l), i)
                        act.activation(osq[:, :], proj[:, b, P * h:P * h + P], ACT.Square,
                                       accum_out=st2[:, i:i + 1]).then_inc(sg("o sq%d" % l), 1)
                act.wait_ge(sg("o ms%d" % l), 1)
                act.activation(st2[:, 32:32 + n], st2[:, 16:16 + n], ACT.Sqrt).then_inc(sg("o rt%d" % l), 1)
                split_upto(at["out", l, 0][0].s + AHEAD)
                for k in range(KD):
                    act.wait_ge(sg("catT ps"), KD * l + k + 1)
                    act.activation(hT_hi[:, k, 0:P * nb], ps[:, k % 2, 0:P * nb], ACT.Copy).then_inc(sg("catT hi"), 1)
                split_upto(last_s(("out", l, 1)))
                act.wait_ge(unit_used, last_s(("out", l, 1)) + 1)
                postnorm("pm%d" % l, [ps[:, 2 * b:2 * b + 2, :] for b in out_blocks(l)],
                         lambda b, src: xn[:, b, :].rearrange("p (a n) -> p a n", a=2))
                prenorm("ffn%d" % l, l, 1, nb)
                if l == 0:
                    split_upto(at["w1", 0][0].s + AHEAD)
                    for g, (c0, gc) in enumerate(groups):
                        for c in range(c0, c0 + gc, 2):
                            split_upto(last_s(("w1", c)) + AHEAD)
                            act.wait_ge(unit_used, last_s(("w1", c)) + 1)
                            if c >= 2:
                                act.wait_ge(sg("gated up"), c)
                            for ci in range(2):
                                act.activation(sgf[:, ci, :], ps[:, ci, :], ACT.Silu).then_inc(sg("silu"), 1)
                            split_upto(last_s(("w3", c)) + AHEAD)
                            for ci in range(2):
                                act.wait_ge(sg("gated up"), c + ci + 1)
                                act.activation(at_hi[:, (c + ci) % ATS, :], a32[:, ci, :], ACT.Copy).then_inc(sg("AT hi"), 1)
                        for n2 in range(2):
                            split_upto(last_s(("w2", g, n2)) + AHEAD)
                    act.wait_ge(sg("y sum"), NB * 2 * len(groups))
                    postnorm("pf0", [y0[:, b, :] for b in range(NB)], lambda b, src: sgf[:, :, :].rearrange("p a n -> p (a n)"))

            def scatters(turn):
                act.wait_ge(sg("slot gates"), turn + 1)
                act.activation(st2[:, 96:104], ps[:, 0, 0:NE], ACT.Copy).then_inc(sg("slot gate"), 1)
                for e in range(NE):
                    act.wait_ge(sg("scat ps"), NE * turn + e + 1)
                    act.activation(scat[:, e, :], ps[:, 2 + e % 2, 0:NLAT * P], ACT.Copy).then_inc(sg("scat"), 1)

            def experts(turn):
                base = turn * NE * UE
                with act.Fori(0, NE) as e:
                    done = [0]

                    def split_to(i1):
                        for i in range(done[0], min(i1, UE - 1) + 1):
                            k, s = K0 + base + i, NS0 + base + i
                            act.wait_ge(raw_in[k % RAW], e * (16 * UE // RAW) + raw_count(k))
                            act.wait_ge(unit_used, e * UE + (s - SPL + 1))
                            act.activation(w_hi[:, s % SPL, :], raw_at(k), ACT.Copy).then_inc(hi_done, 1)
                        done[0] = max(done[0], i1 + 1)

                    split_to(AHEAD)
                    for k in range(KD):
                        act.wait_ge(sg("gathered"), e * 2 + (2 * NE * turn + 1 + k // 4))
                        ins = act.activation(he32[:, k, :], ps[:, 2 + k // 4, P * (k % 4):P * (k % 4) + P], ACT.Identity,
                                             bias=mod_b[:, 1, k, 0:1], scale=mod_a[:, 1, k, 0:1])
                    ins.then_inc(sg("he32"), 1)
                    for s in range(STEPS):
                        split_to(end_w1(s) + AHEAD)
                        act.wait_ge(unit_used, e * UE + (NS0 + base + end_w1(s) + 1))
                        if s >= 2:
                            act.wait_ge(sg("ae32"), e * STEPS + (STEPS * NE * turn + s - 1))
                        act.activation(sge[:, s % 2, :], ps[:, 2 * (s % 2), :], ACT.Silu).then_inc(sg("silu e"), 1)
                        if s:
                            act.wait_ge(sg("ae ps"), e * STEPS + (STEPS * NE * turn + s))
                            act.activation(ae_hi[:, (s - 1) % 2, :], ps[:, 4 + (s - 1) % 2, :], ACT.Copy).then_inc(sg("ae hi"), 1)
                        split_to(end_w3(s) + AHEAD)
                        if s:
                            split_to(end_w2(s - 1) + AHEAD)
                    split_to(UE - 1)
                    act.wait_ge(sg("ae ps"), e * STEPS + (STEPS * NE * turn + STEPS))
                    act.activation(ae_hi[:, (STEPS - 1) % 2, :], ps[:, 4 + (STEPS - 1) % 2, :], ACT.Copy).then_inc(sg("ae hi"), 1)
                    act.wait_ge(unit_used, e * UE + (NS0 + base + UE))
                    act.activation(yg[:, e, :].rearrange("p (a n) -> p a n", a=2), ps[:, 6:8, :], ACT.Identity,
                                   scale=st2[:, bass.ds(e + 96, 1)]).then_inc(sg("yg"), 1)

            def combine(turn):
                act.wait_ge(sg("yg"), NE * (turn + 1))
                for e in range(NE):
                    if e >= 2:
                        act.wait_ge(sg("combined"), NE * turn + e - 1)
                    act.activation(yh[:, e % 2, :], yg[:, e, :], ACT.Copy).then_inc(sg("y hi"), 1)
                act.wait_ge(sg("yout"), NLAT * (turn + 1))

            act.wait_ge(sg("gap"), NLAT)
            act.activation(rs[:, 82:84], rs[:, 80:82], ACT.Exp).then_inc(sg("gap exp"), 1)
            scatters(0)
            experts(0)
            combine(0)
            act.wait_ge(sg("flag set"), 1)
            busiest = act.value_load(flag[0:1, 0:1], min_val=0, max_val=NLAT * P)
            with act.If(busiest > P):
                scatters(1)
                experts(1)
                combine(1)
            postnorm("pf1", [yout[:, b, :] for b in range(NLAT)], lambda b, src: junk[:, :])

        @block.vector
        def _(dve):
            cur = [0]
            chain = [0]
            stage_end = [layer_end]

            def link(ins):
                chain[0] += 1
                ins.then_inc(dve_ch, 1)
                dve.wait_ge(dve_ch, chain[0])

            def split_lo(s_, k, hi_count):
                dve.wait_ge(hi_done, hi_count)
                dve.tensor_tensor(w_lo[:, s_ % SPL, :], raw_at(k), w_hi[:, s_ % SPL, :].bitcast(F32), ALU.subtract)\
                    .then_inc(lo_done, 1)

            def split_upto(s):
                s = min(s, stage_end[0])
                while cur[0] <= s:
                    u = split_units[cur[0]]
                    split_lo(u.s, u.k, u.s + 1)
                    cur[0] += 1

            def last_s(key):
                return at[key][-1].s

            def root(src, ms, rt, out_, key, n):
                dve.tensor_scalar(ms, src, 1.0 / n, EPS, ALU.mult, ALU.add).then_inc(sg("ms " + key), 1)
                dve.wait_ge(sg("rt " + key), 1)
                link(dve.reciprocal(out_, rt))

            link(dve.memset(cstat[:, :, :], 0.0))
            dve.engine_nop().then_inc(sg("cstat"), 1)
            dve.wait_ge(sg("params in"), 16 * 14)
            for l in range(2):
                link(dve.tensor_tensor(lam_t[:, l, :, :], lam_bc[:, l, 0:4:2, :], lam_bc[:, l, 1:4:2, :], ALU.mult))
                link(dve.tensor_reduce(lam_s[:, l, 0:2], lam_t[:, l, :, :], AX.X, ALU.add))
            dve.engine_nop().then_inc(sg("lam dots"), 1)
            dve.wait_ge(sg("lam exp"), 1)
            for l in range(2):
                lam_init = 0.8 - 0.6 * math.exp(-0.3 * l)
                link(dve.tensor_tensor(lam_s[:, l, 4:5], lam_s[:, l, 3:4], lam_s[:, l, 2:3], ALU.subtract))
                link(dve.tensor_scalar(lam_s[:, l, 5:6], lam_s[:, l, 4:5], -lam_init, None, ALU.add))
            dve.wait_ge(sg("small T"), 3)
            for l in range(2):
                dve.tensor_copy(pcol[:, l, :], ps[:, 1 + l, 0:68]).then_inc(sg("pcol"), 1)
            dve.wait_ge(sg("pcol"), 2)

            def ada(l):
                ns = len(streams(l))

                def post(c):
                    part = c // 2
                    if part in (2, 5):
                        g = part // 3
                        dve.wait_ge(sg("ada post"), 12 * l + c + 1)
                        dve.wait_ge(s_bc, 32 * (2 * l + g + 1))
                        half = slice(512 * (c % 2), 512 * (c % 2) + 512)
                        for r in streams(l):
                            link(dve.tensor_tensor(gg[:, g, r, half], ps[:, 3 + r, :], ab_bc[:, half], ALU.add))
                            dve.tensor_tensor(gg[:, g, r, half], gg[:, g, r, half], pg_bc[:, half], ALU.mult)\
                                .then_inc(sg("gg done"), 1)
                    elif c % 6 == 3:
                        w = c // 6
                        dve.wait_ge(sg("ada post"), 12 * l + c + 1)
                        shift = ps[:, 2, 0:2 * KD].rearrange("p (k r) -> p k r", r=2)
                        scale = ps[:, 2, 2 * KD:4 * KD].rearrange("p (k r) -> p k r", r=2)

                        def col(i):
                            return pcol[:, l, i:i + KD].unsqueeze(2).to_broadcast([P, KD, 2])
                        dve.tensor_tensor(mod_b[:, w, :, :], shift, col(24 * w), ALU.add).then_inc(sg("mod done"), 1)
                        link(dve.tensor_tensor(mod_a[:, w, :, :], scale, col(24 * w + KD), ALU.add))
                        dve.scalar_tensor_tensor(out=mod_a[:, w, :, :], in0=mod_a[:, w, :, :], scalar=1.0,
                                                 in1=col(48 + KD * w), op0=ALU.add, op1=ALU.mult).then_inc(sg("mod done"), 1)

                for c in range(12):
                    dve.wait_ge(ada_used, 4 * (12 * l + c + 1))
                    if 12 * l + c >= 2:
                        dve.wait_ge(sg("ada post"), 12 * l + c - 1)
                    dve.tensor_copy(arow[:, c % 2, :], ps[:, c % 2, :]).then_inc(sg("arow"), 1)
                    if c:
                        post(c - 1)
                post(11)

            def prenorm(key, nb):
                dve.wait_ge(sg("ss " + key), nb)
                root(st[:, 0:nb], st[:, 4:4 + nb], st[:, 8:8 + nb], st[:, 12:12 + nb], key, D)
                for b in range(nb):
                    dve.tensor_scalar(xn[:, b, :], xs[:, b, :], st[:, 12 + b:13 + b], None, ALU.mult).then_inc(sg("xn " + key), 1)

            def split_h(key):
                for k in range(KD):
                    dve.wait_ge(sg("hT32 " + key), k + 1)
                    link(dve.tensor_copy(hT_hi[:, k, :], hT32[:, k, :]))
                    dve.tensor_tensor(hT_lo[:, k, :], hT32[:, k, :], hT_hi[:, k, :].bitcast(F32), ALU.subtract)\
                        .then_inc(sg("hT " + key), 1)

            def postnorm(key, srcs, which, done):
                dve.wait_ge(sg("ss " + key), len(srcs))
                n = len(srcs)
                root(st[:, 16:16 + n], st[:, 20:20 + n], st[:, 24:24 + n], st[:, 28:28 + n], key, D)
                for b, src in enumerate(srcs):
                    if b:
                        dve.wait_ge(sg(done), b)
                    r = b // NLAT
                    t, g, o = ptmp[:, :], gg[:, which, r, :], xs[:, b, :]
                    if len(src.shape) == 3:
                        t, g = (v.rearrange("p (a n) -> p a n", a=2) for v in (t, g))
                    link(dve.scalar_tensor_tensor(out=t, in0=src, scalar=st[:, 28 + b:29 + b], in1=g, op0=ALU.mult, op1=ALU.mult))
                    dve.tensor_tensor(o, o, ptmp[:, :], ALU.add).then_inc(sg(done), 1)

            def rope(l):
                for b in range(NLAT):
                    cos = cst[:, C_COS + HD * b:C_COS + HD * b + HD].unsqueeze(1).to_broadcast([P, 16, HD])
                    sin = cst[:, C_SIN + HD * b:C_SIN + HD * b + HD].rearrange("p (r f i) -> p r f i", r=2, f=2)
                    qkv = proj[:, b, 0:D].rearrange("p (h r f i) -> p h r f i", r=2, f=2, i=16)
                    tv = rtmp[:, :].rearrange("p (h r f i) -> p h r f i", r=2, f=2, i=16)
                    dve.tensor_tensor(rk[:, b, :].rearrange("p (h d) -> p h d", d=HD),
                                      proj[:, b, 0:D].rearrange("p (h d) -> p h d", d=HD), cos, ALU.mult)
                    for f in range(2):
                        link(dve.tensor_tensor(tv[:, :, :, f, :], qkv[:, :, :, 1 - f, :],
                                               sin[:, :, f, :].unsqueeze(1).to_broadcast([P, 16, 2, 16]), ALU.mult))
                    dve.tensor_tensor(rk[:, b, :], rk[:, b, :], rtmp[:, :], ALU.add).then_inc(sg("rope%d" % l), 1)
                    dve.wait_ge(sg("rope%d" % l), b + 1)

            def spatial(l):
                nb = len(out_blocks(l))
                for b in range(nb):
                    link(dve.bn_stats(st2[:, 104:110], proj[:, b, 4 * DA:5 * DA]))
                    link(dve.bn_aggr(st[:, 48 + 2 * b:50 + 2 * b], st2[:, 104:110]))
                dve.tensor_scalar(st[:, 40:40 + nb], st[:, 49:49 + 2 * nb:2], EPS, None, ALU.add).then_inc(sg("ln ms%d" % l), 1)
                dve.wait_ge(sg("ln rt%d" % l), 1)
                link(dve.reciprocal(st[:, 36:36 + nb], st[:, 44:44 + nb]))
                for b in range(nb):
                    v = proj[:, b, 4 * DA:5 * DA]
                    link(dve.tensor_scalar(v, v, st[:, 48 + 2 * b:49 + 2 * b], st[:, 36 + b:37 + b], ALU.subtract, ALU.mult))
                    link(dve.tensor_tensor(v, v, lng_bc[:, l, :], ALU.mult))
                    dve.tensor_tensor(v, v, lnb_bc[:, l, :], ALU.add).then_inc(sg("vn%d" % l), 1)
                for b in range(nb):
                    dve.wait_ge(sg("mixed%d" % l), b + 1)
                    for g in range(4):
                        u = proj[:, b, 3 * DA + P * g:3 * DA + P * g + P]
                        ins = dve.scalar_tensor_tensor(out=u, in0=ps[:, 4 + b, P * g:P * g + P], scalar=pcol[:, l, 64 + g:65 + g],
                                                       in1=u, op0=ALU.add, op1=ALU.mult)
                    ins.then_inc(sg("gated%d" % l), 1)

            def attend(l):
                its = items[l]
                n = len(its)
                for t in range(n + 2):
                    if t < n:
                        p = t % 2
                        nk = 512 if its[t][0] < NLAT else 256
                        dve.wait_ge(sg("scores%d" % l), t + 1)
                        link(dve.tensor_reduce(att[:, p, 0:2], ps[:, 2 * p:2 * p + 2, 0:nk], AX.X, ALU.max))
                        dve.tensor_scalar(att[:, p, 2:4], att[:, p, 0:2], -SCALE, None, ALU.mult).then_inc(sg("rowmax%d" % l), 1)
                    if 1 <= t <= n:
                        i = t - 1
                        p = i % 2
                        nk = 512 if its[i][0] < NLAT else 256
                        dve.wait_ge(sg("exp%d" % l), 2 * (i + 1))
                        link(dve.reciprocal(att[:, p, 6:8], att[:, p, 4:6]))
                        link(dve.tensor_scalar(att[:, p, 7:8], att[:, p, 7:8], lam_s[:, l, 5:6], None, ALU.mult))
                        link(dve.tensor_scalar(pr[:, p, 1, 0:nk], pr[:, p, 1, 0:nk], att[:, p, 7:8], None, ALU.mult))
                        dve.scalar_tensor_tensor(out=pr[:, p, 0, 0:nk], in0=pr[:, p, 0, 0:nk], scalar=att[:, p, 6:7],
                                                 in1=pr[:, p, 1, 0:nk], op0=ALU.mult, op1=ALU.add).then_inc(sg("weights%d" % l), 1)
                    if t >= 2:
                        i = t - 2
                        b, h = its[i]
                        dve.wait_ge(sg("pv%d" % l), i + 1)
                        dve.tensor_copy(proj[:, b, P * h:P * h + P], ps[:, 6 + i % 2, 0:P]).then_inc(sg("o%d" % l), 1)
                dve.wait_ge(sg("o sq%d" % l), n)
                dve.wait_ge(sg("o%d" % l), n)
                dve.tensor_scalar(st2[:, 16:16 + n], st2[:, 0:n], 1.0 / P, EPS, ALU.mult, ALU.add).then_inc(sg("o ms%d" % l), 1)
                dve.wait_ge(sg("o rt%d" % l), 1)
                link(dve.reciprocal(st2[:, 48:48 + n], st2[:, 32:32 + n]))
                keep = 1.0 - (0.8 - 0.6 * math.exp(-0.3 * l))
                link(dve.tensor_scalar(st2[:, 48:48 + n], st2[:, 48:48 + n], keep, None, ALU.mult))
                for i, (b, h) in enumerate(its):
                    o = proj[:, b, P * h:P * h + P]
                    dve.scalar_tensor_tensor(out=o, in0=o, scalar=st2[:, 48 + i:49 + i], in1=sub_bc[:, l, :],
                                             op0=ALU.mult, op1=ALU.mult).then_inc(sg("cat%d" % l), 1)

            def ffn():
                for g, (c0, gc) in enumerate(groups):
                    for c in range(c0, c0 + gc, 2):
                        split_upto(last_s(("w1", c)) + AHEAD)
                        split_upto(last_s(("w3", c)) + AHEAD)
                        dve.wait_ge(unit_used, last_s(("w3", c)) + 1)
                        for ci in range(2):
                            dve.wait_ge(sg("silu"), c + ci + 1)
                            if c:
                                dve.wait_ge(sg("AT"), c + ci - 1)
                            dve.tensor_tensor(a32[:, ci, :], sgf[:, ci, :], ps[:, 2 + ci, :], ALU.mult).then_inc(sg("gated up"), 1)
                        for ci in range(2):
                            a = (c + ci) % ATS
                            dve.wait_ge(sg("AT hi"), c + ci + 1)
                            dve.tensor_tensor(at_lo[:, a, :], a32[:, ci, :], at_hi[:, a, :].bitcast(F32), ALU.subtract)\
                                .then_inc(sg("AT"), 1)
                    for n2 in range(2):
                        split_upto(last_s(("w2", g, n2)) + AHEAD)
                        for b in range(NB):
                            if b < NB - 1:
                                dve.wait_ge(sg("y part"), (NB - 1) * (2 * g + n2) + b + 1)
                            else:
                                dve.wait_ge(unit_used, last_s(("w2", g, n2)) + 1)
                            y = y0[:, b, 512 * n2:512 * n2 + 512]
                            if g == 0:
                                dve.tensor_copy(y, ps[:, 4 + b, :]).then_inc(sg("y sum"), 1)
                            else:
                                dve.wait_ge(sg("y sum"), NB * (2 * (g - 1) + n2) + b + 1)
                                dve.tensor_tensor(y, y, ps[:, 4 + b, :], ALU.add).then_inc(sg("y sum"), 1)

            def route():
                lg, mx, idf = rs[:, 0:16], rs[:, 16:32], rs[:, 32:48]
                oh = rs[:, 48:80].rearrange("p (j t e) -> p j t e", j=2, t=NLAT)
                dve.wait_ge(sg("logits"), 1)
                link(dve.tensor_copy(lg, ps[:, 0, 0:16]))
                for tb in range(NLAT):
                    o = slice(8 * tb, 8 * tb + 8)
                    link(dve.max(mx[:, o], lg[:, o]))
                    link(dve.max_index(idx[:, tb, :], mx[:, o], lg[:, o]))
                link(dve.tensor_copy(idf, idx[:, :, :].rearrange("p t e -> p (t e)")))
                for tb in range(NLAT):
                    for j in range(2):
                        link(dve.tensor_scalar(oh[:, j, tb, :], iota[:, 0:8], idf[:, 8 * tb + j:8 * tb + j + 1], None, ALU.is_equal))
                    dve.tensor_tensor(rs[:, 80 + tb:81 + tb], mx[:, 8 * tb + 1:8 * tb + 2], mx[:, 8 * tb:8 * tb + 1], ALU.subtract)\
                        .then_inc(sg("gap"), 1)
                link(dve.tensor_tensor(st2[:, 64:80], rs[:, 48:64], rs[:, 64:80], ALU.add))
                dve.engine_nop().then_inc(sg("mask"), 1)
                dve.wait_ge(sg("gap exp"), 1)
                link(dve.tensor_scalar(rs[:, 84:86], rs[:, 82:84], 1.0, None, ALU.add))
                link(dve.reciprocal(rs[:, 86:88], rs[:, 84:86]))
                link(dve.tensor_tensor(rs[:, 88:90], rs[:, 86:88], rs[:, 82:84], ALU.mult))
                for tb in range(NLAT):
                    gt = st2[:, 80 + 8 * tb:88 + 8 * tb]
                    link(dve.tensor_scalar(gt, oh[:, 0, tb, :], rs[:, 86 + tb:87 + tb], None, ALU.mult))
                    link(dve.scalar_tensor_tensor(out=gt, in0=oh[:, 1, tb, :], scalar=rs[:, 88 + tb:89 + tb], in1=gt,
                                                  op0=ALU.mult, op1=ALU.add))
                dve.wait_ge(sg("counts"), 1)
                link(dve.tensor_tensor(rs[:, 96:112], ps[:, 1, 0:16], st2[:, 64:80], ALU.mult))
                link(dve.tensor_scalar(rs[:, 96:112], rs[:, 96:112], -1.0, None, ALU.add))
                link(dve.tensor_scalar(rs[:, 112:128], rs[:, 96:112], -float(P), None, ALU.add))
                link(dve.tensor_reduce(rs[:, 90:91], ps[:, 1, 16:24], AX.X, ALU.max))
                dve.tensor_copy(flag[:, :], rs[:, 90:91]).then_inc(sg("flag set"), 1)
                dve.wait_ge(sg("flag set"), 1)

            def permute(turn):
                for e in range(NE):
                    for tb in range(NLAT):
                        place_ = 96 + 16 * turn + 8 * tb + e
                        ins = dve.tensor_scalar(perm[:, e, tb, :], iota, rs[:, place_:place_ + 1], None, ALU.is_equal)
                    ins.then_inc(sg("perm"), 1)

            def experts(turn):
                base = turn * NE * UE
                with dve.Fori(0, NE) as e:
                    done = [0]

                    def split_to(i1):
                        for i in range(done[0], min(i1, UE - 1) + 1):
                            split_lo(NS0 + base + i, K0 + base + i, e * UE + (NS0 + base + i + 1))
                        done[0] = max(done[0], i1 + 1)

                    split_to(AHEAD)
                    dve.wait_ge(sg("he32"), e + (NE * turn + 1))
                    dve.tensor_copy(he_hi[:, :, :], he32[:, :, :]).then_inc(sg("he hi"), 1)
                    dve.wait_ge(sg("he hi"), e + (NE * turn + 1))
                    dve.tensor_tensor(he_lo[:, :, :], he32[:, :, :], he_hi[:, :, :].bitcast(F32), ALU.subtract).then_inc(sg("he"), 1)

                    def lo_a(s):
                        dve.wait_ge(sg("ae hi"), e * STEPS + (STEPS * NE * turn + s + 1))
                        dve.tensor_tensor(ae_lo[:, s % 2, :], ps[:, 4 + s % 2, :], ae_hi[:, s % 2, :].bitcast(F32), ALU.subtract)\
                            .then_inc(sg("ae"), 1)

                    for s in range(STEPS):
                        split_to(end_w1(s) + AHEAD)
                        if s:
                            lo_a(s - 1)
                        split_to(end_w3(s) + AHEAD)
                        dve.wait_ge(sg("silu e"), e * STEPS + (STEPS * NE * turn + s + 1))
                        dve.wait_ge(unit_used, e * UE + (NS0 + base + end_w3(s) + 1))
                        dve.tensor_tensor(ae32[:, s % 2, :], sge[:, s % 2, :], ps[:, 2 * (s % 2) + 1, :], ALU.mult)\
                            .then_inc(sg("ae32"), 1)
                        if s:
                            split_to(end_w2(s - 1) + AHEAD)
                    split_to(UE - 1)
                    lo_a(STEPS - 1)

            def combine(turn):
                for e in range(NE):
                    dve.wait_ge(sg("y hi"), NE * turn + e + 1)
                    dve.tensor_tensor(yl[:, e % 2, :], yg[:, e, :], yh[:, e % 2, :].bitcast(F32), ALU.subtract)\
                        .then_inc(sg("y split"), 1)
                dve.wait_ge(sg("combined"), NE * (turn + 1))
                for tb in range(NLAT):
                    y = yout[:, tb, :].rearrange("p (a n) -> p a n", a=2)
                    v = ps[:, 2 * tb:2 * tb + 2, :]
                    if turn == 0:
                        dve.tensor_copy(y, v).then_inc(sg("yout"), 1)
                    else:
                        dve.tensor_tensor(y, y, v, ALU.add).then_inc(sg("yout"), 1)
                dve.wait_ge(sg("yout"), NLAT * (turn + 1))

            for l in range(2):
                nb = len(out_blocks(l))
                if l == 1:
                    stage_end[0] = NS0 - 1
                ada(l)
                prenorm("mix%d" % l, NB)
                split_h("mix%d" % l)
                for j in range(5):
                    split_upto(last_s(("in", l, j)) + AHEAD)
                dve.wait_ge(sg("proj%d" % l), proj_n[l][4])
                rope(l)
                spatial(l)
                attend(l)
                split_upto(at["out", l, 0][0].s + AHEAD)
                for k in range(KD):
                    dve.wait_ge(sg("catT hi"), KD * l + k + 1)
                    dve.tensor_tensor(hT_lo[:, k, 0:P * nb], ps[:, k % 2, 0:P * nb], hT_hi[:, k, 0:P * nb].bitcast(F32), ALU.subtract)\
                        .then_inc(sg("catT"), 1)
                split_upto(last_s(("out", l, 1)))
                postnorm("pm%d" % l, [ps[:, 2 * b:2 * b + 2, :] for b in out_blocks(l)], 0, "x mix%d" % l)
                for b in out_blocks(l):
                    dve.wait_ge(sg("x mix%d" % l), b + 1)
                prenorm("ffn%d" % l, nb)
                if l == 0:
                    split_h("ffn0")
                    split_upto(at["w1", 0][0].s + AHEAD)
                    ffn()
                    postnorm("pf0", [y0[:, b, :] for b in range(NB)], 1, "x ffn")
            dve.wait_ge(sg("xn ffn1"), NLAT)
            link(dve.tensor_copy(xg_hi[:, :, :], xn[:, 0:NLAT, :]))
            link(dve.tensor_tensor(xg_lo[:, :, :], xn[:, 0:NLAT, :], xg_hi[:, :, :].bitcast(F32), ALU.subtract))
            route()
            permute(0)
            experts(0)
            combine(0)
            busiest = dve.value_load(flag[0:1, 0:1], min_val=0, max_val=NLAT * P)
            with dve.If(busiest > P):
                permute(1)
                experts(1)
                combine(1)
            postnorm("pf1", [yout[:, b, :] for b in range(NLAT)], 1, "final x")

    return nc


_INS = ['x', 'c', 'ctx', 'c_ctx', 'ada_w', 'ada_b', 'pre_mix_g', 'post_mix_g', 'pre_ffn_g', 'post_ffn_g', 'w_in',
        'w_out', 'lam_q1', 'lam_k1', 'lam_q2', 'lam_k2', 'subln_g', 'sg_ln_g', 'sg_ln_b', 'sg_w', 'sg_b', 'ffn_w1',
        'ffn_w3', 'ffn_w2', 'router_w', 'moe_w1', 'moe_w3', 'moe_w2']


def kernel(**inputs):
    import numpy as _np
    import concourse.bacc as _bacc
    from concourse import mybir as _mybir
    from concourse.bass_utils import run_bass_kernel_spmd as _run

    nc = _bacc.Bacc("TRN2", target_bir_lowering=False, num_devices=1)
    arrays, args = {}, []
    for name in _INS:
        arrays[f"in_{name}"] = _np.ascontiguousarray(inputs[name])
    arrays["in_const"] = constants()
    for name, a in arrays.items():
        args.append(nc.dram_tensor(name, a.shape, _mybir.dt.from_np(a.dtype), kind="ExternalInput").ap())
    args.append(nc.dram_tensor("out_0", (1, NLAT * P, D), _mybir.dt.float32, kind="ExternalOutput").ap())
    program(nc, *args)
    r = _run(nc, [arrays], core_ids=[0])
    return r.results[0]["out_0"]
```

```python
from contextlib import ExitStack
import math

import numpy as np
import concourse.bass as bass
from concourse import mybir

F32 = mybir.dt.float32
F32R = mybir.dt.float32r
I32 = mybir.dt.int32
U32 = mybir.dt.uint32
ALU = mybir.AluOpType
ACT = mybir.ActivationFunctionType
AX = mybir.AxisListType

P = 128
D = 1024
KD = D // P
NB = 4
NLAT = 2
HEADS = 4
HD = 64
DA = 512
SG = 512
IN = 2560
FF = 2816
NE = 8
DE = 3584
EPS = 1e-6
SCALE = HD ** -0.5

UW = 1024
RAW = 7
ADA_SEQ = ([(0, p, h) for p in range(6) for h in range(2)] + [(1, p, h) for p in (0, 1, 3, 4) for h in range(2)]
           + [(1, p, h) for p in (2, 5) for h in range(2)])
IN_ORDER = (4, 3, 0, 1, 2)
SPL = 4
AHEAD = SPL - 1
ATS = 6
STEPS = DE // 512
UE = 12 * STEPS

C_ID, C_TRIU, C_ONES, C_IOTA, C_SELB, C_SELC, C_COS, C_SIN = 0, 128, 256, 384, 512, 768, 770, 898
C_END = 1026


def constants():
    c = np.zeros((P, C_END), np.float32)
    c[:, C_ID:C_ID + P] = np.eye(P)
    c[:, C_TRIU:C_TRIU + P] = np.triu(np.ones((P, P)))
    c[:, C_ONES:C_ONES + P] = 1
    c[:, C_IOTA:C_IOTA + P] = np.arange(P)
    for q in range(4):
        for r in range(2):
            c[32 * q + r, C_SELB + P * r:C_SELB + P * (r + 1)] = 1
            c[32 * q + r, C_SELC + r] = 1
    half = HD // 2
    inv = (np.float32(10000.0) ** (-np.arange(0, half, 2, dtype=np.float32) / np.float32(half))).astype(np.float32)
    tok = np.arange(NLAT * P)
    row, col = (tok // HD).astype(np.float32), (tok % HD).astype(np.float32)
    ar, ac = row[:, None] * inv, col[:, None] * inv
    ang = np.concatenate([ar, ar, ac, ac], -1)
    sgn = np.concatenate([-np.ones(16), np.ones(16)] * 2).astype(np.float32)
    cos, sin = np.cos(ang).astype(np.float32), np.sin(ang).astype(np.float32) * sgn
    c[:, C_COS:C_COS + 128] = cos.reshape(NLAT, P, HD).transpose(1, 0, 2).reshape(P, 128)
    c[:, C_SIN:C_SIN + 128] = sin.reshape(NLAT, P, HD).transpose(1, 0, 2).reshape(P, 128)
    return c


class Unit:

    def __init__(self, k, s, a, src, split, shape):
        self.k, self.s, self.a, self.src, self.split, self.shape = k, s, a, src, split, shape


def plan_units(ada_w, w_in, w_out, w1, w3, w2):
    units, at = [], {}
    n = dict(s=0, a=0)

    def add(key, src, split, shape):
        u = Unit(len(units), n["s"] if split else None, None if split else n["a"], src, split, shape)
        n["s" if split else "a"] += 1
        units.append(u)
        at.setdefault(key, []).append(u)

    def tall(w, k0, nk, c0, nc_):
        return w[k0 * P:(k0 + nk) * P, c0:c0 + nc_].rearrange("(k p) n -> p k n", p=P)

    def ada(n0, n1):
        for n in range(n0, n1):
            l, part, half = ADA_SEQ[n]
            for u in range(4):
                add(("ada", n), tall(ada_w[l], 2 * u, 2, D * part + 512 * half, 512), False, (2, 512))

    ada(0, 4)
    for l in range(2):
        for j in IN_ORDER:
            for u in range(4):
                add(("in", l, j), tall(w_in[l], 2 * u, 2, 512 * j, 512), True, (2, 512))
        ada(*((4, 20) if l == 0 else (20, 24)))
        for n2 in range(2):
            for u in range(4):
                add(("out", l, n2), tall(w_out[l], 2 * u, 2, 512 * n2, 512), True, (2, 512))
        if l == 0:
            for g, c0 in enumerate(range(0, 22, 4)):
                gc = min(4, 22 - c0)
                for c in range(c0, c0 + gc, 2):
                    for key, w in (("w1", w1), ("w3", w3)):
                        for h in range(2):
                            add((key, c), tall(w[0], 4 * h, 4, P * c, 2 * P), True, (4, 256))
                for n2 in range(2):
                    for c in range(c0, c0 + gc, 2):
                        add(("w2", g, n2), tall(w2[0], c, 2, 512 * n2, 512), True, (2, 512))
    return units, at, n["s"]


def program(nc, x, c, ctx, c_ctx, ada_w, ada_b, pre_mix_g, post_mix_g, pre_ffn_g, post_ffn_g, w_in, w_out,
            lam_q1, lam_k1, lam_q2, lam_k2, subln_g, sg_ln_g, sg_ln_b, sg_w, sg_b, ffn_w1, ffn_w3, ffn_w2,
            router_w, moe_w1, moe_w3, moe_w2, const, out):
    units, at, NS0 = plan_units(ada_w, w_in, w_out, ffn_w1, ffn_w3, ffn_w2)
    K0 = len(units)
    split_units = [u for u in units if u.split]

    with ExitStack() as stack:
        def sem(name):
            return stack.enter_context(nc.semaphore(name))

        end = [16512]

        def place(name, shape, dt, offset=None):
            size = 4 * int(np.prod(shape[1:]))
            if offset is None:
                offset = end[0]
                end[0] += -(-size // 32) * 32
            return nc.alloc_sbuf_tensor_at(name, shape, dt, offset=offset)

        raw = place("raw", [P, RAW, UW], F32)
        w_hi = place("w_hi", [P, SPL, UW], F32R)
        w_lo = place("w_lo", [P, SPL, UW], F32R)
        xs = place("xs", [P, NB, D], F32)
        H = end[0]
        hT_hi = place("hT_hi", [P, KD, 512], F32R)
        hT_lo = place("hT_lo", [P, KD, 512], F32R)
        cst = place("cst", [P, C_END], F32)
        pcol = place("pcol", [P, 2, 68], F32)
        cstat = place("cstat", [P, KD, 32], F32)
        mod_a = place("mod_a", [P, 2, 2, KD, 2], F32)
        mod_b = place("mod_b", [P, 2, 2, KD, 2], F32)
        sub_bc = place("sub_bc", [P, 2, P], F32)
        lng_bc = place("lng_bc", [P, 2, SG], F32)
        lnb_bc = place("lnb_bc", [P, 2, SG], F32)
        lam_s = place("lam_s", [P, 2, 8], F32)
        rs = place("rs", [P, 128], F32)
        idx = place("idx", [P, NLAT, 8], U32)
        st = place("st", [P, 64], F32)
        st2 = place("st2", [P, 128], F32)
        att = place("att", [P, 2, 8], F32)
        flag = place("flag", [P, 1], I32)
        ab_bc = place("ab_bc", [P, 512], F32)
        pg_bc = place("pg_bc", [P, 512], F32)
        arow = place("arow", [P, 512], F32)
        wsT = place("wsT", [P, SG], F32)
        gg = place("gg", [P, 4, D], F32)
        G1 = end[0] - 4 * 4 * D
        Z = end[0]
        proj = place("proj", [P, NB, IN], F32, Z)
        xn = place("xn", [P, NB, D], F32, Z)
        hT32 = place("hT32", [P, KD, 512], F32, Z + 16384)
        qT = place("qT", [P, HEADS, 512], F32, H + 16384)
        kT = place("kT", [P, HEADS, 512], F32, H + 24576)
        pr = place("pr", [P, 2, 2, 512], F32, Z + 40960)
        wT = place("wT", [P, 2, 512], F32, Z + 49152)
        rtmp = place("rtmp", [P, D], F32, Z + 40960)
        ws_raw = place("ws_raw", [P, SG], F32, Z + 53248)
        osq = place("osq", [P, P], F32, Z + 55296)
        rows = place("rows", [68, 2, P], F32, Z + 32768)
        crow = place("crow", [16, P], F32, Z + 33792)
        lam_bc = place("lam_bc", [P, 2, 4, HD], F32, Z + 34304)
        lam_t = place("lam_t", [P, 2, 2, HD], F32, Z + 36352)
        y0 = place("y0", [P, NB, D], F32, Z)
        at_hi = place("at_hi", [P, ATS, 512], F32R, Z + 16384)
        at_lo = place("at_lo", [P, ATS, 512], F32R, Z + 28672)
        ptmp = place("ptmp", [P, D], F32, Z + 40960)
        sgf = place("sgf", [P, 2, 512], F32, Z + 45056)
        a32 = place("a32", [P, 2, 512], F32, Z + 49152)
        xg_hi = place("xg_hi", [P, NLAT, D], F32R, H)
        xg_lo = place("xg_lo", [P, NLAT, D], F32R, H + 8192)
        he_hi = place("he_hi", [P, KD, P], F32R, H + 16384)
        he_lo = place("he_lo", [P, KD, P], F32R, H + 20480)
        he32 = place("he32", [P, KD, P], F32, H + 24576)
        rw = place("rw", [P, KD, NE], F32, H + 28672)
        yg = place("yg", [P, NE, D], F32, Z)
        Z2 = Z + 32768
        perm = place("perm", [P, NE + 1, NLAT, P], F32R, Z2)
        scat = place("scat", [P, NE, NLAT * P], F32R, Z2 + 9216)
        ae_hi = place("ae_hi", [P, 2, 512], F32R, G1 + 8192)
        sge = place("sge", [P, 2, 512], F32, Z2 + 17408)
        ae32 = place("ae32", [P, 2, 512], F32, Z2 + 21504)
        ae_lo = place("ae_lo", [P, 2, 512], F32R, G1 + 12288)
        yh = place("yh", [P, 2, D], F32R, H + 16384)
        yl = place("yl", [P, 2, D], F32R, Z2 + 17408)
        ptm = place("ptm", [P, D], F32, Z)
        junk = place("junk", [P, D], F32, Z + 4096)
        assert Z2 + 25600 <= nc.sbuf_usable_end, (Z2 + 25600, nc.sbuf_usable_end)
        yout = xs[:, 2:4, :]
        ps = stack.enter_context(nc.psum_tensor("ps", [P, 8, 512], F32))

        ident = cst[:, C_ID:C_ID + P]
        ones = cst[:, C_ONES:C_ONES + P]
        triu = cst[:, C_TRIU:C_TRIU + P]
        iota = cst[:, C_IOTA:C_IOTA + P]

        raw_in = [sem(f"raw_in{i}") for i in range(RAW)]
        hi_done, lo_done = sem("hi_done"), sem("lo_done")
        unit_used, ada_used = sem("unit_used"), sem("ada_used")
        s_small, s_x, s_bc, s_out = sem("s_small"), sem("s_x"), sem("s_bc"), sem("s_out")
        dve_ch, act_ch = sem("dve_ch"), sem("act_ch")
        S = {}

        def sg(name):
            if name not in S:
                S[name] = sem(name.replace(" ", "_"))
            return S[name]

        def view(ring, u):
            return ring.rearrange("p (k n) -> p k n", k=u.shape[0])

        def raw_at(k):
            return raw[:, k % RAW, :]

        def raw_count(k):
            return 16 * (k // RAW + 1)

        block = stack.enter_context(nc.Block())

        def blocks(l):
            return range(NB)

        def in_blocks(l, j):
            return range(NB) if l == 0 or j in (1, 2) else range(NLAT)

        def out_blocks(l):
            return range(NB) if l == 0 else range(NLAT)

        items = {l: [(b, h) for b in out_blocks(l) for h in range(HEADS)] for l in range(2)}
        qk = {l: [(t, b) for b in range(NB) for t in ((0, 1) if l == 0 or b < NLAT else (1,))] for l in range(2)}
        proj_n = {l: [sum(len(in_blocks(l, i)) for i in IN_ORDER[:j + 1]) for j in range(5)] for l in range(2)}
        in_end = [at["in", l, IN_ORDER[-1]][-1].s for l in range(2)] + [NS0 - 1]
        groups = [(c0, min(4, 22 - c0)) for c0 in range(0, 22, 4)]

        def expert_units():
            seq = []
            for s in range(STEPS):
                seq += [(0, s, n) for n in range(4)] + [(1, s, n) for n in range(4)]
                if s:
                    seq += [(2, s - 1, 4 * (s - 1) + n) for n in range(4)]
            return seq + [(2, STEPS - 1, 4 * (STEPS - 1) + n) for n in range(4)]

        def end_w1(s):
            return 3 if s == 0 else 12 * s - 1

        def end_w3(s):
            return end_w1(s) + 4

        def end_w2(s):
            return end_w3(s + 1) + 4 if s + 1 < STEPS else UE - 1

        def ada_slot(l, t):
            if l == 0:
                return 8 + t if 0 <= t < 12 else None
            return 20 + t if 0 <= t < 4 else None

        ADA0 = 3
        ADA1 = 6
        gate_chunks = [c for c in range(24) if ADA_SEQ[c][1] in (2, 5)]

        def last_gate(c):
            return gate_chunks[gate_chunks.index(c) - 1]

        def gate_at(l, which, r):
            return 2 * which + r if l == 0 else which

        def streams(l):
            return (0, 1) if l == 0 else (0,)

        NSMALL = 16 * 11

        @block.sync
        def _(sp):
            small = [(cst[:, :], const), (crow[0:8, :], c.rearrange("a (k p) -> (a k) p", p=P)),
                     (crow[8:16, :], c_ctx.rearrange("(k p) -> k p", p=P))]
            for l in range(2):
                small += [(rows[0:48, l, :], ada_b[l].rearrange("(k p) -> k p", p=P)),
                          (rows[48:56, l, :], pre_mix_g[l].rearrange("(k p) -> k p", p=P)),
                          (rows[56:64, l, :], pre_ffn_g[l].rearrange("(k p) -> k p", p=P)),
                          (rows[64:68, l, :], sg_b[l])]
            for dst, src in small:
                sp.dma_start(dst, src).then_inc(s_small, 16)
            xv = x.rearrange("a (b p) d -> p (a b) d", p=P)
            cv = ctx.rearrange("a (b p) d -> p (a b) d", p=P)
            for b in range(NB):
                sp.dma_start(xs[:, b, :], xv[:, b, :] if b < NLAT else cv[:, b - NLAT, :]).then_inc(s_x, 16)
            for u in units:
                if u.k >= RAW:
                    o = units[u.k - RAW]
                    sp.wait_ge(*((lo_done, o.s + 1) if o.split else (ada_used, o.a + 1)))
                sp.dma_start(view(raw_at(u.k), u), u.src).then_inc(raw_in[u.k % RAW], 16)

            def experts(turn):
                base = turn * NE * UE
                with sp.Fori(0, NE) as e:
                    for i, (w, s, n) in enumerate(expert_units()):
                        sp.wait_ge(lo_done, e * UE + (NS0 + base + i - RAW + 1))
                        k = K0 + base + i
                        if w == 2:
                            src, dst = moe_w2[0][e][n * P:(n + 1) * P, :], raw_at(k)
                        else:
                            wt = moe_w1 if w == 0 else moe_w3
                            src = wt[0][e][2 * n * P:2 * (n + 1) * P, 512 * s:512 * s + 512].rearrange("(k p) n -> p k n", p=P)
                            dst = raw_at(k).rearrange("p (k n) -> p k n", k=2)
                        sp.dma_start(dst, src).then_inc(raw_in[k % RAW], 16)

            experts(0)
            sp.wait_ge(sg("flag set"), 1)
            busiest = sp.value_load(flag[0:1, 0:1], min_val=0, max_val=NLAT * P)
            with sp.If(busiest > P):
                experts(1)
            for b in range(NLAT):
                sp.wait_ge(sg("final x"), b + 1)
                sp.dma_start(out.rearrange("a (b p) d -> p (a b) d", p=P)[:, b, :], xs[:, b, :]).then_inc(s_out, 16)
            sp.wait_ge(s_out, 16 * NLAT)

        @block.gpsimd
        def _(pool):
            for l in range(2):
                for i, v in enumerate((lam_q1, lam_k1, lam_q2, lam_k2)):
                    pool.dma_start(lam_bc[:, l, i, :], v[l].partition_broadcast(P)).then_inc(sg("params in"), 16)
                pool.dma_start(sub_bc[:, l, :], subln_g[l].partition_broadcast(P)).then_inc(sg("params in"), 16)
                pool.dma_start(lng_bc[:, l, :], sg_ln_g[l].partition_broadcast(P)).then_inc(sg("params in"), 16)
                pool.dma_start(lnb_bc[:, l, :], sg_ln_b[l].partition_broadcast(P)).then_inc(sg("params in"), 16)
            for l in range(2):
                if l:
                    pool.wait_ge(sg("wsT ps"), l)
                pool.dma_start(ws_raw[:, :].rearrange("p (g q) -> p g q", g=4), sg_w[l].rearrange("g p q -> p g q")).then_inc(sg("ws in"), 16)
                for c in gate_chunks:
                    ll, part, half = ADA_SEQ[c]
                    if ll == l:
                        if c != gate_chunks[0]:
                            pool.wait_ge(sg("ada fin"), last_gate(c) + 1)
                        o = part * D + 512 * half
                        gain = (post_mix_g, post_ffn_g)[part // 3]
                        pool.dma_start(ab_bc[:, :], ada_b[ll][o:o + 512].partition_broadcast(P)).then_inc(s_bc, 16)
                        pool.dma_start(pg_bc[:, :], gain[ll][512 * half:512 * half + 512].partition_broadcast(P)).then_inc(s_bc, 16)
            pool.wait_ge(unit_used, NS0)
            pool.dma_start(rw[:, :, :], router_w[0].rearrange("(k p) e -> p k e", p=P)).then_inc(sg("rw in"), 16)

        @block.tensor
        def _(pe):
            def mm3(o, lh, ll, rh, rl, start, stop):
                pe.matmul(o, lh, rh, start=start, stop=False)
                pe.matmul(o, lh, rl, start=False, stop=False)
                return pe.matmul(o, ll, rh, start=False, stop=stop)

            def split_at(s):
                return w_hi[:, s % SPL, :], w_lo[:, s % SPL, :]

            pe.wait_ge(s_small, NSMALL)
            pe.transpose(ps[:, 0, 0:16], crow[:, :], ident[0:16, 0:16]).then_inc(sg("small T"), 1)
            for l in range(2):
                pe.transpose(ps[:, 1 + l, 0:68], rows[:, l, :], ident[0:68, 0:68]).then_inc(sg("small T"), 1)

            def ada_rows(c, bank):
                if c:
                    pe.wait_ge(sg("ada fin"), c)
                for u in at["ada", c]:
                    pe.wait_ge(raw_in[u.k % RAW], raw_count(u.k))
                    w = view(raw_at(u.k), u)
                    for kk in range(2):
                        k = 2 * (u.a % 4) + kk
                        q = k % 4
                        m = pe.matmul(ps[32 * q:32 * q + 32, bank, :], cstat[:, k, :], w[:, kk, :],
                                      start=(k < 4), stop=(k >= 4), tile_position=(0, 32 * q))
                    m.then_inc(ada_used, 1)

            def ada_turn(c, bank):
                pe.wait_ge(sg("arow"), c + 1)
                if ADA_SEQ[c][1] in (2, 5):
                    for r in streams(ADA_SEQ[c][0]):
                        m = pe.matmul(ps[:, bank + 1 - r, :], cst[:, C_SELB + P * r:C_SELB + P * r + P], arow[:, :],
                                      start=True, stop=True)
                else:
                    for j in range(4):
                        m = pe.matmul(ps[:, bank + 1, 2 * j:2 * j + 2], arow[:, P * j:P * j + P], cst[:, C_SELC:C_SELC + 2],
                                      start=True, stop=True)
                m.then_inc(sg("ada post"), 1)

            def turn_h(key, bank, nb):
                pe.wait_ge(sg("xn " + key), nb)
                for k in range(KD):
                    if k >= 2:
                        pe.wait_ge(sg("hT32 " + key), k - 1)
                    for b in range(nb):
                        m = pe.transpose(ps[:, bank + k % 2, P * b:P * b + P], xn[:, b, P * k:P * k + P], ident)
                    m.then_inc(sg("hT ps " + key), 1)

            def project_in(l):
                pe.wait_ge(sg("ada fin"), 4 if l == 0 else 20)
                for jn, j in enumerate(IN_ORDER):
                    if jn >= 2:
                        pe.wait_ge(sg("proj%d" % l), proj_n[l][jn - 2])
                    for i, u in enumerate(at["in", l, j]):
                        pe.wait_ge(lo_done, u.s + 1)
                        h, lo = (view(t, u) for t in split_at(u.s))
                        if jn == 0:
                            pe.wait_ge(sg("hT mix%d" % l), 2 * i + 2)
                        for kk in range(2):
                            k = 2 * i + kk
                            for b in in_blocks(l, j):
                                m = mm3(ps[:, 4 * (jn % 2) + b, :], hT_hi[:, k, P * b:P * b + P], hT_lo[:, k, P * b:P * b + P],
                                        h[:, kk, :], lo[:, kk, :], k == 0, k == KD - 1)
                        m.then_inc(unit_used, 1)

            def ada_some(c0, c1):
                for c in range(c0, c1):
                    ada_rows(c, ADA1)
                    ada_turn(c, ADA1)

            def turn_qk(l):
                pe.wait_ge(sg("rope%d" % l), 2 * NLAT)
                for i, (t, b) in enumerate(qk[l]):
                    if i >= 2:
                        pe.wait_ge(sg("qkT%d" % l), i - 1)
                    src = proj[:, b, :]
                    for h in range(HEADS):
                        m = pe.transpose(ps[:, i % 2, P * h:P * h + P], src[:, t * DA + P * h:t * DA + P * h + P], ident)
                    m.then_inc(sg("qk ps%d" % l), 1)

            def spatial(l):
                pe.wait_ge(sg("proj%d" % l), proj_n[l][4])
                pe.wait_ge(sg("ws in"), 16 * (l + 1))
                for g in range(4):
                    m = pe.transpose(ps[:, 2, P * g:P * g + P], ws_raw[:, P * g:P * g + P], ident)
                m.then_inc(sg("wsT ps"), 1)
                pe.wait_ge(sg("wsT"), l + 1)
                for b in out_blocks(l):
                    pe.wait_ge(sg("vn%d" % l), b + 1)
                    for g in range(4):
                        m = pe.matmul(ps[:, 4 + b, P * g:P * g + P], wsT[:, P * g:P * g + P],
                                      proj[:, b, 4 * DA + P * g:4 * DA + P * g + P], start=True, stop=True)
                    m.then_inc(sg("mixed%d" % l), 1)

            def attend(l):
                its = items[l]
                n = len(its)
                pe.wait_ge(sg("qkT%d" % l), len(qk[l]))
                pe.wait_ge(sg("gated%d" % l), len(out_blocks(l)))
                for t in range(n + 2):
                    if ada_slot(l, t - 1):
                        ada_turn(ada_slot(l, t - 1), ADA1)
                    if t < n:
                        b, h = its[t]
                        k0 = 0 if b < NLAT else 256
                        if t >= 2:
                            pe.wait_ge(sg("exp%d" % l), 2 * (t - 1))
                        for m_ in range(2):
                            m = pe.matmul(ps[:, 2 * (t % 2) + m_, 0:512 - k0], qT[HD * m_:HD * m_ + HD, h, P * b:P * b + P],
                                          kT[HD * m_:HD * m_ + HD, h, k0:512], start=True, stop=True)
                        m.then_inc(sg("scores%d" % l), 1)
                    if 1 <= t <= n:
                        i = t - 1
                        b, h = its[i]
                        nk = 4 if b < NLAT else 2
                        pe.wait_ge(sg("weights%d" % l), i + 1)
                        if i:
                            pe.wait_ge(sg("wT%d" % l), i)
                        for kb in range(nk):
                            m = pe.transpose(ps[:, 4, P * kb:P * kb + P], pr[:, i % 2, 0, P * kb:P * kb + P], ident)
                        m.then_inc(sg("wT ps%d" % l), 1)
                    if t >= 2:
                        i = t - 2
                        b, h = its[i]
                        kb0, nk = (0, 4) if b < NLAT else (2, 2)
                        pe.wait_ge(sg("wT%d" % l), i + 1)
                        if i:
                            pe.wait_ge(sg("o%d" % l), i)
                        for kb in range(nk):
                            m = pe.matmul(ps[:, 5, 0:P], wT[:, i % 2, P * kb:P * kb + P],
                                          proj[:, kb0 + kb, 2 * DA + P * h:2 * DA + P * h + P], start=(kb == 0), stop=(kb == nk - 1))
                        m.then_inc(sg("pv%d" % l), 1)
                    if ada_slot(l, t):
                        ada_rows(ada_slot(l, t), ADA1)

            def turn_cat(l):
                nb = len(out_blocks(l))
                pe.wait_ge(sg("cat%d" % l), nb * HEADS)
                for k in range(KD):
                    if k >= 2:
                        pe.wait_ge(sg("catT"), KD * l + k - 1)
                    for b in range(nb):
                        col = P * k if k < 4 else 3 * DA + P * (k - 4)
                        m = pe.transpose(ps[:, 1 + 2 * (k % 2), P * b:P * b + P], proj[:, b, col:col + P], ident)
                    m.then_inc(sg("catT ps"), 1)

            def project_out(l):
                for n2 in range(2):
                    for i, u in enumerate(at["out", l, n2]):
                        pe.wait_ge(lo_done, u.s + 1)
                        h, lo = (view(t, u) for t in split_at(u.s))
                        pe.wait_ge(sg("catT"), KD * l + 2 * i + 2)
                        for kk in range(2):
                            k = 2 * i + kk
                            for b in out_blocks(l):
                                m = mm3(ps[:, 2 * b + n2, :], hT_hi[:, k, P * b:P * b + P], hT_lo[:, k, P * b:P * b + P],
                                        h[:, kk, :], lo[:, kk, :], k == 0, k == KD - 1)
                        m.then_inc(unit_used, 1)

            def ffn():
                for g, (c0, gc) in enumerate(groups):
                    for c in range(c0, c0 + gc, 2):
                        for wi, key in enumerate(("w1", "w3")):
                            if c >= 2:
                                pe.wait_ge(sg(("silu", "gated up")[wi]), c)
                            for i, u in enumerate(at[key, c]):
                                pe.wait_ge(lo_done, u.s + 1)
                                h, lo = (view(t, u) for t in split_at(u.s))
                                if c + wi == 0:
                                    pe.wait_ge(sg("hT ffn0"), 4 * i + 4)
                                for ci in range(2):
                                    for kk in range(4):
                                        k = 4 * i + kk
                                        m = mm3(ps[:, 2 * wi + ci, :], h[:, kk, P * ci:P * ci + P], lo[:, kk, P * ci:P * ci + P],
                                                hT_hi[:, k, :], hT_lo[:, k, :], k == 0, k == KD - 1)
                                m.then_inc(unit_used, 1)
                    for n2 in range(2):
                        us = at["w2", g, n2]
                        for i, u in enumerate(us):
                            pe.wait_ge(lo_done, u.s + 1)
                            pe.wait_ge(sg("AT"), c0 + 2 * i + 2)
                            h, lo = (view(t, u) for t in split_at(u.s))
                            for b in range(NB):
                                if i == 0 and 2 * g + n2 > 0:
                                    pe.wait_ge(sg("y sum"), NB * (2 * g + n2 - 1) + b + 1)
                                for kk in range(2):
                                    a = (c0 + 2 * i + kk) % ATS
                                    m = mm3(ps[:, 4 + b, :], at_hi[:, a, P * b:P * b + P], at_lo[:, a, P * b:P * b + P],
                                            h[:, kk, :], lo[:, kk, :], i == 0 and kk == 0, i == len(us) - 1 and kk == 1)
                                if i == len(us) - 1 and b < NB - 1:
                                    m.then_inc(sg("y part"), 1)
                            m.then_inc(unit_used, 1)

            def route():
                pe.wait_ge(sg("hT32 ffn1"), KD)
                pe.wait_ge(sg("rw in"), 16)
                for tb in range(NLAT):
                    for k in range(KD):
                        m = pe.matmul(ps[:, 0, NE * tb:NE * tb + NE], hT32[:, k, P * tb:P * tb + P], rw[:, k, :],
                                      start=(k == 0), stop=(k == KD - 1))
                m.then_inc(sg("logits"), 1)
                pe.wait_ge(sg("mask"), 1)
                mask = st2[:, 64:80]
                pe.matmul(ps[:, 1, 0:8], triu, mask[:, 0:8], start=True, stop=True)
                pe.matmul(ps[:, 1, 8:16], ones, mask[:, 0:8], start=True, stop=False)
                pe.matmul(ps[:, 1, 8:16], triu, mask[:, 8:16], start=False, stop=True)
                pe.matmul(ps[:, 1, 16:24], ones, mask[:, 0:8], start=True, stop=False)
                pe.matmul(ps[:, 1, 16:24], ones, mask[:, 8:16], start=False, stop=True).then_inc(sg("counts"), 1)

            def permute(turn):
                pe.wait_ge(sg("perm"), NE * (turn + 1))
                for e in range(NE):
                    for tb in range(NLAT):
                        m = pe.matmul(ps[:, 0, e:e + 1], perm[:, e, tb, :].bitcast(F32), st2[:, 80 + 8 * tb + e:81 + 8 * tb + e],
                                      start=(tb == 0), stop=(tb == 1))
                m.then_inc(sg("slot gates"), 1)
                for e in range(NE):
                    if e >= 2:
                        pe.wait_ge(sg("scat"), NE * turn + e - 1)
                    for tb in range(NLAT):
                        m = pe.transpose(ps[:, 2 + e % 2, P * tb:P * tb + P], perm[:, e, tb, :].bitcast(F32), ident)
                    m.then_inc(sg("scat ps"), 1)
                pe.wait_ge(sg("scat"), NE * (turn + 1))
                pe.wait_ge(sg("slot gate"), turn + 1)

            def gather(e):
                for k in range(KD):
                    for tb in range(NLAT):
                        for part, src in enumerate((xg_hi, xg_lo)):
                            m = pe.matmul(ps[:, 2 + k // 4, P * (k % 4):P * (k % 4) + P], src[:, tb, P * k:P * k + P],
                                          perm[:, e, tb, :], start=(tb + part == 0), stop=(tb + part == 2))
                    if k % 4 == 3:
                        m.then_inc(sg("gathered"), 1)

            def experts(turn):
                base = NS0 + turn * NE * UE
                gather(0)
                with pe.Fori(0, NE) as e:
                    def took(s):
                        return e * UE + (base + s + 1)

                    def up(s, w):
                        for n in range(4):
                            i = (end_w1, end_w3)[w](s) - 3 + n
                            pe.wait_ge(lo_done, took(i))
                            for kk in range(2):
                                k = 2 * n + kk
                                r = [t[:, (base + i) % SPL, 512 * kk:512 * kk + 512] for t in (w_hi, w_lo)]
                                m = mm3(ps[:, 2 * (s % 2) + w, :], he_hi[:, k, :], he_lo[:, k, :], *r, k == 0, k == KD - 1)
                            m.then_inc(unit_used, 1)

                    def turn_a(s):
                        pe.wait_ge(sg("ae32"), e * STEPS + (STEPS * NE * turn + s + 1))
                        for j in range(4):
                            m = pe.transpose(ps[:, 4 + s % 2, P * j:P * j + P], ae32[:, s % 2, P * j:P * j + P], ident)
                        m.then_inc(sg("ae ps"), 1)

                    def down(s):
                        pe.wait_ge(sg("ae"), e * STEPS + (STEPS * NE * turn + s + 1))
                        for n in range(4):
                            i = end_w2(s) - 3 + n
                            pe.wait_ge(lo_done, took(i))
                            for n2 in range(2):
                                r = [t[:, (base + i) % SPL, 512 * n2:512 * n2 + 512] for t in (w_hi, w_lo)]
                                m = mm3(ps[:, 6 + n2, :], ae_hi[:, s % 2, P * n:P * n + P], ae_lo[:, s % 2, P * n:P * n + P],
                                        *r, s == 0 and n == 0, s == STEPS - 1 and n == 3)
                            m.then_inc(unit_used, 1)

                    pe.wait_ge(sg("he"), e + ((NE + 1) * turn + 1))
                    for s in range(STEPS):
                        up(s, 0)
                        if s:
                            turn_a(s - 1)
                        up(s, 1)
                        if s == 1:
                            pe.wait_ge(sg("yg"), e + ((NE + 1) * turn + 1))
                        if s:
                            down(s - 1)
                    turn_a(STEPS - 1)
                    gather(e + 1)
                    down(STEPS - 1)

            def combine(turn):
                for e in range(NE):
                    pe.wait_ge(sg("y split"), NE * turn + e + 1)
                    for tb in range(NLAT):
                        for n2 in range(2):
                            for part, src in enumerate((yh, yl)):
                                m = pe.matmul(ps[:, 2 * tb + n2, :], scat[:, e, P * tb:P * tb + P],
                                              src[:, e % 2, 512 * n2:512 * n2 + 512],
                                              start=(e == 0 and part == 0), stop=(e == NE - 1 and part == 1))
                    m.then_inc(sg("combined"), 1)
                pe.wait_ge(sg("yout"), NLAT * (turn + 1))

            pe.wait_ge(sg("cstat"), 1 + 2 * KD)
            pe.wait_ge(sg("pcol"), 2)
            for c in range(4):
                ada_rows(c, ADA0)
                ada_turn(c, ADA0)
            for l in range(2):
                turn_h("mix%d" % l, 5, NB)
                project_in(l)
                spatial(l)
                turn_qk(l)
                if l == 0:
                    pe.wait_ge(sg("gated0"), NB)
                    ada_some(4, 8)
                attend(l)
                turn_cat(l)
                project_out(l)
                turn_h("ffn%d" % l, 4, len(out_blocks(l)))
                if l == 0:
                    ffn()
            route()
            permute(0)
            experts(0)
            combine(0)
            pe.wait_ge(sg("flag set"), 1)
            busiest = pe.value_load(flag[0:1, 0:1], min_val=0, max_val=NLAT * P)
            with pe.If(busiest > P):
                permute(1)
                experts(1)
                combine(1)

        @block.scalar
        def _(act):
            cur = [0]
            chain = [0]
            stage_end = [in_end[0]]

            def link(ins):
                chain[0] += 1
                ins.then_inc(act_ch, 1)
                act.wait_ge(act_ch, chain[0])

            def split_upto(s):
                s = min(s, stage_end[0])
                while cur[0] <= s:
                    u = split_units[cur[0]]
                    act.wait_ge(raw_in[u.k % RAW], raw_count(u.k))
                    if u.s >= SPL:
                        act.wait_ge(unit_used, u.s - SPL + 1)
                    act.activation(w_hi[:, u.s % SPL, :], raw_at(u.k), ACT.Copy).then_inc(hi_done, 1)
                    cur[0] += 1

            def last_s(key):
                return at[key][-1].s

            act.wait_ge(sg("cstat"), 1)
            act.wait_ge(sg("small T"), 3)
            for r in range(2):
                for k in range(KD):
                    act.activation(cstat[:, k, r:r + 1], ps[:, 0, KD * r + k:KD * r + k + 1], ACT.Silu).then_inc(sg("cstat"), 1)

            act.wait_ge(sg("lam dots"), 1)
            act.activation(lam_s[:, :, 2:4], lam_s[:, :, 0:2], ACT.Exp).then_inc(sg("lam exp"), 1)

            def prenorm(key, l, which, nb):
                for b in range(nb):
                    if key == "mix0":
                        act.wait_ge(s_x, 16 * NB)
                    else:
                        act.wait_ge(sg("x " + ("ffn" if which == 0 else "mix%d" % l)), b + 1)
                    act.activation(xn[:, b, :], xs[:, b, :], ACT.Square, accum_out=st[:, b:b + 1]).then_inc(sg("ss " + key), 1)
                act.wait_ge(sg("ms " + key), 1)
                act.activation(st[:, 8:8 + nb], st[:, 4:4 + nb], ACT.Sqrt).then_inc(sg("rt " + key), 1)
                act.wait_ge(sg("ada fin"), 4 if key == "mix0" else 20)
                for k in range(KD):
                    act.wait_ge(sg("hT ps " + key), k + 1)
                    bank = (5 if which == 0 else 4) + k % 2
                    for r in range(nb // 2):
                        ins = act.activation(hT32[:, k, 256 * r:256 * r + 256], ps[:, bank, 256 * r:256 * r + 256], ACT.Identity,
                                             bias=mod_b[:, l, which, k, r:r + 1], scale=mod_a[:, l, which, k, r:r + 1])
                    ins.then_inc(sg("hT32 " + key), 1)

            def postnorm(key, srcs, junk_):
                for b, src in enumerate(srcs):
                    if b:
                        act.wait_ge(sg("ss " + key), b)
                    act.activation(junk_(b, src), src, ACT.Square, accum_out=st[:, 16 + b:17 + b]).then_inc(sg("ss " + key), 1)
                act.wait_ge(sg("ms " + key), 1)
                act.activation(st[:, 24:24 + len(srcs)], st[:, 20:20 + len(srcs)], ACT.Sqrt).then_inc(sg("rt " + key), 1)

            for l in range(2):
                nb = len(out_blocks(l))
                if l == 1:
                    act.wait_ge(sg("x ffn"), NB)
                prenorm("mix%d" % l, l, 0, NB)
                for jn, j in enumerate(IN_ORDER):
                    split_upto(last_s(("in", l, j)) + AHEAD)
                    act.wait_ge(unit_used, last_s(("in", l, j)) + 1)
                    if jn == 0:
                        act.wait_ge(sg("hT mix%d" % l), KD)
                    for b in in_blocks(l, j):
                        act.activation(proj[:, b, 512 * j:512 * j + 512], ps[:, 4 * (jn % 2) + b, :], ACT.Copy)\
                            .then_inc(sg("proj%d" % l), 1)
                    if jn == 2:
                        act.wait_ge(sg("ln ms%d" % l), 1)
                        act.activation(st[:, 44:44 + nb], st[:, 40:40 + nb], ACT.Sqrt).then_inc(sg("ln rt%d" % l), 1)
                act.wait_ge(sg("wsT ps"), l + 1)
                act.activation(wsT[:, :], ps[:, 2, :], ACT.Copy).then_inc(sg("wsT"), 1)
                for i, (t, b) in enumerate(qk[l]):
                    act.wait_ge(sg("qk ps%d" % l), i + 1)
                    dst = (qT, kT)[t]
                    act.activation(dst[:, :, P * b:P * b + P], ps[:, i % 2, :].rearrange("p (h t) -> p h t", h=HEADS), ACT.Copy)\
                        .then_inc(sg("qkT%d" % l), 1)
                its = items[l]
                n = len(its)
                for t in range(n + 2):
                    if t < n:
                        nk = 512 if its[t][0] < NLAT else 256
                        act.wait_ge(sg("rowmax%d" % l), t + 1)
                        if t >= 2:
                            act.wait_ge(sg("wT ps%d" % l), t - 1)
                        for m_ in range(2):
                            act.activation(pr[:, t % 2, m_, 0:nk], ps[:, 2 * (t % 2) + m_, 0:nk], ACT.Exp, scale=SCALE,
                                           bias=att[:, t % 2, 2 + m_:3 + m_], accum_out=att[:, t % 2, 4 + m_:5 + m_])\
                                .then_inc(sg("exp%d" % l), 1)
                    if 1 <= t <= n:
                        i = t - 1
                        nk = 512 if its[i][0] < NLAT else 256
                        act.wait_ge(sg("wT ps%d" % l), i + 1)
                        if i >= 2:
                            act.wait_ge(sg("pv%d" % l), i - 1)
                        act.activation(wT[:, i % 2, 0:nk], ps[:, 4, 0:nk], ACT.Copy).then_inc(sg("wT%d" % l), 1)
                    if t >= 2:
                        i = t - 2
                        b, h = its[i]
                        act.wait_ge(sg("o%d" % l), i + 1)
                        if i:
                            act.wait_ge(sg("o sq%d" % l), i)
                        act.activation(osq[:, :], proj[:, b, P * h:P * h + P], ACT.Square,
                                       accum_out=st2[:, i:i + 1]).then_inc(sg("o sq%d" % l), 1)
                act.wait_ge(sg("o ms%d" % l), 1)
                act.activation(st2[:, 32:32 + n], st2[:, 16:16 + n], ACT.Sqrt).then_inc(sg("o rt%d" % l), 1)
                stage_end[0] = in_end[l + 1]
                split_upto(at["out", l, 0][0].s + AHEAD)
                for k in range(KD):
                    act.wait_ge(sg("catT ps"), KD * l + k + 1)
                    act.activation(hT_hi[:, k, 0:P * nb], ps[:, 1 + 2 * (k % 2), 0:P * nb], ACT.Copy).then_inc(sg("catT hi"), 1)
                split_upto(last_s(("out", l, 1)))
                act.wait_ge(unit_used, last_s(("out", l, 1)) + 1)
                postnorm("pm%d" % l, [ps[:, 2 * b:2 * b + 2, :] for b in out_blocks(l)],
                         lambda b, src: xn[:, b, :].rearrange("p (a n) -> p a n", a=2))
                prenorm("ffn%d" % l, l, 1, nb)
                if l == 0:
                    split_upto(at["w1", 0][0].s + AHEAD)
                    for g, (c0, gc) in enumerate(groups):
                        for c in range(c0, c0 + gc, 2):
                            split_upto(last_s(("w1", c)) + AHEAD)
                            act.wait_ge(unit_used, last_s(("w1", c)) + 1)
                            if c >= 2:
                                act.wait_ge(sg("gated up"), c)
                            for ci in range(2):
                                act.activation(sgf[:, ci, :], ps[:, ci, :], ACT.Silu).then_inc(sg("silu"), 1)
                            split_upto(last_s(("w3", c)) + AHEAD)
                            for ci in range(2):
                                act.wait_ge(sg("gated up"), c + ci + 1)
                                act.activation(at_hi[:, (c + ci) % ATS, :], a32[:, ci, :], ACT.Copy).then_inc(sg("AT hi"), 1)
                        for n2 in range(2):
                            split_upto(last_s(("w2", g, n2)) + AHEAD)
                    act.wait_ge(sg("y sum"), NB * 2 * len(groups))
                    postnorm("pf0", [y0[:, b, :] for b in range(NB)], lambda b, src: sgf[:, :, :].rearrange("p a n -> p (a n)"))

            def scatters(turn):
                act.wait_ge(sg("slot gates"), turn + 1)
                act.activation(st2[:, 96:104], ps[:, 0, 0:NE], ACT.Copy).then_inc(sg("slot gate"), 1)
                for e in range(NE):
                    act.wait_ge(sg("scat ps"), NE * turn + e + 1)
                    act.activation(scat[:, e, :], ps[:, 2 + e % 2, 0:NLAT * P], ACT.Copy).then_inc(sg("scat"), 1)

            def modulate(gathered):
                for k in range(KD):
                    act.wait_ge(sg("gathered"), gathered + (1 + k // 4))
                    ins = act.activation(he32[:, k, :], ps[:, 2 + k // 4, P * (k % 4):P * (k % 4) + P], ACT.Identity,
                                         bias=mod_b[:, 1, 1, k, 0:1], scale=mod_a[:, 1, 1, k, 0:1])
                ins.then_inc(sg("he32"), 1)

            def outputs(dst, gate):
                act.activation(dst.rearrange("p (a n) -> p a n", a=2), ps[:, 6:8, :], ACT.Identity, scale=gate).then_inc(sg("yg"), 1)

            def experts(turn):
                base = turn * NE * UE
                modulate(2 * (NE + 1) * turn)
                with act.Fori(0, NE) as e:
                    done = [0]

                    def split_to(i1):
                        for i in range(done[0], min(i1, UE - 1) + 1):
                            k, s = K0 + base + i, NS0 + base + i
                            act.wait_ge(raw_in[k % RAW], e * (16 * UE // RAW) + raw_count(k))
                            act.wait_ge(unit_used, e * UE + (s - SPL + 1))
                            act.activation(w_hi[:, s % SPL, :], raw_at(k), ACT.Copy).then_inc(hi_done, 1)
                        done[0] = max(done[0], i1 + 1)

                    split_to(AHEAD)
                    act.wait_ge(unit_used, e * UE + (NS0 + base))
                    outputs(yg[:, e, :], st2[:, bass.ds(e + 95, 1)])
                    for s in range(STEPS):
                        split_to(end_w1(s) + AHEAD)
                        act.wait_ge(unit_used, e * UE + (NS0 + base + end_w1(s) + 1))
                        if s >= 2:
                            act.wait_ge(sg("ae32"), e * STEPS + (STEPS * NE * turn + s - 1))
                        act.activation(sge[:, s % 2, :], ps[:, 2 * (s % 2), :], ACT.Silu).then_inc(sg("silu e"), 1)
                        if s:
                            act.wait_ge(sg("ae ps"), e * STEPS + (STEPS * NE * turn + s))
                            act.activation(ae_hi[:, (s - 1) % 2, :], ps[:, 4 + (s - 1) % 2, :], ACT.Copy).then_inc(sg("ae hi"), 1)
                        split_to(end_w3(s) + AHEAD)
                        if s:
                            split_to(end_w2(s - 1) + AHEAD)
                    act.wait_ge(sg("ae ps"), e * STEPS + (STEPS * NE * turn + STEPS))
                    act.activation(ae_hi[:, (STEPS - 1) % 2, :], ps[:, 4 + (STEPS - 1) % 2, :], ACT.Copy).then_inc(sg("ae hi"), 1)
                    split_to(UE - 1)
                    modulate(e * 2 + (2 * (NE + 1) * turn + 2))
                act.wait_ge(unit_used, NS0 + base + NE * UE)
                outputs(yg[:, 0, :], st2[:, 96 + NE - 1:96 + NE])

            def combine(turn):
                act.wait_ge(sg("yg"), (NE + 1) * (turn + 1))
                act.wait_ge(sg("he"), (NE + 1) * (turn + 1))
                for e in range(NE):
                    if e >= 2:
                        act.wait_ge(sg("combined"), NE * turn + e - 1)
                    act.activation(yh[:, e % 2, :], yg[:, (e + 1) % NE, :], ACT.Copy).then_inc(sg("y hi"), 1)
                act.wait_ge(sg("yout"), NLAT * (turn + 1))

            act.wait_ge(sg("gap"), NLAT)
            act.activation(rs[:, 82:84], rs[:, 80:82], ACT.Exp).then_inc(sg("gap exp"), 1)
            scatters(0)
            experts(0)
            combine(0)
            act.wait_ge(sg("flag set"), 1)
            busiest = act.value_load(flag[0:1, 0:1], min_val=0, max_val=NLAT * P)
            with act.If(busiest > P):
                scatters(1)
                experts(1)
                combine(1)
            postnorm("pf1", [yout[:, b, :] for b in range(NLAT)], lambda b, src: junk[:, :])

        @block.vector
        def _(dve):
            cur = [0]
            chain = [0]
            stage_end = [in_end[0]]

            def link(ins):
                chain[0] += 1
                ins.then_inc(dve_ch, 1)
                dve.wait_ge(dve_ch, chain[0])

            def split_lo(s_, k, hi_count):
                dve.wait_ge(hi_done, hi_count)
                dve.tensor_tensor(w_lo[:, s_ % SPL, :], raw_at(k), w_hi[:, s_ % SPL, :].bitcast(F32), ALU.subtract)\
                    .then_inc(lo_done, 1)

            def split_upto(s):
                s = min(s, stage_end[0])
                while cur[0] <= s:
                    u = split_units[cur[0]]
                    split_lo(u.s, u.k, u.s + 1)
                    cur[0] += 1

            def last_s(key):
                return at[key][-1].s

            def root(src, ms, rt, out_, key, n):
                dve.tensor_scalar(ms, src, 1.0 / n, EPS, ALU.mult, ALU.add).then_inc(sg("ms " + key), 1)
                dve.wait_ge(sg("rt " + key), 1)
                link(dve.reciprocal(out_, rt))

            link(dve.memset(cstat[:, :, :], 0.0))
            dve.engine_nop().then_inc(sg("cstat"), 1)
            dve.wait_ge(sg("params in"), 16 * 14)
            for l in range(2):
                link(dve.tensor_tensor(lam_t[:, l, :, :], lam_bc[:, l, 0:4:2, :], lam_bc[:, l, 1:4:2, :], ALU.mult))
                link(dve.tensor_reduce(lam_s[:, l, 0:2], lam_t[:, l, :, :], AX.X, ALU.add))
            dve.engine_nop().then_inc(sg("lam dots"), 1)
            dve.wait_ge(sg("lam exp"), 1)
            for l in range(2):
                lam_init = 0.8 - 0.6 * math.exp(-0.3 * l)
                link(dve.tensor_tensor(lam_s[:, l, 4:5], lam_s[:, l, 3:4], lam_s[:, l, 2:3], ALU.subtract))
                link(dve.tensor_scalar(lam_s[:, l, 5:6], lam_s[:, l, 4:5], -lam_init, None, ALU.add))
            dve.wait_ge(sg("small T"), 3)
            for l in range(2):
                dve.tensor_copy(pcol[:, l, :], ps[:, 1 + l, 0:68]).then_inc(sg("pcol"), 1)
            dve.wait_ge(sg("pcol"), 2)

            def ada_copy(c, bank):
                dve.wait_ge(ada_used, 4 * (c + 1))
                dve.tensor_copy(arow[:, :], ps[:, bank, :]).then_inc(sg("arow"), 1)

            def ada_finish(c, bank):
                l, part, half = ADA_SEQ[c]
                dve.wait_ge(sg("ada post"), c + 1)
                if part in (2, 5):
                    dve.wait_ge(s_bc, 32 * (gate_chunks.index(c) + 1))
                    for r in streams(l):
                        g = gg[:, gate_at(l, part // 3, r), 512 * half:512 * half + 512]
                        link(dve.tensor_tensor(g, ps[:, bank + 1 - r, :], ab_bc[:, :], ALU.add))
                        ins = dve.tensor_tensor(g, g, pg_bc[:, :], ALU.mult)
                else:
                    w, ks = part // 3, slice(4 * half, 4 * half + 4)
                    new = ps[:, bank + 1, 0:8].rearrange("p (k r) -> p k r", r=2)

                    def col(i):
                        return pcol[:, l, i + 4 * half:i + 4 * half + 4].unsqueeze(2).to_broadcast([P, 4, 2])
                    if part % 3 == 0:
                        ins = dve.tensor_tensor(mod_b[:, l, w, ks, :], new, col(part * KD), ALU.add)
                    else:
                        a = mod_a[:, l, w, ks, :]
                        link(dve.tensor_tensor(a, new, col(part * KD), ALU.add))
                        ins = dve.scalar_tensor_tensor(out=a, in0=a, scalar=1.0, in1=col(48 + KD * w), op0=ALU.add, op1=ALU.mult)
                ins.then_inc(sg("ada fin"), 1)

            def prenorm(key, nb):
                dve.wait_ge(sg("ss " + key), nb)
                root(st[:, 0:nb], st[:, 4:4 + nb], st[:, 8:8 + nb], st[:, 12:12 + nb], key, D)
                for b in range(nb):
                    dve.tensor_scalar(xn[:, b, :], xs[:, b, :], st[:, 12 + b:13 + b], None, ALU.mult).then_inc(sg("xn " + key), 1)

            def split_h(key):
                for k in range(KD):
                    dve.wait_ge(sg("hT32 " + key), k + 1)
                    link(dve.tensor_copy(hT_hi[:, k, :], hT32[:, k, :]))
                    dve.tensor_tensor(hT_lo[:, k, :], hT32[:, k, :], hT_hi[:, k, :].bitcast(F32), ALU.subtract)\
                        .then_inc(sg("hT " + key), 1)

            def postnorm(key, srcs, which, done):
                layer = int(key[-1])
                dve.wait_ge(sg("ss " + key), len(srcs))
                n = len(srcs)
                root(st[:, 16:16 + n], st[:, 20:20 + n], st[:, 24:24 + n], st[:, 28:28 + n], key, D)
                for b, src in enumerate(srcs):
                    if b:
                        dve.wait_ge(sg(done), b)
                    r = b // NLAT
                    t, g, o = ptmp[:, :], gg[:, gate_at(layer, which, r), :], xs[:, b, :]
                    if len(src.shape) == 3:
                        t, g = (v.rearrange("p (a n) -> p a n", a=2) for v in (t, g))
                    link(dve.scalar_tensor_tensor(out=t, in0=src, scalar=st[:, 28 + b:29 + b], in1=g, op0=ALU.mult, op1=ALU.mult))
                    dve.tensor_tensor(o, o, ptmp[:, :], ALU.add).then_inc(sg(done), 1)

            def rope(l, b, t):
                cos = cst[:, C_COS + HD * b:C_COS + HD * b + HD].unsqueeze(1).to_broadcast([P, 8, HD])
                sin = cst[:, C_SIN + HD * b:C_SIN + HD * b + HD].rearrange("p (r f i) -> p r f i", r=2, f=2)
                src, tmp, turned = proj[:, b, DA * t:DA * t + DA], rtmp[:, 0:DA], rtmp[:, DA:2 * DA]
                pair = src.rearrange("p (h r f i) -> p h r f i", r=2, f=2, i=16)
                tv = tmp.rearrange("p (h r f i) -> p h r f i", r=2, f=2, i=16)
                dve.tensor_tensor(turned.rearrange("p (h d) -> p h d", d=HD), src.rearrange("p (h d) -> p h d", d=HD), cos, ALU.mult)
                for f in range(2):
                    link(dve.tensor_tensor(tv[:, :, :, f, :], pair[:, :, :, 1 - f, :],
                                           sin[:, :, f, :].unsqueeze(1).to_broadcast([P, 8, 2, 16]), ALU.mult))
                dve.tensor_tensor(src, turned, tmp, ALU.add).then_inc(sg("rope%d" % l), 1)
                dve.wait_ge(sg("rope%d" % l), NLAT * t + b + 1)

            def spatial_stats(l, b):
                link(dve.bn_stats(st2[:, 104:110], proj[:, b, 4 * DA:5 * DA]))
                link(dve.bn_aggr(st[:, 48 + 2 * b:50 + 2 * b], st2[:, 104:110]))

            def spatial_root(l, nb):
                dve.tensor_scalar(st[:, 40:40 + nb], st[:, 49:49 + 2 * nb:2], EPS, None, ALU.add).then_inc(sg("ln ms%d" % l), 1)

            def spatial_norm(l, b):
                v = proj[:, b, 4 * DA:5 * DA]
                link(dve.reciprocal(st[:, 36 + b:37 + b], st[:, 44 + b:45 + b]))
                link(dve.tensor_scalar(v, v, st[:, 48 + 2 * b:49 + 2 * b], st[:, 36 + b:37 + b], ALU.subtract, ALU.mult))
                link(dve.tensor_tensor(v, v, lng_bc[:, l, :], ALU.mult))
                dve.tensor_tensor(v, v, lnb_bc[:, l, :], ALU.add).then_inc(sg("vn%d" % l), 1)

            def project_in(l):
                nb = len(out_blocks(l))
                for jn, j in enumerate(IN_ORDER):
                    for n, u in enumerate(at["in", l, j]):
                        split_upto(u.s + AHEAD)
                        if n == 0 and jn in (1, 3, 4):
                            dve.wait_ge(sg("proj%d" % l), proj_n[l][jn - 1])
                        if jn == 1 and n < nb:
                            spatial_stats(l, n)
                        if jn == 2 and n == 0:
                            spatial_root(l, nb)
                        if jn == 3 and n == 0:
                            dve.wait_ge(sg("ln rt%d" % l), 1)
                        if jn == 3 and n < nb:
                            spatial_norm(l, n)
                        if jn in (3, 4) and n >= NLAT:
                            rope(l, n - NLAT, jn - 3)
                dve.wait_ge(sg("proj%d" % l), proj_n[l][4])

            def gate(l):
                for b in out_blocks(l):
                    dve.wait_ge(sg("mixed%d" % l), b + 1)
                    for g in range(4):
                        u = proj[:, b, 3 * DA + P * g:3 * DA + P * g + P]
                        ins = dve.scalar_tensor_tensor(out=u, in0=ps[:, 4 + b, P * g:P * g + P], scalar=pcol[:, l, 64 + g:65 + g],
                                                       in1=u, op0=ALU.add, op1=ALU.mult)
                    ins.then_inc(sg("gated%d" % l), 1)

            def attend(l):
                its = items[l]
                n = len(its)
                for t in range(n + 2):
                    if 1 <= t <= n:
                        i = t - 1
                        p = i % 2
                        nk = 512 if its[i][0] < NLAT else 256
                        dve.wait_ge(sg("exp%d" % l), 2 * (i + 1))
                        link(dve.reciprocal(att[:, p, 6:8], att[:, p, 4:6]))
                        link(dve.tensor_scalar(att[:, p, 7:8], att[:, p, 7:8], lam_s[:, l, 5:6], None, ALU.mult))
                        link(dve.tensor_scalar(pr[:, p, 1, 0:nk], pr[:, p, 1, 0:nk], att[:, p, 7:8], None, ALU.mult))
                        dve.scalar_tensor_tensor(out=pr[:, p, 0, 0:nk], in0=pr[:, p, 0, 0:nk], scalar=att[:, p, 6:7],
                                                 in1=pr[:, p, 1, 0:nk], op0=ALU.mult, op1=ALU.add).then_inc(sg("weights%d" % l), 1)
                    if ada_slot(l, t - 1):
                        ada_finish(ada_slot(l, t - 1), ADA1)
                    if t < n:
                        p = t % 2
                        nk = 512 if its[t][0] < NLAT else 256
                        dve.wait_ge(sg("scores%d" % l), t + 1)
                        link(dve.tensor_reduce(att[:, p, 0:2], ps[:, 2 * p:2 * p + 2, 0:nk], AX.X, ALU.max))
                        dve.tensor_scalar(att[:, p, 2:4], att[:, p, 0:2], -SCALE, None, ALU.mult).then_inc(sg("rowmax%d" % l), 1)
                    if t >= 2:
                        i = t - 2
                        b, h = its[i]
                        dve.wait_ge(sg("pv%d" % l), i + 1)
                        dve.tensor_copy(proj[:, b, P * h:P * h + P], ps[:, 5, 0:P]).then_inc(sg("o%d" % l), 1)
                    if ada_slot(l, t):
                        ada_copy(ada_slot(l, t), ADA1)
                dve.wait_ge(sg("o sq%d" % l), n)
                dve.wait_ge(sg("o%d" % l), n)
                dve.tensor_scalar(st2[:, 16:16 + n], st2[:, 0:n], 1.0 / P, EPS, ALU.mult, ALU.add).then_inc(sg("o ms%d" % l), 1)
                dve.wait_ge(sg("o rt%d" % l), 1)
                link(dve.reciprocal(st2[:, 48:48 + n], st2[:, 32:32 + n]))
                keep = 1.0 - (0.8 - 0.6 * math.exp(-0.3 * l))
                link(dve.tensor_scalar(st2[:, 48:48 + n], st2[:, 48:48 + n], keep, None, ALU.mult))
                for i, (b, h) in enumerate(its):
                    o = proj[:, b, P * h:P * h + P]
                    dve.scalar_tensor_tensor(out=o, in0=o, scalar=st2[:, 48 + i:49 + i], in1=sub_bc[:, l, :],
                                             op0=ALU.mult, op1=ALU.mult).then_inc(sg("cat%d" % l), 1)

            def ffn():
                for g, (c0, gc) in enumerate(groups):
                    for c in range(c0, c0 + gc, 2):
                        split_upto(last_s(("w1", c)) + AHEAD)
                        split_upto(last_s(("w3", c)) + AHEAD)
                        dve.wait_ge(unit_used, last_s(("w3", c)) + 1)
                        for ci in range(2):
                            dve.wait_ge(sg("silu"), c + ci + 1)
                            if c:
                                dve.wait_ge(sg("AT"), c + ci - 1)
                            dve.tensor_tensor(a32[:, ci, :], sgf[:, ci, :], ps[:, 2 + ci, :], ALU.mult).then_inc(sg("gated up"), 1)
                        for ci in range(2):
                            a = (c + ci) % ATS
                            dve.wait_ge(sg("AT hi"), c + ci + 1)
                            dve.tensor_tensor(at_lo[:, a, :], a32[:, ci, :], at_hi[:, a, :].bitcast(F32), ALU.subtract)\
                                .then_inc(sg("AT"), 1)
                    for n2 in range(2):
                        split_upto(last_s(("w2", g, n2)) + AHEAD)
                        for b in range(NB):
                            if b < NB - 1:
                                dve.wait_ge(sg("y part"), (NB - 1) * (2 * g + n2) + b + 1)
                            else:
                                dve.wait_ge(unit_used, last_s(("w2", g, n2)) + 1)
                            y = y0[:, b, 512 * n2:512 * n2 + 512]
                            if g == 0:
                                dve.tensor_copy(y, ps[:, 4 + b, :]).then_inc(sg("y sum"), 1)
                            else:
                                dve.wait_ge(sg("y sum"), NB * (2 * (g - 1) + n2) + b + 1)
                                dve.tensor_tensor(y, y, ps[:, 4 + b, :], ALU.add).then_inc(sg("y sum"), 1)

            def route():
                lg, mx, idf = rs[:, 0:16], rs[:, 16:32], rs[:, 32:48]
                oh = rs[:, 48:80].rearrange("p (j t e) -> p j t e", j=2, t=NLAT)
                dve.wait_ge(sg("logits"), 1)
                link(dve.tensor_copy(lg, ps[:, 0, 0:16]))
                for tb in range(NLAT):
                    o = slice(8 * tb, 8 * tb + 8)
                    link(dve.max(mx[:, o], lg[:, o]))
                    link(dve.max_index(idx[:, tb, :], mx[:, o], lg[:, o]))
                link(dve.tensor_copy(idf, idx[:, :, :].rearrange("p t e -> p (t e)")))
                for tb in range(NLAT):
                    for j in range(2):
                        link(dve.tensor_scalar(oh[:, j, tb, :], iota[:, 0:8], idf[:, 8 * tb + j:8 * tb + j + 1], None, ALU.is_equal))
                    dve.tensor_tensor(rs[:, 80 + tb:81 + tb], mx[:, 8 * tb + 1:8 * tb + 2], mx[:, 8 * tb:8 * tb + 1], ALU.subtract)\
                        .then_inc(sg("gap"), 1)
                link(dve.tensor_tensor(st2[:, 64:80], rs[:, 48:64], rs[:, 64:80], ALU.add))
                dve.engine_nop().then_inc(sg("mask"), 1)
                dve.wait_ge(sg("gap exp"), 1)
                link(dve.tensor_scalar(rs[:, 84:86], rs[:, 82:84], 1.0, None, ALU.add))
                link(dve.reciprocal(rs[:, 86:88], rs[:, 84:86]))
                link(dve.tensor_tensor(rs[:, 88:90], rs[:, 86:88], rs[:, 82:84], ALU.mult))
                for tb in range(NLAT):
                    gt = st2[:, 80 + 8 * tb:88 + 8 * tb]
                    link(dve.tensor_scalar(gt, oh[:, 0, tb, :], rs[:, 86 + tb:87 + tb], None, ALU.mult))
                    link(dve.scalar_tensor_tensor(out=gt, in0=oh[:, 1, tb, :], scalar=rs[:, 88 + tb:89 + tb], in1=gt,
                                                  op0=ALU.mult, op1=ALU.add))
                dve.wait_ge(sg("counts"), 1)
                link(dve.tensor_tensor(rs[:, 96:112], ps[:, 1, 0:16], st2[:, 64:80], ALU.mult))
                link(dve.tensor_scalar(rs[:, 96:112], rs[:, 96:112], -1.0, None, ALU.add))
                link(dve.tensor_scalar(rs[:, 112:128], rs[:, 96:112], -float(P), None, ALU.add))
                link(dve.tensor_reduce(rs[:, 90:91], ps[:, 1, 16:24], AX.X, ALU.max))
                dve.tensor_copy(flag[:, :], rs[:, 90:91]).then_inc(sg("flag set"), 1)
                dve.wait_ge(sg("flag set"), 1)

            def permute(turn):
                dve.tensor_scalar(perm[:, NE, :, :], cst[:, C_IOTA:C_IOTA + P].unsqueeze(1).to_broadcast([P, NLAT, P]), -1.0, None,
                                  ALU.is_equal)
                for e in range(NE):
                    for tb in range(NLAT):
                        place_ = 96 + 16 * turn + 8 * tb + e
                        ins = dve.tensor_scalar(perm[:, e, tb, :], iota, rs[:, place_:place_ + 1], None, ALU.is_equal)
                    ins.then_inc(sg("perm"), 1)

            def split_he(n):
                dve.wait_ge(sg("he32"), n)
                dve.tensor_copy(he_hi[:, :, :], he32[:, :, :]).then_inc(sg("he hi"), 1)
                dve.wait_ge(sg("he hi"), n)
                dve.tensor_tensor(he_lo[:, :, :], he32[:, :, :], he_hi[:, :, :].bitcast(F32), ALU.subtract).then_inc(sg("he"), 1)

            def experts(turn):
                base = turn * NE * UE
                split_he((NE + 1) * turn + 1)
                with dve.Fori(0, NE) as e:
                    done = [0]

                    def split_to(i1):
                        for i in range(done[0], min(i1, UE - 1) + 1):
                            split_lo(NS0 + base + i, K0 + base + i, e * UE + (NS0 + base + i + 1))
                        done[0] = max(done[0], i1 + 1)

                    split_to(AHEAD)

                    def lo_a(s):
                        dve.wait_ge(sg("ae hi"), e * STEPS + (STEPS * NE * turn + s + 1))
                        dve.tensor_tensor(ae_lo[:, s % 2, :], ps[:, 4 + s % 2, :], ae_hi[:, s % 2, :].bitcast(F32), ALU.subtract)\
                            .then_inc(sg("ae"), 1)

                    for s in range(STEPS):
                        split_to(end_w1(s) + AHEAD)
                        if s:
                            lo_a(s - 1)
                        split_to(end_w3(s) + AHEAD)
                        dve.wait_ge(sg("silu e"), e * STEPS + (STEPS * NE * turn + s + 1))
                        dve.wait_ge(unit_used, e * UE + (NS0 + base + end_w3(s) + 1))
                        dve.tensor_tensor(ae32[:, s % 2, :], sge[:, s % 2, :], ps[:, 2 * (s % 2) + 1, :], ALU.mult)\
                            .then_inc(sg("ae32"), 1)
                        if s:
                            split_to(end_w2(s - 1) + AHEAD)
                    lo_a(STEPS - 1)
                    split_to(UE - 1)
                    split_he(e + ((NE + 1) * turn + 2))

            def combine(turn):
                for e in range(NE):
                    dve.wait_ge(sg("y hi"), NE * turn + e + 1)
                    dve.tensor_tensor(yl[:, e % 2, :], yg[:, (e + 1) % NE, :], yh[:, e % 2, :].bitcast(F32), ALU.subtract)\
                        .then_inc(sg("y split"), 1)
                dve.wait_ge(sg("combined"), NE * (turn + 1))
                for tb in range(NLAT):
                    y = yout[:, tb, :].rearrange("p (a n) -> p a n", a=2)
                    v = ps[:, 2 * tb:2 * tb + 2, :]
                    if turn == 0:
                        dve.tensor_copy(y, v).then_inc(sg("yout"), 1)
                    else:
                        dve.tensor_tensor(y, y, v, ALU.add).then_inc(sg("yout"), 1)
                dve.wait_ge(sg("yout"), NLAT * (turn + 1))

            for c in range(4):
                ada_copy(c, ADA0)
                ada_finish(c, ADA0)
            for l in range(2):
                nb = len(out_blocks(l))
                prenorm("mix%d" % l, NB)
                split_h("mix%d" % l)
                project_in(l)
                gate(l)
                if l == 0:
                    for c in range(4, 8):
                        ada_copy(c, ADA1)
                        ada_finish(c, ADA1)
                attend(l)
                stage_end[0] = in_end[l + 1]
                split_upto(at["out", l, 0][0].s + AHEAD)
                for k in range(KD):
                    dve.wait_ge(sg("catT hi"), KD * l + k + 1)
                    dve.tensor_tensor(hT_lo[:, k, 0:P * nb], ps[:, 1 + 2 * (k % 2), 0:P * nb], hT_hi[:, k, 0:P * nb].bitcast(F32), ALU.subtract)\
                        .then_inc(sg("catT"), 1)
                split_upto(last_s(("out", l, 1)))
                postnorm("pm%d" % l, [ps[:, 2 * b:2 * b + 2, :] for b in out_blocks(l)], 0, "x mix%d" % l)
                for b in out_blocks(l):
                    dve.wait_ge(sg("x mix%d" % l), b + 1)
                prenorm("ffn%d" % l, nb)
                if l == 0:
                    split_h("ffn0")
                    split_upto(at["w1", 0][0].s + AHEAD)
                    ffn()
                    postnorm("pf0", [y0[:, b, :] for b in range(NB)], 1, "x ffn")
            dve.wait_ge(sg("xn ffn1"), NLAT)
            link(dve.tensor_copy(xg_hi[:, :, :], xn[:, 0:NLAT, :]))
            link(dve.tensor_tensor(xg_lo[:, :, :], xn[:, 0:NLAT, :], xg_hi[:, :, :].bitcast(F32), ALU.subtract))
            route()
            permute(0)
            experts(0)
            combine(0)
            busiest = dve.value_load(flag[0:1, 0:1], min_val=0, max_val=NLAT * P)
            with dve.If(busiest > P):
                permute(1)
                experts(1)
                combine(1)
            postnorm("pf1", [yout[:, b, :] for b in range(NLAT)], 1, "final x")

    return nc


_INS = ['x', 'c', 'ctx', 'c_ctx', 'ada_w', 'ada_b', 'pre_mix_g', 'post_mix_g', 'pre_ffn_g', 'post_ffn_g', 'w_in',
        'w_out', 'lam_q1', 'lam_k1', 'lam_q2', 'lam_k2', 'subln_g', 'sg_ln_g', 'sg_ln_b', 'sg_w', 'sg_b', 'ffn_w1',
        'ffn_w3', 'ffn_w2', 'router_w', 'moe_w1', 'moe_w3', 'moe_w2']


def kernel(**inputs):
    import numpy as _np
    import concourse.bacc as _bacc
    from concourse import mybir as _mybir
    from concourse.bass_utils import run_bass_kernel_spmd as _run

    nc = _bacc.Bacc("TRN2", target_bir_lowering=False, num_devices=1)
    arrays, args = {}, []
    for name in _INS:
        arrays[f"in_{name}"] = _np.ascontiguousarray(inputs[name])
    arrays["in_const"] = constants()
    for name, a in arrays.items():
        args.append(nc.dram_tensor(name, a.shape, _mybir.dt.from_np(a.dtype), kind="ExternalInput").ap())
    args.append(nc.dram_tensor("out_0", (1, NLAT * P, D), _mybir.dt.float32, kind="ExternalOutput").ap())
    program(nc, *args)
    r = _run(nc, [arrays], core_ids=[0])
    return r.results[0]["out_0"]
```

```python
from contextlib import ExitStack
import math

import numpy as np
import concourse.bass as bass
from concourse import mybir

F32 = mybir.dt.float32
F32R = mybir.dt.float32r
I32 = mybir.dt.int32
U32 = mybir.dt.uint32
ALU = mybir.AluOpType
ACT = mybir.ActivationFunctionType
AX = mybir.AxisListType

P = 128
D = 1024
KD = D // P
NB = 4
NLAT = 2
HEADS = 4
HD = 64
DA = 512
SG = 512
IN = 2560
FF = 2816
NE = 8
DE = 3584
EPS = 1e-6
SCALE = HD ** -0.5

UW = 1024
RAW = 8
RAW_E = 12
ADA_SEQ = ([(0, p, h) for p in range(6) for h in range(2)] + [(1, p, h) for p in (0, 1, 3, 4) for h in range(2)]
           + [(1, p, h) for p in (2, 5) for h in range(2)])
ADA_L1 = 18
CAT = (4, 5, 6, 7, 0, 1, 2, 3)
IN_ORDER = (4, 3, 0, 1, 2)
SPL = 4
AHEAD = SPL - 1
ATS = 6
STEPS = DE // 512
SLOT_STEP = 4
SLOT_BANK = 4
UE = 12 * STEPS

C_ID, C_TRIU, C_ONES, C_IOTA, C_SELB, C_SELC, C_COS, C_SIN = 0, 128, 256, 384, 512, 768, 770, 898
C_END = 1026


def constants():
    c = np.zeros((P, C_END), np.float32)
    c[:, C_ID:C_ID + P] = np.eye(P)
    c[:, C_TRIU:C_TRIU + P] = np.triu(np.ones((P, P)))
    c[:, C_ONES:C_ONES + P] = 1
    c[:, C_IOTA:C_IOTA + P] = np.arange(P)
    for q in range(4):
        for r in range(2):
            c[32 * q + r, C_SELB + P * r:C_SELB + P * (r + 1)] = 1
            c[32 * q + r, C_SELC + r] = 1
    half = HD // 2
    inv = (np.float32(10000.0) ** (-np.arange(0, half, 2, dtype=np.float32) / np.float32(half))).astype(np.float32)
    tok = np.arange(NLAT * P)
    row, col = (tok // HD).astype(np.float32), (tok % HD).astype(np.float32)
    ar, ac = row[:, None] * inv, col[:, None] * inv
    ang = np.concatenate([ar, ar, ac, ac], -1)
    sgn = np.concatenate([-np.ones(16), np.ones(16)] * 2).astype(np.float32)
    cos, sin = np.cos(ang).astype(np.float32), np.sin(ang).astype(np.float32) * sgn
    c[:, C_COS:C_COS + 128] = cos.reshape(NLAT, P, HD).transpose(1, 0, 2).reshape(P, 128)
    c[:, C_SIN:C_SIN + 128] = sin.reshape(NLAT, P, HD).transpose(1, 0, 2).reshape(P, 128)
    return c


class Unit:

    def __init__(self, k, s, a, src, split, shape):
        self.k, self.s, self.a, self.src, self.split, self.shape = k, s, a, src, split, shape


def plan_units(ada_w, w_in, w_out, w1, w3, w2):
    units, at = [], {}
    n = dict(s=0, a=0)

    def add(key, src, split, shape):
        u = Unit(len(units), n["s"] if split else None, None if split else n["a"], src, split, shape)
        n["s" if split else "a"] += 1
        units.append(u)
        at.setdefault(key, []).append(u)

    def tall(w, k0, nk, c0, nc_):
        return w[k0 * P:(k0 + nk) * P, c0:c0 + nc_].rearrange("(k p) n -> p k n", p=P)

    def ada(n0, n1):
        for n in range(n0, n1):
            l, part, half = ADA_SEQ[n]
            for u in range(4):
                add(("ada", n), tall(ada_w[l], 2 * u, 2, D * part + 512 * half, 512), False, (2, 512))

    ada(0, 4)
    for l in range(2):
        for j in IN_ORDER:
            for u in range(4):
                add(("in", l, j), tall(w_in[l], 2 * u, 2, 512 * j, 512), True, (2, 512))
        ada(*((4, ADA_L1) if l == 0 else (ADA_L1, 24)))
        for n2 in range(2):
            for u in range(4):
                add(("out", l, n2), tall(w_out[l], CAT[2 * u], 2, 512 * n2, 512), True, (2, 512))
        if l == 0:
            for g, c0 in enumerate(range(0, 22, 4)):
                gc = min(4, 22 - c0)
                for c in range(c0, c0 + gc, 2):
                    for key, w in (("w1", w1), ("w3", w3)):
                        for h in range(2):
                            add((key, c), tall(w[0], 4 * h, 4, P * c, 2 * P), True, (4, 256))
                for n2 in range(2):
                    for c in range(c0, c0 + gc, 2):
                        add(("w2", g, n2), tall(w2[0], c, 2, 512 * n2, 512), True, (2, 512))
    return units, at, n["s"]


def program(nc, x, c, ctx, c_ctx, ada_w, ada_b, pre_mix_g, post_mix_g, pre_ffn_g, post_ffn_g, w_in, w_out,
            lam_q1, lam_k1, lam_q2, lam_k2, subln_g, sg_ln_g, sg_ln_b, sg_w, sg_b, ffn_w1, ffn_w3, ffn_w2,
            router_w, moe_w1, moe_w3, moe_w2, const, out):
    units, at, NS0 = plan_units(ada_w, w_in, w_out, ffn_w1, ffn_w3, ffn_w2)
    K0 = len(units)
    split_units = [u for u in units if u.split]

    with ExitStack() as stack:
        def sem(name):
            return stack.enter_context(nc.semaphore(name))

        end = [16512]

        def place(name, shape, dt, offset=None):
            size = 4 * int(np.prod(shape[1:]))
            if offset is None:
                offset = end[0]
                end[0] += -(-size // 32) * 32
            return nc.alloc_sbuf_tensor_at(name, shape, dt, offset=offset)

        raw = place("raw", [P, RAW, UW], F32)
        w_hi = place("w_hi", [P, SPL, UW], F32R)
        w_lo = place("w_lo", [P, SPL, UW], F32R)
        xs = place("xs", [P, NB, D], F32)
        H = end[0]
        hT_hi = place("hT_hi", [P, KD, 512], F32R)
        hT_lo = place("hT_lo", [P, KD, 512], F32R)
        cst = place("cst", [P, C_END], F32)
        pcol = place("pcol", [P, 2, 68], F32)
        cstat = place("cstat", [P, KD, 32], F32)
        mod_a = place("mod_a", [P, 2, 2, KD, 2], F32)
        mod_b = place("mod_b", [P, 2, 2, KD, 2], F32)
        sub_bc = place("sub_bc", [P, 2, P], F32)
        lng_bc = place("lng_bc", [P, 2, SG], F32)
        lnb_bc = place("lnb_bc", [P, 2, SG], F32)
        lam_s = place("lam_s", [P, 2, 8], F32)
        rs = place("rs", [P, 128], F32)
        idx = place("idx", [P, NLAT, 8], U32)
        st = place("st", [P, 64], F32)
        st2 = place("st2", [P, 128], F32)
        att = place("att", [P, 2, 8], F32)
        flag = place("flag", [P, 1], I32)
        ab_bc = place("ab_bc", [P, 512], F32)
        pg_bc = place("pg_bc", [P, 512], F32)
        arow = place("arow", [P, 512], F32)
        wsT = place("wsT", [P, SG], F32)
        gg = place("gg", [P, 4, D], F32)
        G1 = end[0] - 4 * 4 * D
        Z = end[0]
        proj = place("proj", [P, NB, IN], F32, Z)
        xn = place("xn", [P, NB, D], F32, Z)
        hT32 = place("hT32", [P, KD, 512], F32, Z + 16384)
        qT = place("qT", [P, HEADS, 512], F32, H + 16384)
        kT = place("kT", [P, HEADS, 512], F32, H + 24576)
        pr = place("pr", [P, 2, 2, 512], F32, Z + 40960)
        wT = place("wT", [P, 2, 512], F32, Z + 49152)
        rtmp = place("rtmp", [P, D], F32, Z + 40960)
        ws_raw = place("ws_raw", [P, SG], F32, Z + 53248)
        osq = place("osq", [P, P], F32, Z + 55296)
        rows = place("rows", [68, 2, P], F32, Z + 32768)
        crow = place("crow", [16, P], F32, Z + 33792)
        lam_bc = place("lam_bc", [P, 2, 4, HD], F32, Z + 45056)
        lam_t = place("lam_t", [P, 2, 2, HD], F32, Z + 47104)
        zmix = place("zmix", [P, NB, D], F32, Z + 16384)
        y0 = place("y0", [P, NB, D], F32, Z)
        at_hi = place("at_hi", [P, ATS, 512], F32R, Z + 16384)
        at_lo = place("at_lo", [P, ATS, 512], F32R, Z + 28672)
        ptmp = place("ptmp", [P, D], F32, Z + 32768)
        sgf = place("sgf", [P, 2, 512], F32, Z + 45056)
        a32 = place("a32", [P, 2, 512], F32, Z + 49152)
        xg_hi = place("xg_hi", [P, NLAT, D], F32R, H)
        xg_lo = place("xg_lo", [P, NLAT, D], F32R, H + 8192)
        he_hi = place("he_hi", [P, KD, P], F32R, H + 16384)
        he_lo = place("he_lo", [P, KD, P], F32R, H + 20480)
        he32 = place("he32", [P, KD, P], F32, H + 24576)
        rw = place("rw", [P, KD, NE], F32, H + 28672)
        yg = place("yg", [P, D], F32, Z)
        yh = place("yh", [P, D], F32R, Z + 4096)
        yl = place("yl", [P, D], F32R, Z + 8192)
        ident_r = place("ident_r", [P, P], F32R, Z + 13312)
        scat_now = place("scat_now", [P, NLAT * P], F32R, Z + 12288)
        Z2 = Z + 14336
        perm = place("perm", [P, NE + 1, NLAT, P], F32R, Z2)
        scat = place("scat", [P, NE, NLAT * P], F32, Z2 + 9216)
        ae_hi = place("ae_hi", [P, 2, 512], F32R, G1 + 8192)
        sge = place("sge", [P, 2, 512], F32, Z2 + 17408)
        ae32 = place("ae32", [P, 2, 512], F32, Z2 + 21504)
        ae_lo = place("ae_lo", [P, 2, 512], F32R, G1 + 12288)
        junk = place("junk", [P, D], F32, Z + 4096)
        raw_more = place("raw_more", [P, RAW_E - RAW, UW], F32, Z2 + 25600)
        assert Z2 + 41984 <= nc.sbuf_usable_end
        assert UE % RAW_E == 0
        yout = xs[:, 2:4, :]
        ps = stack.enter_context(nc.psum_tensor("ps", [P, 8, 512], F32))

        ident = cst[:, C_ID:C_ID + P]
        ones = cst[:, C_ONES:C_ONES + P]
        triu = cst[:, C_TRIU:C_TRIU + P]
        iota = cst[:, C_IOTA:C_IOTA + P]

        raw_in = [sem(f"raw_in{i}") for i in range(RAW_E)]
        hi_done, lo_done = sem("hi_done"), sem("lo_done")
        unit_used, ada_used = sem("unit_used"), sem("ada_used")
        s_small, s_x, s_bc, s_out = sem("s_small"), sem("s_x"), sem("s_bc"), sem("s_out")
        dve_ch, act_ch = sem("dve_ch"), sem("act_ch")
        S = {}

        def sg(name):
            if name not in S:
                S[name] = sem(name.replace(" ", "_"))
            return S[name]

        def view(ring, u):
            return ring.rearrange("p (k n) -> p k n", k=u.shape[0])

        def raw_at(k):
            return raw[:, k % RAW, :]

        def raw_count(k):
            return 16 * (k // RAW + 1)

        def expert_raw(i):
            i = i % RAW_E
            return raw_more[:, i, :] if i < RAW_E - RAW else raw_at(K0 + i - (RAW_E - RAW))

        def expert_in(i):
            j = i % RAW_E
            if j < RAW_E - RAW:
                return raw_in[RAW + j], 16 * (i // RAW_E + 1)
            k = K0 + j - (RAW_E - RAW)
            return raw_in[k % RAW], 16 * (k // RAW + 1 + i // RAW_E)

        block = stack.enter_context(nc.Block())

        def in_blocks(l, j):
            return range(NB) if l == 0 or j in (1, 2) else range(NLAT)

        def out_blocks(l):
            return range(NB) if l == 0 else range(NLAT)

        items = {l: [(b, h) for b in out_blocks(l) for h in range(HEADS)] for l in range(2)}
        qk = {l: [(t, b) for b in range(NB) for t in ((0, 1) if l == 0 or b < NLAT else (1,))] for l in range(2)}
        proj_n = {l: [sum(len(in_blocks(l, i)) for i in IN_ORDER[:j + 1]) for j in range(5)] for l in range(2)}
        in_end = [at["in", l, IN_ORDER[-1]][-1].s for l in range(2)] + [NS0 - 1]
        first_units = {"mix0": at["in", 0, IN_ORDER[0]][0].s, "ffn0": at["w1", 0][0].s, "mix1": at["in", 1, IN_ORDER[0]][0].s}
        groups = [(c0, min(4, 22 - c0)) for c0 in range(0, 22, 4)]

        def expert_units():
            seq = []
            for s in range(STEPS):
                seq += [(0, s, n) for n in range(4)] + [(1, s, n) for n in range(4)]
                if s:
                    seq += [(2, s - 1, 4 * (s - 1) + n) for n in range(4)]
            return seq + [(2, STEPS - 1, 4 * (STEPS - 1) + n) for n in range(4)]

        def end_w1(s):
            return 3 if s == 0 else 12 * s - 1

        def end_w3(s):
            return end_w1(s) + 4

        def end_w2(s):
            return end_w3(s + 1) + 4 if s + 1 < STEPS else UE - 1

        def spread(t, c0, c1, steps):
            c = c0 + -(-t * (c1 - c0) // steps)
            return c if 0 <= t < steps and -(-(t + 1) * (c1 - c0) // steps) > c - c0 else None

        def ada_slot(l, t):
            if l == 0:
                return spread(t, 4, ADA_L1, NB * HEADS)
            return spread(t, ADA_L1, 24, NLAT * HEADS)

        ADA = 6
        gate_chunks = [c for c in range(24) if ADA_SEQ[c][1] in (2, 5)]

        def last_gate(c):
            return gate_chunks[gate_chunks.index(c) - 1]

        def gate_at(l, which, r):
            return 2 * which + r if l == 0 else which

        def two_gates(c):
            return ADA_SEQ[c][1] in (2, 5) and len(streams(ADA_SEQ[c][0])) == 2

        def streams(l):
            return (0, 1) if l == 0 else (0,)

        NSMALL = 16 * 11

        small = [(cst[:, :], const), (crow[0:8, :], c.rearrange("a (k p) -> (a k) p", p=P)),
                 (crow[8:16, :], c_ctx.rearrange("(k p) -> k p", p=P))]
        for l in range(2):
            small += [(rows[0:48, l, :], ada_b[l].rearrange("(k p) -> k p", p=P)),
                      (rows[48:56, l, :], pre_mix_g[l].rearrange("(k p) -> k p", p=P)),
                      (rows[56:64, l, :], pre_ffn_g[l].rearrange("(k p) -> k p", p=P)),
                      (rows[64:68, l, :], sg_b[l])]

        @block.sync
        def _(sp):
            for dst, src in small:
                sp.dma_start(dst, src).then_inc(s_small, 16)
            xv = x.rearrange("a (b p) d -> p (a b) d", p=P)
            cv = ctx.rearrange("a (b p) d -> p (a b) d", p=P)
            for u in units:
                if u.k == 4:
                    for b in range(NB):
                        sp.dma_start(xs[:, b, :], xv[:, b, :] if b < NLAT else cv[:, b - NLAT, :]).then_inc(s_x, 16)
                if u.k >= RAW:
                    o = units[u.k - RAW]
                    sp.wait_ge(*((lo_done, o.s + 1) if o.split else (ada_used, o.a + 1)))
                sp.dma_start(view(raw_at(u.k), u), u.src).then_inc(raw_in[u.k % RAW], 16)

            def experts(turn):
                base = turn * NE * UE
                with sp.Fori(0, NE) as e:
                    for i, (w, s, n) in enumerate(expert_units()):
                        sp.wait_ge(lo_done, e * UE + (NS0 + base + i - RAW_E + 1))
                        if w == 2:
                            src, dst = moe_w2[0][e][n * P:(n + 1) * P, :], expert_raw(i)
                        else:
                            wt = moe_w1 if w == 0 else moe_w3
                            src = wt[0][e][2 * n * P:2 * (n + 1) * P, 512 * s:512 * s + 512].rearrange("(k p) n -> p k n", p=P)
                            dst = expert_raw(i).rearrange("p (k n) -> p k n", k=2)
                        sp.dma_start(dst, src).then_inc(expert_in(i)[0], 16)

            sp.wait_ge(sg("cat1"), HEADS * NLAT)
            experts(0)
            sp.wait_ge(sg("flag set"), 1)
            busiest = sp.value_load(flag[0:1, 0:1], min_val=0, max_val=NLAT * P)
            with sp.If(busiest > P):
                experts(1)
            for b in range(NLAT):
                sp.wait_ge(sg("final x"), b + 1)
                sp.dma_start(out.rearrange("a (b p) d -> p (a b) d", p=P)[:, b, :], xs[:, b, :]).then_inc(s_out, 16)
            sp.wait_ge(s_out, 16 * NLAT)

        @block.gpsimd
        def _(pool):
            pool.wait_ge(ada_used, 4)
            for l in range(2):
                for i, v in enumerate((lam_q1, lam_k1, lam_q2, lam_k2)):
                    pool.dma_start(lam_bc[:, l, i, :], v[l].partition_broadcast(P)).then_inc(sg("params in"), 16)
                pool.dma_start(sub_bc[:, l, :], subln_g[l].partition_broadcast(P)).then_inc(sg("params in"), 16)
                pool.dma_start(lng_bc[:, l, :], sg_ln_g[l].partition_broadcast(P)).then_inc(sg("params in"), 16)
                pool.dma_start(lnb_bc[:, l, :], sg_ln_b[l].partition_broadcast(P)).then_inc(sg("params in"), 16)
            for l in range(2):
                if l:
                    pool.wait_ge(sg("wsT ps"), l)
                pool.dma_start(ws_raw[:, :].rearrange("p (g q) -> p g q", g=4), sg_w[l].rearrange("g p q -> p g q")).then_inc(sg("ws in"), 16)
                for c in gate_chunks:
                    ll, part, half = ADA_SEQ[c]
                    if ll == l:
                        if c != gate_chunks[0]:
                            pool.wait_ge(sg("ada fin"), last_gate(c) + 1)
                        o = part * D + 512 * half
                        gain = (post_mix_g, post_ffn_g)[part // 3]
                        pool.dma_start(ab_bc[:, :], ada_b[ll][o:o + 512].partition_broadcast(P)).then_inc(s_bc, 16)
                        pool.dma_start(pg_bc[:, :], gain[ll][512 * half:512 * half + 512].partition_broadcast(P)).then_inc(s_bc, 16)
            pool.wait_ge(unit_used, NS0)
            pool.dma_start(rw[:, :, :], router_w[0].rearrange("(k p) e -> p k e", p=P)).then_inc(sg("rw in"), 16)

        @block.tensor
        def _(pe):
            def mm3(o, lh, ll, rh, rl, start, stop):
                pe.matmul(o, lh, rh, start=start, stop=False)
                pe.matmul(o, lh, rl, start=False, stop=False)
                return pe.matmul(o, ll, rh, start=False, stop=stop)

            def split_at(s):
                return w_hi[:, s % SPL, :], w_lo[:, s % SPL, :]

            pe.wait_ge(s_small, NSMALL)
            pe.transpose(ps[:, 0, 0:16], crow[:, :], ident[0:16, 0:16]).then_inc(sg("small T"), 1)
            for l in range(2):
                pe.transpose(ps[:, 1 + l, 0:68], rows[:, l, :], ident[0:68, 0:68]).then_inc(sg("small T"), 1)

            def ada_rows(c, bank, which=range(4)):
                if c and which[0] == 0:
                    if two_gates(c - 1):
                        pe.wait_ge(sg("ada fin"), c)
                    else:
                        pe.wait_ge(sg("arow"), c)
                for u in [at["ada", c][i] for i in which]:
                    pe.wait_ge(raw_in[u.k % RAW], raw_count(u.k))
                    w = view(raw_at(u.k), u)
                    for kk in range(2):
                        k = 2 * (u.a % 4) + kk
                        q = k % 4
                        m = pe.matmul(ps[32 * q:32 * q + 32, bank, :], cstat[:, k, :], w[:, kk, :],
                                      start=(k < 4), stop=(k >= 4), tile_position=(0, 32 * q))
                    m.then_inc(ada_used, 1)

            def ada_turn(c, bank):
                pe.wait_ge(sg("arow"), c + 1)
                if c:
                    pe.wait_ge(sg("ada fin"), c)
                if ADA_SEQ[c][1] in (2, 5):
                    for r in streams(ADA_SEQ[c][0]):
                        m = pe.matmul(ps[:, bank + 1 - r, :], cst[:, C_SELB + P * r:C_SELB + P * r + P], arow[:, :],
                                      start=True, stop=True)
                else:
                    for j in range(4):
                        m = pe.matmul(ps[:, bank + 1, 2 * j:2 * j + 2], arow[:, P * j:P * j + P], cst[:, C_SELC:C_SELC + 2],
                                      start=True, stop=True)
                m.then_inc(sg("ada post"), 1)

            def turn_h(key, nb, ks=range(KD)):
                for b in range(nb):
                    pe.wait_ge(sg("xn " + key), b + 1)
                    for k in ks:
                        m = pe.transpose(ps[:, k, P * b:P * b + P], xn[:, b, P * k:P * k + P], ident)
                        if b == nb - 1:
                            m.then_inc(sg("hT ps " + key), 1)

            def project_in(l):
                pe.wait_ge(sg("ada fin"), 4 if l == 0 else 16)
                for jn, j in enumerate(IN_ORDER):
                    if jn >= 2:
                        pe.wait_ge(sg("proj%d" % l), proj_n[l][jn - 2])
                    for i, u in enumerate(at["in", l, j]):
                        pe.wait_ge(lo_done, u.s + 1)
                        h, lo = (view(t, u) for t in split_at(u.s))
                        if jn == 0:
                            pe.wait_ge(sg("hT mix%d" % l), max(2 * i + 2, 4))
                        for kk in range(2):
                            k = 2 * i + kk
                            for b in in_blocks(l, j):
                                m = mm3(ps[:, 4 * (jn % 2) + b, :], hT_hi[:, k, P * b:P * b + P], hT_lo[:, k, P * b:P * b + P],
                                        h[:, kk, :], lo[:, kk, :], k == 0, k == KD - 1)
                        m.then_inc(unit_used, 1)

            def turn_qk(l):
                pe.wait_ge(sg("rope%d" % l), 2 * NLAT)
                for i, (t, b) in enumerate(qk[l]):
                    if i >= 2:
                        pe.wait_ge(sg("qkT%d" % l), i - 1)
                    src = proj[:, b, :]
                    for h in range(HEADS):
                        m = pe.transpose(ps[:, i % 2, P * h:P * h + P], src[:, t * DA + P * h:t * DA + P * h + P], ident)
                    m.then_inc(sg("qk ps%d" % l), 1)

            def spatial(l):
                pe.wait_ge(sg("proj%d" % l), proj_n[l][4])
                pe.wait_ge(sg("ws in"), 16 * (l + 1))
                for g in range(4):
                    m = pe.transpose(ps[:, 2, P * g:P * g + P], ws_raw[:, P * g:P * g + P], ident)
                m.then_inc(sg("wsT ps"), 1)
                pe.wait_ge(sg("wsT"), l + 1)
                for b in out_blocks(l):
                    pe.wait_ge(sg("vn%d" % l), b + 1)
                    for g in range(4):
                        m = pe.matmul(ps[:, 4 + b, P * g:P * g + P], wsT[:, P * g:P * g + P],
                                      proj[:, b, 4 * DA + P * g:4 * DA + P * g + P], start=True, stop=True)
                    m.then_inc(sg("mixed"), 1)

            def attend(l):
                its = items[l]
                n = len(its)
                pe.wait_ge(sg("qkT%d" % l), len(qk[l]))
                pe.wait_ge(sg("gated"), NB * l + len(out_blocks(l)))
                for t in range(n + 2):
                    if t < n:
                        b, h = its[t]
                        k0 = 0 if b < NLAT else 256
                        if t >= 2:
                            pe.wait_ge(sg("exp%d" % l), 2 * (t - 1))
                        for m_ in range(2):
                            m = pe.matmul(ps[:, 2 * (t % 2) + m_, 0:512 - k0], qT[HD * m_:HD * m_ + HD, h, P * b:P * b + P],
                                          kT[HD * m_:HD * m_ + HD, h, k0:512], start=True, stop=True)
                        m.then_inc(sg("scores%d" % l), 1)
                    if ada_slot(l, t - 1):
                        ada_turn(ada_slot(l, t - 1), ADA)
                    if t >= 2:
                        i = t - 2
                        b, h = its[i]
                        kb0, nk = (0, 4) if b < NLAT else (2, 2)
                        pe.wait_ge(sg("wT%d" % l), i + 1)
                        if i:
                            pe.wait_ge(sg("o%d" % l), i)
                        for kb in range(nk):
                            m = pe.matmul(ps[:, 5, 0:P], wT[:, i % 2, P * kb:P * kb + P],
                                          proj[:, kb0 + kb, 2 * DA + P * h:2 * DA + P * h + P], start=(kb == 0), stop=(kb == nk - 1))
                        m.then_inc(sg("pv%d" % l), 1)
                    if ada_slot(l, t):
                        ada_rows(ada_slot(l, t), ADA, (0, 1))
                    if 1 <= t <= n:
                        i = t - 1
                        b, h = its[i]
                        nk = 4 if b < NLAT else 2
                        pe.wait_ge(sg("weights%d" % l), i + 1)
                        if i:
                            pe.wait_ge(sg("wT%d" % l), i)
                        for kb in range(nk):
                            m = pe.transpose(ps[:, 4, P * kb:P * kb + P], pr[:, i % 2, 0, P * kb:P * kb + P], ident)
                        m.then_inc(sg("wT ps%d" % l), 1)
                    if ada_slot(l, t):
                        ada_rows(ada_slot(l, t), ADA, (2, 3))

            def turn_cat(l, js):
                nb = len(out_blocks(l))
                for j in js:
                    k = CAT[j]
                    if j == 0:
                        pe.wait_ge(sg("exp%d" % l), 2 * len(items[l]))
                    if j == 2:
                        pe.wait_ge(sg("o%d" % l), len(items[l]))
                    if j == 3:
                        pe.wait_ge(sg("ada fin"), ADA_L1 if l == 0 else 24)
                    if k == 0:
                        pe.wait_ge(sg("cat%d" % l), nb * HEADS)
                    if j >= 4:
                        pe.wait_ge(sg("catT"), KD * l + j - 3)
                    for b in range(nb):
                        col = P * k if k < 4 else 3 * DA + P * (k - 4)
                        m = pe.transpose(ps[:, 1 + 2 * (j % 4), P * b:P * b + P], proj[:, b, col:col + P], ident)
                    m.then_inc(sg("catT ps"), 1)

            def project_out(l):
                def part(n2, i, u, b):
                    h, lo = (view(t, u) for t in split_at(u.s))
                    for kk in range(2):
                        j = 2 * i + kk
                        k = CAT[j]
                        m = mm3(ps[:, 2 * b + n2, :], hT_hi[:, k, P * b:P * b + P], hT_lo[:, k, P * b:P * b + P],
                                h[:, kk, :], lo[:, kk, :], j == 0, j == KD - 1)
                    return m

                for i, u in enumerate(at["out", l, 0]):
                    if i % 2 == 0:
                        turn_cat(l, range(2 * i, 2 * i + 4))
                    pe.wait_ge(lo_done, u.s + 1)
                    pe.wait_ge(sg("catT"), KD * l + 2 * i + 2)
                    for b in out_blocks(l):
                        m = part(0, i, u, b)
                    m.then_inc(unit_used, 1)
                us = at["out", l, 1]
                assert len(us) == SPL
                for b in out_blocks(l):
                    for i, u in enumerate(us):
                        if b == 0:
                            pe.wait_ge(lo_done, u.s + 1)
                        m = part(1, i, u, b)
                        if b == out_blocks(l)[-1]:
                            m.then_inc(unit_used, 1)
                    if b < out_blocks(l)[-1]:
                        m.then_inc(sg("out"), 1)
                pe.wait_ge(sg("z pm%d" % l), 2 * len(out_blocks(l)))

            def ffn():
                for g, (c0, gc) in enumerate(groups):
                    for c in range(c0, c0 + gc, 2):
                        for wi, key in enumerate(("w1", "w3")):
                            if c >= 2:
                                pe.wait_ge(sg(("silu", "gated up")[wi]), c)
                            for i, u in enumerate(at[key, c]):
                                pe.wait_ge(lo_done, u.s + 1)
                                h, lo = (view(t, u) for t in split_at(u.s))
                                if c + wi == 0:
                                    pe.wait_ge(sg("hT ffn0"), 4 * i + 4)
                                for ci in range(2):
                                    for kk in range(4):
                                        k = 4 * i + kk
                                        m = mm3(ps[:, 2 * wi + ci, :], h[:, kk, P * ci:P * ci + P], lo[:, kk, P * ci:P * ci + P],
                                                hT_hi[:, k, :], hT_lo[:, k, :], k == 0, k == KD - 1)
                                m.then_inc(unit_used, 1)
                    for n2 in range(2):
                        us = at["w2", g, n2]
                        for i, u in enumerate(us):
                            pe.wait_ge(lo_done, u.s + 1)
                            pe.wait_ge(sg("AT"), c0 + 2 * i + 2)
                            h, lo = (view(t, u) for t in split_at(u.s))
                            for b in range(NB):
                                if i == 0 and 2 * g + n2 > 0:
                                    pe.wait_ge(sg("y sum"), NB * (2 * g + n2 - 1) + b + 1)
                                for kk in range(2):
                                    a = (c0 + 2 * i + kk) % ATS
                                    m = mm3(ps[:, 4 + b, :], at_hi[:, a, P * b:P * b + P], at_lo[:, a, P * b:P * b + P],
                                            h[:, kk, :], lo[:, kk, :], i == 0 and kk == 0, i == len(us) - 1 and kk == 1)
                                if i == len(us) - 1 and b < NB - 1:
                                    m.then_inc(sg("y part"), 1)
                            m.then_inc(unit_used, 1)

            def route():
                pe.wait_ge(sg("hT32 ffn1"), KD)
                pe.wait_ge(sg("rw in"), 16)
                for tb in range(NLAT):
                    for k in range(KD):
                        m = pe.matmul(ps[:, 0, NE * tb:NE * tb + NE], hT32[:, k, P * tb:P * tb + P], rw[:, k, :],
                                      start=(k == 0), stop=(k == KD - 1))
                m.then_inc(sg("logits"), 1)
                pe.wait_ge(sg("mask"), 1)
                mask = st2[:, 64:80]
                pe.matmul(ps[:, 1, 0:8], triu, mask[:, 0:8], start=True, stop=True)
                pe.matmul(ps[:, 1, 8:16], ones, mask[:, 0:8], start=True, stop=False)
                pe.matmul(ps[:, 1, 8:16], triu, mask[:, 8:16], start=False, stop=True)
                pe.matmul(ps[:, 1, 16:24], ones, mask[:, 0:8], start=True, stop=False)
                pe.matmul(ps[:, 1, 16:24], ones, mask[:, 8:16], start=False, stop=True).then_inc(sg("counts"), 1)

            def gather(e):
                for k in range(KD):
                    for tb in range(NLAT):
                        for part, src in enumerate((xg_hi, xg_lo)):
                            m = pe.matmul(ps[:, 2 + k // 4, P * (k % 4):P * (k % 4) + P], src[:, tb, P * k:P * k + P],
                                          perm[:, e, tb, :], start=(tb + part == 0), stop=(tb + part == 2))
                    if k % 4 == 3:
                        m.then_inc(sg("gathered"), 1)

            def slots(turn):
                pe.wait_ge(sg("perm"), NE * (turn + 1))
                pe.wait_ge(sg("gates"), 1)
                pe.wait_ge(sg("ident r"), 1)
                for e in range(NE):
                    for tb in range(NLAT):
                        m = pe.matmul(ps[:, SLOT_BANK, e:e + 1], perm[:, e, tb, :].bitcast(F32), st2[:, 80 + 8 * tb + e:81 + 8 * tb + e],
                                      start=(tb == 0), stop=(tb == 1))
                m.then_inc(sg("slot gates"), 1)
                pe.wait_ge(sg("slot gate"), turn + 1)
                for e in range(NE):
                    if e >= 2:
                        pe.wait_ge(sg("scat"), NE * turn + e - 1)
                    for tb in range(NLAT):
                        m = pe.matmul(ps[:, 4 + e % 2, P * tb:P * tb + P], perm[:, e, tb, :], ident_r[:, :], start=True, stop=True)
                    m.then_inc(sg("scat ps"), 1)
                pe.wait_ge(sg("scat"), NE * (turn + 1))

            def scatter(count):
                pe.wait_ge(sg("y split"), count)
                for tb in range(NLAT):
                    for n2 in range(2):
                        for part, src in enumerate((yh, yl)):
                            m = pe.matmul(ps[:, 4 + 2 * tb + n2, :], scat_now[:, P * tb:P * tb + P], src[:, 512 * n2:512 * n2 + 512],
                                          start=(part == 0), stop=(part == 1))
                m.then_inc(sg("scattered"), 1)

            def experts(turn):
                base = NS0 + turn * NE * UE
                pe.wait_ge(sg("perm"), NE * turn + 1)
                gather(0)

                def expert(e, first):
                    def took(s):
                        return e * UE + (base + s + 1)

                    def up(s, w):
                        for n in range(4):
                            i = (end_w1, end_w3)[w](s) - 3 + n
                            pe.wait_ge(lo_done, took(i))
                            if s + w == 0 and n % 2 == 0:
                                pe.wait_ge(sg("he"), e * 2 + (2 * (NE + 1) * turn + 1 + n // 2))
                            for kk in range(2):
                                k = 2 * n + kk
                                r = [t[:, (base + i) % SPL, 512 * kk:512 * kk + 512] for t in (w_hi, w_lo)]
                                m = mm3(ps[:, 2 * (s % 2) + w, :], he_hi[:, k, :], he_lo[:, k, :], *r, k == 0, k == KD - 1)
                            m.then_inc(unit_used, 1)

                    def turn_a(s):
                        pe.wait_ge(sg("ae32"), e * STEPS + (STEPS * NE * turn + s + 1))
                        for j in range(4):
                            m = pe.transpose(ps[:, 4 + s % 2, P * j:P * j + P], ae32[:, s % 2, P * j:P * j + P], ident)
                        m.then_inc(sg("ae ps"), 1)

                    def down(s):
                        pe.wait_ge(sg("ae"), e * STEPS + (STEPS * NE * turn + s + 1))
                        for n in range(4):
                            i = end_w2(s) - 3 + n
                            pe.wait_ge(lo_done, took(i))
                            for n2 in range(2):
                                r = [t[:, (base + i) % SPL, 512 * n2:512 * n2 + 512] for t in (w_hi, w_lo)]
                                m = mm3(ps[:, 6 + n2, :], ae_hi[:, s % 2, P * n:P * n + P], ae_lo[:, s % 2, P * n:P * n + P],
                                        *r, s == 0 and n == 0, s == STEPS - 1 and n == 3)
                            m.then_inc(unit_used, 1)

                    for s in range(STEPS):
                        up(s, 0)
                        if s == 1 and not first:
                            pe.wait_ge(sg("yout"), e + (NE * turn + 1))
                        if s:
                            turn_a(s - 1)
                        up(s, 1)
                        if s == 0 and not first:
                            scatter(e + NE * turn)
                        if s:
                            down(s - 1)
                        if s == SLOT_STEP and first:
                            slots(turn)
                    turn_a(STEPS - 1)
                    gather(e + 1)
                    down(STEPS - 1)

                expert(0, True)
                if turn == 0:
                    pe.wait_ge(sg("flag set"), 1)
                    busiest.append(pe.value_load(flag[0:1, 0:1], min_val=0, max_val=NLAT * P))
                with pe.Fori(1, NE) as e:
                    expert(e, False)
                scatter(NE * (turn + 1))
                pe.wait_ge(sg("yout"), NE * (turn + 1) + 1)

            pe.wait_ge(sg("cstat"), 1 + 2 * KD)
            pe.wait_ge(sg("pcol"), 2)
            for c in range(4):
                if c == 3:
                    turn_h("mix0", NB, range(6))
                ada_rows(c, ADA)
                ada_turn(c, ADA)
            pe.wait_ge(sg("ada fin"), 4)
            turn_h("mix0", NB, range(6, KD))
            for l in range(2):
                if l:
                    turn_h("mix1", NB)
                project_in(l)
                spatial(l)
                turn_qk(l)
                attend(l)
                project_out(l)
                turn_h("ffn%d" % l, len(out_blocks(l)))
                if l == 0:
                    ffn()
            route()
            busiest = []
            experts(0)
            with pe.If(busiest[0] > P):
                experts(1)

        @block.scalar
        def _(act):
            cur = [0]
            chain = [0]
            stage_end = [in_end[0]]

            def link(ins):
                chain[0] += 1
                ins.then_inc(act_ch, 1)
                act.wait_ge(act_ch, chain[0])

            def split_upto(s):
                s = min(s, stage_end[0])
                while cur[0] <= s:
                    u = split_units[cur[0]]
                    act.wait_ge(raw_in[u.k % RAW], raw_count(u.k))
                    if u.s >= SPL:
                        act.wait_ge(unit_used, u.s - SPL + 1)
                    act.activation(w_hi[:, u.s % SPL, :], raw_at(u.k), ACT.Copy).then_inc(hi_done, 1)
                    cur[0] += 1

            def last_s(key):
                return at[key][-1].s

            act.wait_ge(sg("cstat"), 1)
            act.wait_ge(sg("small T"), 3)
            for r in range(2):
                for k in range(KD):
                    act.activation(cstat[:, k, r:r + 1], ps[:, 0, KD * r + k:KD * r + k + 1], ACT.Silu).then_inc(sg("cstat"), 1)


            def pre_square(key, l, which, b):
                if key == "mix0":
                    act.wait_ge(s_x, 16 * NB)
                else:
                    act.wait_ge(sg("x ffn" if which == 0 else "x mix%d" % l), b + 1)
                act.activation(xn[:, b, :], xs[:, b, :], ACT.Square, accum_out=st[:, b:b + 1]).then_inc(sg("ss " + key), 1)

            def pre_root(key, b):
                act.wait_ge(sg("ms " + key), b + 1)
                act.activation(st[:, 8 + b:9 + b], st[:, 4 + b:5 + b], ACT.Sqrt).then_inc(sg("rt " + key), 1)

            def prenorm(key, l, which, nb):
                for t in range(nb + 1):
                    if t < nb:
                        pre_square(key, l, which, t)
                    if t:
                        pre_root(key, t - 1)
                modulate_h(key, l, which, nb)

            def modulate_h(key, l, which, nb):
                for k in range(KD):
                    if key == "mix0":
                        act.wait_ge(sg("ada fin"), 3 + k // 4)
                    elif k == 0:
                        act.wait_ge(sg("ada fin"), 20 if key == "ffn1" else 16)
                    act.wait_ge(sg("hT ps " + key), k + 1)
                    for r in range(nb // 2):
                        ins = act.activation(hT32[:, k, 256 * r:256 * r + 256], ps[:, k, 256 * r:256 * r + 256], ACT.Identity,
                                             bias=mod_b[:, l, which, k, r:r + 1], scale=mod_a[:, l, which, k, r:r + 1])
                    ins.then_inc(sg("hT32 " + key), 1)
                    if key in first_units:
                        split_first(key, k)

            def split_first(key, k):
                if k % 2 and (k > 4 or key != "mix0"):
                    split_upto(first_units[key] + (k // 2 - 2 if key == "mix0" else k // 2))

            def post_squares(key, half, srcs, junk_, ready):
                n = len(srcs)
                for b, src in enumerate(srcs):
                    ready(b)
                    if half * n + b:
                        act.wait_ge(sg("ss " + key), half * n + b)
                    act.activation(junk_, src, ACT.Square, accum_out=st[:, 16 + 4 * half + b:17 + 4 * half + b])\
                        .then_inc(sg("ss " + key), 1)
                if half:
                    act.wait_ge(sg("ms " + key), 1)
                    act.activation(st[:, 24:24 + n], st[:, 20:20 + n], ACT.Sqrt).then_inc(sg("rt " + key), 1)

            for l in range(2):
                nb = len(out_blocks(l))
                prenorm("mix%d" % l, l, 0, NB)
                for jn, j in enumerate(IN_ORDER):
                    split_upto(last_s(("in", l, j)) + AHEAD)
                    act.wait_ge(unit_used, last_s(("in", l, j)) + 1)
                    if jn == 0:
                        act.wait_ge(sg("hT mix%d" % l), KD)
                    for b in in_blocks(l, j):
                        act.activation(proj[:, b, 512 * j:512 * j + 512], ps[:, 4 * (jn % 2) + b, :], ACT.Copy)\
                            .then_inc(sg("proj%d" % l), 1)
                    if jn == 2:
                        act.wait_ge(sg("ln ms"), l + 1)
                        act.activation(st[:, 44:44 + nb], st[:, 40:40 + nb], ACT.Sqrt).then_inc(sg("ln rt"), 1)
                if l == 0:
                    act.wait_ge(sg("lam dots"), 1)
                    act.activation(lam_s[:, :, 2:4], lam_s[:, :, 0:2], ACT.Exp).then_inc(sg("lam exp"), 1)
                act.wait_ge(sg("wsT ps"), l + 1)
                act.activation(wsT[:, :], ps[:, 2, :], ACT.Copy).then_inc(sg("wsT"), 1)
                for i, (t, b) in enumerate(qk[l]):
                    act.wait_ge(sg("qk ps%d" % l), i + 1)
                    dst = (qT, kT)[t]
                    act.activation(dst[:, :, P * b:P * b + P], ps[:, i % 2, :].rearrange("p (h t) -> p h t", h=HEADS), ACT.Copy)\
                        .then_inc(sg("qkT%d" % l), 1)
                its = items[l]
                n = len(its)
                for t in range(n + 2):
                    if t < n:
                        nk = 512 if its[t][0] < NLAT else 256
                        act.wait_ge(sg("rowmax%d" % l), t + 1)
                        if t >= 2:
                            act.wait_ge(sg("wT ps%d" % l), t - 1)
                        for m_ in range(2):
                            act.activation(pr[:, t % 2, m_, 0:nk], ps[:, 2 * (t % 2) + m_, 0:nk], ACT.Exp, scale=SCALE,
                                           bias=att[:, t % 2, 2 + m_:3 + m_], accum_out=att[:, t % 2, 4 + m_:5 + m_])\
                                .then_inc(sg("exp%d" % l), 1)
                    if 1 <= t <= n:
                        i = t - 1
                        nk = 512 if its[i][0] < NLAT else 256
                        act.wait_ge(sg("wT ps%d" % l), i + 1)
                        if i >= 2:
                            act.wait_ge(sg("pv%d" % l), i - 1)
                        act.activation(wT[:, i % 2, 0:nk], ps[:, 4, 0:nk], ACT.Copy).then_inc(sg("wT%d" % l), 1)
                    if t >= 2:
                        i = t - 2
                        b, h = its[i]
                        act.wait_ge(sg("o%d" % l), i + 1)
                        if i:
                            act.wait_ge(sg("o sq%d" % l), i)
                        act.activation(osq[:, :], proj[:, b, P * h:P * h + P], ACT.Square,
                                       accum_out=st2[:, i:i + 1]).then_inc(sg("o sq%d" % l), 1)
                        if i % HEADS == HEADS - 1:
                            act.wait_ge(sg("o ms%d" % l), b + 1)
                            act.activation(st2[:, 32 + i - 3:33 + i], st2[:, 16 + i - 3:17 + i], ACT.Sqrt).then_inc(sg("o rt%d" % l), 1)
                stage_end[0] = in_end[l + 1]
                for j, k in enumerate(CAT):
                    if j % 2 == 0:
                        split_upto(at["out", l, 0][0].s + j // 2)
                    act.wait_ge(sg("catT ps"), KD * l + j + 1)
                    act.activation(hT_hi[:, k, 0:P * nb], ps[:, 1 + 2 * (j % 4), 0:P * nb], ACT.Copy).then_inc(sg("catT hi"), 1)
                split_upto(last_s(("out", l, 1)))
                post_squares("pm%d" % l, 0, [ps[:, 2 * b, :] for b in out_blocks(l)], ptmp[:, 0:512],
                             lambda b: act.wait_ge(unit_used, last_s(("out", l, 0)) + 1))
                for b in out_blocks(l):
                    if b == nb - 1:
                        act.wait_ge(unit_used, last_s(("out", l, 1)) + 1)
                    else:
                        act.wait_ge(sg("out"), (NB - 1) * l + b + 1)
                    act.wait_ge(sg("ss pm%d" % l), nb + b)
                    act.activation(ptmp[:, 0:512], ps[:, 2 * b + 1, :], ACT.Square, accum_out=st[:, 20 + b:21 + b])\
                        .then_inc(sg("ss pm%d" % l), 1)
                    act.wait_ge(sg("ms pm%d" % l), b + 1)
                    act.activation(st[:, 24 + b:25 + b], st[:, 20 + b:21 + b], ACT.Sqrt).then_inc(sg("rt pm%d" % l), 1)
                    pre_square("ffn%d" % l, l, 1, b)
                    pre_root("ffn%d" % l, b)
                modulate_h("ffn%d" % l, l, 1, nb)
                if l == 0:
                    for g, (c0, gc) in enumerate(groups):
                        for c in range(c0, c0 + gc, 2):
                            split_upto(last_s(("w1", c)) + AHEAD)
                            act.wait_ge(unit_used, last_s(("w1", c)) + 1)
                            if c >= 2:
                                act.wait_ge(sg("gated up"), c)
                            for ci in range(2):
                                act.activation(sgf[:, ci, :], ps[:, ci, :], ACT.Silu).then_inc(sg("silu"), 1)
                            split_upto(last_s(("w3", c)) + AHEAD)
                            for ci in range(2):
                                act.wait_ge(sg("gated up"), c + ci + 1)
                                act.activation(at_hi[:, (c + ci) % ATS, :], a32[:, ci, :], ACT.Copy).then_inc(sg("AT hi"), 1)
                        for n2 in range(2):
                            split_upto(last_s(("w2", g, n2)) + AHEAD)
                            if g == len(groups) - 1:
                                post_squares("pf0", n2, [y0[:, b, 512 * n2:512 * n2 + 512] for b in range(NB)], sgf[:, 0, :],
                                             lambda b: act.wait_ge(sg("y sum"), NB * (2 * g + n2) + b + 1))

            def scatters(turn):
                act.wait_ge(sg("slot gates"), turn + 1)
                act.activation(st2[:, 96:104], ps[:, SLOT_BANK, 0:NE], ACT.Copy).then_inc(sg("slot gate"), 1)
                for e in range(NE):
                    act.wait_ge(sg("scat ps"), NE * turn + e + 1)
                    act.activation(scat[:, e, :], ps[:, 4 + e % 2, 0:NLAT * P], ACT.Copy).then_inc(sg("scat"), 1)

            def modulate(gathered):
                for k in range(KD):
                    act.wait_ge(sg("gathered"), gathered + (1 + k // 4))
                    ins = act.activation(he32[:, k, :], ps[:, 2 + k // 4, P * (k % 4):P * (k % 4) + P], ACT.Identity,
                                         bias=mod_b[:, 1, 1, k, 0:1], scale=mod_a[:, 1, 1, k, 0:1])
                    if k % 4 == 3:
                        ins.then_inc(sg("he32"), 1)

            def outputs(gate, i, count):
                act.activation(yg[:, :].rearrange("p (a n) -> p a n", a=2), ps[:, 6:8, :], ACT.Identity, scale=gate)\
                    .then_inc(sg("yg"), 1)
                act.activation(scat_now[:, :], scat[:, i, :], ACT.Copy)
                act.wait_ge(sg("yg"), count)
                act.activation(yh[:, :], yg[:, :], ACT.Copy).then_inc(sg("y hi"), 1)

            def split_expert_unit(i, e, base):
                s = NS0 + base + i
                landed, count = expert_in(base + i)
                act.wait_ge(landed, e * (16 * UE // RAW_E) + count)
                act.wait_ge(unit_used, e * UE + (s - SPL + 1))
                act.activation(w_hi[:, s % SPL, :], expert_raw(i), ACT.Copy).then_inc(hi_done, 1)

            def experts(turn):
                base = turn * NE * UE
                modulate(2 * (NE + 1) * turn)

                def expert(e, first):
                    done = [AHEAD + 1 if first and turn == 0 else 0]

                    def split_to(i1):
                        for i in range(done[0], min(i1, UE - 1) + 1):
                            split_expert_unit(i, e, base)
                        done[0] = max(done[0], i1 + 1)

                    split_to(AHEAD)
                    if not first:
                        act.wait_ge(unit_used, e * UE + (NS0 + base))
                        outputs(st2[:, bass.ds(e + 95, 1)], e - 1, e + NE * turn)
                    for s in range(STEPS):
                        split_to(end_w1(s) + AHEAD)
                        act.wait_ge(unit_used, e * UE + (NS0 + base + end_w1(s) + 1))
                        if s >= 2:
                            act.wait_ge(sg("ae32"), e * STEPS + (STEPS * NE * turn + s - 1))
                        act.activation(sge[:, s % 2, :], ps[:, 2 * (s % 2), :], ACT.Silu).then_inc(sg("silu e"), 1)
                        if s:
                            act.wait_ge(sg("ae ps"), e * STEPS + (STEPS * NE * turn + s))
                            act.activation(ae_hi[:, (s - 1) % 2, :], ps[:, 4 + (s - 1) % 2, :], ACT.Copy).then_inc(sg("ae hi"), 1)
                        split_to(end_w3(s) + AHEAD)
                        if s:
                            split_to(end_w2(s - 1) + AHEAD)
                        if s == SLOT_STEP and first:
                            scatters(turn)
                    act.wait_ge(sg("ae ps"), e * STEPS + (STEPS * NE * turn + STEPS))
                    act.activation(ae_hi[:, (STEPS - 1) % 2, :], ps[:, 4 + (STEPS - 1) % 2, :], ACT.Copy).then_inc(sg("ae hi"), 1)
                    split_to(UE - 1)
                    modulate(e * 2 + (2 * (NE + 1) * turn + 2))

                expert(0, True)
                if turn == 0:
                    act.wait_ge(sg("flag set"), 1)
                    busiest.append(act.value_load(flag[0:1, 0:1], min_val=0, max_val=NLAT * P))
                with act.Fori(1, NE) as e:
                    expert(e, False)
                act.wait_ge(unit_used, NS0 + base + NE * UE)
                outputs(st2[:, 96 + NE - 1:96 + NE], NE - 1, NE * (turn + 1))
                act.wait_ge(sg("yout"), NE * (turn + 1) + 1)

            for i in range(AHEAD + 1):
                split_expert_unit(i, 0, 0)
            act.wait_ge(sg("gap"), NLAT)
            act.activation(rs[:, 82:84], rs[:, 80:82], ACT.Exp).then_inc(sg("gap exp"), 1)
            busiest = []
            experts(0)
            with act.If(busiest[0] > P):
                experts(1)
            for half in range(2):
                post_squares("pf1", half, [yout[:, b, 512 * half:512 * half + 512] for b in range(NLAT)], junk[:, 0:512],
                             lambda b: None)

        @block.vector
        def _(dve):
            cur = [0]
            chain = [0]
            stage_end = [in_end[0]]

            def link(ins):
                chain[0] += 1
                ins.then_inc(dve_ch, 1)
                dve.wait_ge(dve_ch, chain[0])

            def split_lo(s_, src, hi_count):
                dve.wait_ge(hi_done, hi_count)
                dve.tensor_tensor(w_lo[:, s_ % SPL, :], src, w_hi[:, s_ % SPL, :].bitcast(F32), ALU.subtract)\
                    .then_inc(lo_done, 1)

            def split_upto(s):
                s = min(s, stage_end[0])
                while cur[0] <= s:
                    u = split_units[cur[0]]
                    split_lo(u.s, raw_at(u.k), u.s + 1)
                    cur[0] += 1

            def last_s(key):
                return at[key][-1].s

            link(dve.memset(cstat[:, :, :], 0.0))
            dve.engine_nop().then_inc(sg("cstat"), 1)
            dve.wait_ge(sg("small T"), 3)
            for l in range(2):
                dve.tensor_copy(pcol[:, l, :], ps[:, 1 + l, 0:68]).then_inc(sg("pcol"), 1)
            dve.wait_ge(sg("pcol"), 2)

            def lambdas():
                dve.wait_ge(sg("params in"), 16 * 14)
                for l in range(2):
                    link(dve.tensor_tensor(lam_t[:, l, :, :], lam_bc[:, l, 0:4:2, :], lam_bc[:, l, 1:4:2, :], ALU.mult))
                    link(dve.tensor_reduce(lam_s[:, l, 0:2], lam_t[:, l, :, :], AX.X, ALU.add))
                dve.engine_nop().then_inc(sg("lam dots"), 1)
                dve.wait_ge(sg("lam exp"), 1)
                for l in range(2):
                    lam_init = 0.8 - 0.6 * math.exp(-0.3 * l)
                    link(dve.tensor_tensor(lam_s[:, l, 4:5], lam_s[:, l, 3:4], lam_s[:, l, 2:3], ALU.subtract))
                    link(dve.tensor_scalar(lam_s[:, l, 5:6], lam_s[:, l, 4:5], -lam_init, None, ALU.add))

            def ada_copy(c, bank):
                dve.wait_ge(ada_used, 4 * (c + 1))
                dve.tensor_copy(arow[:, :], ps[:, bank, :]).then_inc(sg("arow"), 1)

            def ada_finish(c, bank):
                l, part, half = ADA_SEQ[c]
                dve.wait_ge(sg("ada post"), c + 1)
                if part in (2, 5):
                    dve.wait_ge(s_bc, 32 * (gate_chunks.index(c) + 1))
                    for r in streams(l):
                        g = gg[:, gate_at(l, part // 3, r), 512 * half:512 * half + 512]
                        link(dve.tensor_tensor(g, ps[:, bank + 1 - r, :], ab_bc[:, :], ALU.add))
                        ins = dve.tensor_tensor(g, g, pg_bc[:, :], ALU.mult)
                else:
                    w, ks = part // 3, slice(4 * half, 4 * half + 4)
                    new = ps[:, bank + 1, 0:8].rearrange("p (k r) -> p k r", r=2)

                    def col(i):
                        return pcol[:, l, i + 4 * half:i + 4 * half + 4].unsqueeze(2).to_broadcast([P, 4, 2])
                    if part % 3 == 0:
                        ins = dve.tensor_tensor(mod_b[:, l, w, ks, :], new, col(part * KD), ALU.add)
                    else:
                        a = mod_a[:, l, w, ks, :]
                        link(dve.tensor_tensor(a, new, col(part * KD), ALU.add))
                        ins = dve.scalar_tensor_tensor(out=a, in0=a, scalar=1.0, in1=col(48 + KD * w), op0=ALU.add, op1=ALU.mult)
                ins.then_inc(sg("ada fin"), 1)

            def pre_mean(key, b):
                dve.wait_ge(sg("ss " + key), b + 1)
                dve.tensor_scalar(st[:, 4 + b:5 + b], st[:, b:b + 1], 1.0 / D, EPS, ALU.mult, ALU.add).then_inc(sg("ms " + key), 1)

            def pre_scale(key, b):
                dve.wait_ge(sg("rt " + key), b + 1)
                link(dve.reciprocal(st[:, 12 + b:13 + b], st[:, 8 + b:9 + b]))
                dve.tensor_scalar(xn[:, b, :], xs[:, b, :], st[:, 12 + b:13 + b], None, ALU.mult).then_inc(sg("xn " + key), 1)

            def prenorm(key, nb, update):
                for t in range(nb + 2):
                    if t < nb:
                        update(t)
                    if 1 <= t <= nb:
                        pre_mean(key, t - 1)
                    if t >= 2:
                        pre_scale(key, t - 2)

            def split_h(key, ks=range(KD)):
                for k in ks:
                    dve.wait_ge(sg("hT32 " + key), k + 1)
                    link(dve.tensor_copy(hT_hi[:, k, :], hT32[:, k, :]))
                    dve.tensor_tensor(hT_lo[:, k, :], hT32[:, k, :], hT_hi[:, k, :].bitcast(F32), ALU.subtract)\
                        .then_inc(sg("hT " + key), 1)
                    if k % 2 and (k > 4 or key != "mix0"):
                        split_upto(first_units[key] + (k // 2 - 2 if key == "mix0" else k // 2))

            def post_gates(key, half, which, dst, srcs):
                layer, n = int(key[-1]), len(srcs)
                for b, src in enumerate(srcs):
                    dve.wait_ge(sg("ss " + key), half * n + b + 1)
                    o = slice(512 * half, 512 * half + 512)
                    dve.tensor_tensor(dst[:, b, o], src, gg[:, gate_at(layer, which, b // NLAT), o], ALU.mult)\
                        .then_inc(sg("z " + key), 1)

            def post_root(key, n):
                dve.wait_ge(sg("ss " + key), 2 * n)
                link(dve.tensor_tensor(st[:, 20:20 + n], st[:, 16:16 + n], st[:, 20:20 + n], ALU.add))
                dve.tensor_scalar(st[:, 20:20 + n], st[:, 20:20 + n], 1.0 / D, EPS, ALU.mult, ALU.add).then_inc(sg("ms " + key), 1)
                dve.wait_ge(sg("rt " + key), 1)
                link(dve.reciprocal(st[:, 28:28 + n], st[:, 24:24 + n]))
                dve.wait_ge(sg("z " + key), 2 * n)

            def residual(src, done):
                def update(b):
                    dve.scalar_tensor_tensor(out=xs[:, b, :], in0=src[:, b, :], scalar=st[:, 28 + b:29 + b], in1=xs[:, b, :],
                                             op0=ALU.mult, op1=ALU.add).then_inc(sg(done), 1)
                    if done != "final x":
                        dve.wait_ge(sg(done), b + 1)
                return update

            def rope(l, b, t):
                cos = cst[:, C_COS + HD * b:C_COS + HD * b + HD].unsqueeze(1).to_broadcast([P, 8, HD])
                sin = cst[:, C_SIN + HD * b:C_SIN + HD * b + HD].rearrange("p (r f i) -> p r f i", r=2, f=2)
                src, tmp, turned = proj[:, b, DA * t:DA * t + DA], rtmp[:, 0:DA], rtmp[:, DA:2 * DA]
                pair = src.rearrange("p (h r f i) -> p h r f i", r=2, f=2, i=16)
                tv = tmp.rearrange("p (h r f i) -> p h r f i", r=2, f=2, i=16)
                dve.tensor_tensor(turned.rearrange("p (h d) -> p h d", d=HD), src.rearrange("p (h d) -> p h d", d=HD), cos, ALU.mult)
                for f in range(2):
                    link(dve.tensor_tensor(tv[:, :, :, f, :], pair[:, :, :, 1 - f, :],
                                           sin[:, :, f, :].unsqueeze(1).to_broadcast([P, 8, 2, 16]), ALU.mult))
                dve.tensor_tensor(src, turned, tmp, ALU.add).then_inc(sg("rope%d" % l), 1)
                dve.wait_ge(sg("rope%d" % l), NLAT * t + b + 1)

            def spatial_stats(l, b):
                link(dve.bn_stats(st2[:, 104:110], proj[:, b, 4 * DA:5 * DA]))
                link(dve.bn_aggr(st[:, 48 + 2 * b:50 + 2 * b], st2[:, 104:110]))

            def spatial_root(l, nb):
                dve.tensor_scalar(st[:, 40:40 + nb], st[:, 49:49 + 2 * nb:2], EPS, None, ALU.add).then_inc(sg("ln ms"), 1)

            def spatial_norm(l, b):
                v = proj[:, b, 4 * DA:5 * DA]
                link(dve.reciprocal(st[:, 36 + b:37 + b], st[:, 44 + b:45 + b]))
                link(dve.tensor_scalar(v, v, st[:, 48 + 2 * b:49 + 2 * b], st[:, 36 + b:37 + b], ALU.subtract, ALU.mult))
                link(dve.tensor_tensor(v, v, lng_bc[:, l, :], ALU.mult))
                dve.tensor_tensor(v, v, lnb_bc[:, l, :], ALU.add).then_inc(sg("vn%d" % l), 1)

            def project_in(l):
                nb = len(out_blocks(l))
                for jn, j in enumerate(IN_ORDER):
                    for n, u in enumerate(at["in", l, j]):
                        split_upto(u.s + AHEAD)
                        if n == 0 and jn in (1, 3, 4):
                            dve.wait_ge(sg("proj%d" % l), proj_n[l][jn - 1])
                        if jn == 1 and n < nb:
                            spatial_stats(l, n)
                        if jn == 2 and n == 0:
                            spatial_root(l, nb)
                        if jn == 3 and n == 0:
                            dve.wait_ge(sg("ln rt"), l + 1)
                            dve.wait_ge(sg("params in"), 16 * 14)
                        if jn == 3 and n < nb:
                            spatial_norm(l, n)
                        if jn in (3, 4) and n >= NLAT:
                            rope(l, n - NLAT, jn - 3)
                if l == 0:
                    lambdas()
                dve.wait_ge(sg("proj%d" % l), proj_n[l][4])

            def gate(l):
                for b in out_blocks(l):
                    dve.wait_ge(sg("mixed"), NB * l + b + 1)
                    for g in range(4):
                        u = proj[:, b, 3 * DA + P * g:3 * DA + P * g + P]
                        ins = dve.scalar_tensor_tensor(out=u, in0=ps[:, 4 + b, P * g:P * g + P], scalar=pcol[:, l, 64 + g:65 + g],
                                                       in1=u, op0=ALU.add, op1=ALU.mult)
                    ins.then_inc(sg("gated"), 1)

            def attend(l):
                its = items[l]
                n = len(its)
                for t in range(n + 2):
                    if 1 <= t <= n:
                        i = t - 1
                        p = i % 2
                        nk = 512 if its[i][0] < NLAT else 256
                        dve.wait_ge(sg("exp%d" % l), 2 * (i + 1))
                        link(dve.reciprocal(att[:, p, 6:8], att[:, p, 4:6]))
                        link(dve.tensor_scalar(att[:, p, 7:8], att[:, p, 7:8], lam_s[:, l, 5:6], None, ALU.mult))
                        link(dve.tensor_scalar(pr[:, p, 1, 0:nk], pr[:, p, 1, 0:nk], att[:, p, 7:8], None, ALU.mult))
                        dve.scalar_tensor_tensor(out=pr[:, p, 0, 0:nk], in0=pr[:, p, 0, 0:nk], scalar=att[:, p, 6:7],
                                                 in1=pr[:, p, 1, 0:nk], op0=ALU.mult, op1=ALU.add).then_inc(sg("weights%d" % l), 1)
                    if t < n:
                        p = t % 2
                        nk = 512 if its[t][0] < NLAT else 256
                        dve.wait_ge(sg("scores%d" % l), t + 1)
                        link(dve.tensor_reduce(att[:, p, 0:2], ps[:, 2 * p:2 * p + 2, 0:nk], AX.X, ALU.max))
                        dve.tensor_scalar(att[:, p, 2:4], att[:, p, 0:2], -SCALE, None, ALU.mult).then_inc(sg("rowmax%d" % l), 1)
                    if ada_slot(l, t - 1):
                        ada_finish(ada_slot(l, t - 1), ADA)
                    if t >= 2:
                        i = t - 2
                        b, h = its[i]
                        dve.wait_ge(sg("pv%d" % l), i + 1)
                        dve.tensor_copy(proj[:, b, P * h:P * h + P], ps[:, 5, 0:P]).then_inc(sg("o%d" % l), 1)
                    if ada_slot(l, t):
                        ada_copy(ada_slot(l, t), ADA)
                    if t >= 2 and (t - 2) % HEADS == HEADS - 1:
                        head_norm(l, (t - 2) // HEADS)

            def split_cat(l, nb, js):
                for j in js:
                    if j % 2 == 0:
                        split_upto(at["out", l, 0][0].s + j // 2)
                    k = CAT[j]
                    dve.wait_ge(sg("catT hi"), KD * l + j + 1)
                    dve.tensor_tensor(hT_lo[:, k, 0:P * nb], ps[:, 1 + 2 * (j % 4), 0:P * nb], hT_hi[:, k, 0:P * nb].bitcast(F32), ALU.subtract)\
                        .then_inc(sg("catT"), 1)

            def head_norm(l, b):
                o = slice(HEADS * b, HEADS * b + HEADS)
                keep = 1.0 - (0.8 - 0.6 * math.exp(-0.3 * l))
                ss, ms, rt, rstd = (st2[:, k:k + 16][:, o] for k in (0, 16, 32, 48))
                dve.wait_ge(sg("o sq%d" % l), HEADS * (b + 1))
                dve.wait_ge(sg("o%d" % l), HEADS * (b + 1))
                dve.tensor_scalar(ms, ss, 1.0 / P, EPS, ALU.mult, ALU.add).then_inc(sg("o ms%d" % l), 1)
                if b == out_blocks(l)[-1]:
                    stage_end[0] = in_end[l + 1]
                    split_cat(l, b + 1, range(4))
                dve.wait_ge(sg("o rt%d" % l), b + 1)
                link(dve.reciprocal(rstd, rt))
                link(dve.tensor_scalar(rstd, rstd, keep, None, ALU.mult))
                for h in range(HEADS):
                    v = proj[:, b, P * h:P * h + P]
                    dve.scalar_tensor_tensor(out=v, in0=v, scalar=rstd[:, h:h + 1], in1=sub_bc[:, l, :],
                                             op0=ALU.mult, op1=ALU.mult).then_inc(sg("cat%d" % l), 1)

            def ffn():
                for g, (c0, gc) in enumerate(groups):
                    for c in range(c0, c0 + gc, 2):
                        split_upto(last_s(("w1", c)) + AHEAD)
                        split_upto(last_s(("w3", c)) + AHEAD)
                        dve.wait_ge(unit_used, last_s(("w3", c)) + 1)
                        for ci in range(2):
                            dve.wait_ge(sg("silu"), c + ci + 1)
                            if c:
                                dve.wait_ge(sg("AT"), c + ci - 1)
                            dve.tensor_tensor(a32[:, ci, :], sgf[:, ci, :], ps[:, 2 + ci, :], ALU.mult).then_inc(sg("gated up"), 1)
                        for ci in range(2):
                            a = (c + ci) % ATS
                            dve.wait_ge(sg("AT hi"), c + ci + 1)
                            dve.tensor_tensor(at_lo[:, a, :], a32[:, ci, :], at_hi[:, a, :].bitcast(F32), ALU.subtract)\
                                .then_inc(sg("AT"), 1)
                    for n2 in range(2):
                        split_upto(last_s(("w2", g, n2)) + AHEAD)
                        for b in range(NB):
                            if b < NB - 1:
                                dve.wait_ge(sg("y part"), (NB - 1) * (2 * g + n2) + b + 1)
                            else:
                                dve.wait_ge(unit_used, last_s(("w2", g, n2)) + 1)
                            y = y0[:, b, 512 * n2:512 * n2 + 512]
                            if g == 0:
                                dve.tensor_copy(y, ps[:, 4 + b, :]).then_inc(sg("y sum"), 1)
                            else:
                                dve.wait_ge(sg("y sum"), NB * (2 * (g - 1) + n2) + b + 1)
                                dve.tensor_tensor(y, y, ps[:, 4 + b, :], ALU.add).then_inc(sg("y sum"), 1)
                        if g == len(groups) - 1:
                            post_gates("pf0", n2, 1, y0, [y0[:, b, 512 * n2:512 * n2 + 512] for b in range(NB)])

            def route():
                lg, mx, idf = rs[:, 0:16], rs[:, 16:32], rs[:, 32:48]
                oh = rs[:, 48:80].rearrange("p (j t e) -> p j t e", j=2, t=NLAT)
                dve.wait_ge(sg("logits"), 1)
                link(dve.tensor_copy(lg, ps[:, 0, 0:16]))
                for tb in range(NLAT):
                    o = slice(8 * tb, 8 * tb + 8)
                    link(dve.max(mx[:, o], lg[:, o]))
                    link(dve.max_index(idx[:, tb, :], mx[:, o], lg[:, o]))
                link(dve.tensor_copy(idf, idx[:, :, :].rearrange("p t e -> p (t e)")))
                for tb in range(NLAT):
                    for j in range(2):
                        link(dve.tensor_scalar(oh[:, j, tb, :], iota[:, 0:8], idf[:, 8 * tb + j:8 * tb + j + 1], None, ALU.is_equal))
                    dve.tensor_tensor(rs[:, 80 + tb:81 + tb], mx[:, 8 * tb + 1:8 * tb + 2], mx[:, 8 * tb:8 * tb + 1], ALU.subtract)\
                        .then_inc(sg("gap"), 1)
                link(dve.tensor_tensor(st2[:, 64:80], rs[:, 48:64], rs[:, 64:80], ALU.add))
                dve.engine_nop().then_inc(sg("mask"), 1)
                dve.wait_ge(sg("counts"), 1)
                link(dve.tensor_tensor(rs[:, 96:112], ps[:, 1, 0:16], st2[:, 64:80], ALU.mult))
                link(dve.tensor_scalar(rs[:, 96:112], rs[:, 96:112], -1.0, None, ALU.add))
                permute(0)
                dve.wait_ge(sg("gap exp"), 1)
                link(dve.tensor_scalar(rs[:, 84:86], rs[:, 82:84], 1.0, None, ALU.add))
                link(dve.reciprocal(rs[:, 86:88], rs[:, 84:86]))
                link(dve.tensor_tensor(rs[:, 88:90], rs[:, 86:88], rs[:, 82:84], ALU.mult))
                for tb in range(NLAT):
                    gt = st2[:, 80 + 8 * tb:88 + 8 * tb]
                    link(dve.tensor_scalar(gt, oh[:, 0, tb, :], rs[:, 86 + tb:87 + tb], None, ALU.mult))
                    link(dve.scalar_tensor_tensor(out=gt, in0=oh[:, 1, tb, :], scalar=rs[:, 88 + tb:89 + tb], in1=gt,
                                                  op0=ALU.mult, op1=ALU.add))
                dve.engine_nop().then_inc(sg("gates"), 1)
                link(dve.tensor_scalar(rs[:, 112:128], rs[:, 96:112], -float(P), None, ALU.add))
                link(dve.tensor_reduce(rs[:, 90:91], ps[:, 1, 16:24], AX.X, ALU.max))
                dve.tensor_copy(flag[:, :], rs[:, 90:91]).then_inc(sg("flag set"), 1)
                dve.wait_ge(sg("flag set"), 1)

            def permute(turn):
                dve.tensor_scalar(perm[:, NE, :, :], cst[:, C_IOTA:C_IOTA + P].unsqueeze(1).to_broadcast([P, NLAT, P]), -1.0, None,
                                  ALU.is_equal)
                for e in range(NE):
                    for tb in range(NLAT):
                        place_ = 96 + 16 * turn + 8 * tb + e
                        ins = dve.tensor_scalar(perm[:, e, tb, :], iota, rs[:, place_:place_ + 1], None, ALU.is_equal)
                    ins.then_inc(sg("perm"), 1)

            def split_he(n):
                for half in range(2):
                    ks = slice(4 * half, 4 * half + 4)
                    dve.wait_ge(sg("he32"), 2 * n + (half - 1))
                    dve.tensor_copy(he_hi[:, ks, :], he32[:, ks, :]).then_inc(sg("he hi"), 1)
                    dve.wait_ge(sg("he hi"), 2 * n + (half - 1))
                    dve.tensor_tensor(he_lo[:, ks, :], he32[:, ks, :], he_hi[:, ks, :].bitcast(F32), ALU.subtract).then_inc(sg("he"), 1)

            def add_up(count):
                dve.wait_ge(sg("scattered"), count)
                dve.wait_ge(sg("yout"), count)
                y = yout[:, :, :].rearrange("p t (a n) -> p (t a) n", a=2)
                dve.tensor_tensor(y, y, ps[:, 4:8, :], ALU.add).then_inc(sg("yout"), 1)

            def split_y(count):
                dve.wait_ge(sg("y hi"), count)
                dve.tensor_tensor(yl[:, :], yg[:, :], yh[:, :].bitcast(F32), ALU.subtract).then_inc(sg("y split"), 1)

            def experts(turn):
                base = turn * NE * UE
                split_he((NE + 1) * turn + 1)

                def expert(e, first):
                    done = [AHEAD + 1 if first and turn == 0 else 0]

                    def split_to(i1):
                        for i in range(done[0], min(i1, UE - 1) + 1):
                            split_lo(NS0 + base + i, expert_raw(i), e * UE + (NS0 + base + i + 1))
                        done[0] = max(done[0], i1 + 1)

                    split_to(AHEAD)
                    if not first:
                        split_y(e + NE * turn)

                    def lo_a(s):
                        dve.wait_ge(sg("ae hi"), e * STEPS + (STEPS * NE * turn + s + 1))
                        dve.tensor_tensor(ae_lo[:, s % 2, :], ps[:, 4 + s % 2, :], ae_hi[:, s % 2, :].bitcast(F32), ALU.subtract)\
                            .then_inc(sg("ae"), 1)

                    for s in range(STEPS):
                        split_to(end_w1(s) + AHEAD)
                        if s:
                            lo_a(s - 1)
                        split_to(end_w3(s) + AHEAD)
                        dve.wait_ge(sg("silu e"), e * STEPS + (STEPS * NE * turn + s + 1))
                        dve.wait_ge(unit_used, e * UE + (NS0 + base + end_w3(s) + 1))
                        dve.tensor_tensor(ae32[:, s % 2, :], sge[:, s % 2, :], ps[:, 2 * (s % 2) + 1, :], ALU.mult)\
                            .then_inc(sg("ae32"), 1)
                        if s == 0 and not first:
                            add_up(e + NE * turn)
                        if s:
                            split_to(end_w2(s - 1) + AHEAD)
                    lo_a(STEPS - 1)
                    split_to(UE - 1)
                    split_he(e + ((NE + 1) * turn + 2))

                expert(0, True)
                if turn == 0:
                    busiest.append(dve.value_load(flag[0:1, 0:1], min_val=0, max_val=NLAT * P))
                with dve.Fori(1, NE) as e:
                    expert(e, False)
                split_y(NE * (turn + 1))
                add_up(NE * (turn + 1))
                dve.wait_ge(sg("yout"), NE * (turn + 1) + 1)

            for c in range(4):
                if c == 2:
                    prenorm("mix0", NB, lambda b: None)
                if c == 3:
                    split_h("mix0", range(4))
                ada_copy(c, ADA)
                ada_finish(c, ADA)
            split_h("mix0", range(4, KD))
            for l in range(2):
                nb = len(out_blocks(l))
                if l:
                    split_h("mix1")
                project_in(l)
                gate(l)
                attend(l)
                split_cat(l, nb, range(4, KD))
                split_upto(last_s(("out", l, 1)))
                key = "pm%d" % l
                post_gates(key, 0, 0, zmix, [ps[:, 2 * b, :] for b in out_blocks(l)])
                for b in out_blocks(l):
                    dve.wait_ge(sg("ss " + key), nb + b + 1)
                    link(dve.tensor_tensor(st[:, 20 + b:21 + b], st[:, 16 + b:17 + b], st[:, 20 + b:21 + b], ALU.add))
                    dve.tensor_scalar(st[:, 20 + b:21 + b], st[:, 20 + b:21 + b], 1.0 / D, EPS, ALU.mult, ALU.add)\
                        .then_inc(sg("ms " + key), 1)
                    dve.tensor_tensor(zmix[:, b, 512:1024], ps[:, 2 * b + 1, :], gg[:, gate_at(l, 0, b // NLAT), 512:1024], ALU.mult)\
                        .then_inc(sg("z " + key), 1)
                    dve.wait_ge(sg("rt " + key), b + 1)
                    link(dve.reciprocal(st[:, 28 + b:29 + b], st[:, 24 + b:25 + b]))
                    dve.wait_ge(sg("z " + key), nb + b + 1)
                    residual(zmix, "x mix%d" % l)(b)
                    pre_mean("ffn%d" % l, b)
                    pre_scale("ffn%d" % l, b)
                if l == 0:
                    split_h("ffn0")
                    ffn()
                    post_root("pf0", NB)
                    prenorm("mix1", NB, residual(y0, "x ffn"))
            dve.wait_ge(sg("xn ffn1"), NLAT)
            link(dve.tensor_copy(xg_hi[:, :, :], xn[:, 0:NLAT, :]))
            link(dve.tensor_tensor(xg_lo[:, :, :], xn[:, 0:NLAT, :], xg_hi[:, :, :].bitcast(F32), ALU.subtract))
            dve.memset(yout, 0.0).then_inc(sg("yout"), 1)
            dve.tensor_copy(ident_r[:, :], ident).then_inc(sg("ident r"), 1)
            for i in range(AHEAD + 1):
                split_lo(NS0 + i, expert_raw(i), NS0 + i + 1)
            route()
            busiest = []
            experts(0)
            with dve.If(busiest[0] > P):
                permute(1)
                experts(1)
            for half in range(2):
                post_gates("pf1", half, 1, yout, [yout[:, b, 512 * half:512 * half + 512] for b in range(NLAT)])
            post_root("pf1", NLAT)
            for b in range(NLAT):
                residual(yout, "final x")(b)

    return nc


_INS = ['x', 'c', 'ctx', 'c_ctx', 'ada_w', 'ada_b', 'pre_mix_g', 'post_mix_g', 'pre_ffn_g', 'post_ffn_g', 'w_in',
        'w_out', 'lam_q1', 'lam_k1', 'lam_q2', 'lam_k2', 'subln_g', 'sg_ln_g', 'sg_ln_b', 'sg_w', 'sg_b', 'ffn_w1',
        'ffn_w3', 'ffn_w2', 'router_w', 'moe_w1', 'moe_w3', 'moe_w2']


def kernel(**inputs):
    import numpy as _np
    import concourse.bacc as _bacc
    from concourse import mybir as _mybir
    from concourse.bass_utils import run_bass_kernel_spmd as _run

    nc = _bacc.Bacc("TRN2", target_bir_lowering=False, num_devices=1)
    arrays, args = {}, []
    for name in _INS:
        arrays[f"in_{name}"] = _np.ascontiguousarray(inputs[name])
    arrays["in_const"] = constants()
    for name, a in arrays.items():
        args.append(nc.dram_tensor(name, a.shape, _mybir.dt.from_np(a.dtype), kind="ExternalInput").ap())
    args.append(nc.dram_tensor("out_0", (1, NLAT * P, D), _mybir.dt.float32, kind="ExternalOutput").ap())
    program(nc, *args)
    r = _run(nc, [arrays], core_ids=[0])
    return r.results[0]["out_0"]
```
